# Optimizing a Trainium2 kernel written in Bass

```python
import jax, jax.numpy as jnp
from jax import lax
import numpy as np
import jax
import jax.numpy as jnp

D_MODEL = 1024
BATCH = 1
SEQ = 256
DEPTH = 1

N_HEADS = 8
HEAD_DIM = 64
ATTN_WIDTH = N_HEADS * HEAD_DIM
Q_BLOCK = 128
CONV_WIDTH = D_MODEL // 2
CONV_KERNEL = 31
N_EXPERTS = 32
TOP_K = 4
D_EXPERT = D_MODEL
SWIGLU_LIMIT = 7.0
SWIGLU_ALPHA = 1.702
MOE_BLOCK = 128
RMS_EPS = 1e-5
LN_EPS = 1e-5
N_MOD = 6
COL_SIZES = (CONV_WIDTH, CONV_WIDTH,
             ATTN_WIDTH, ATTN_WIDTH, ATTN_WIDTH,
             N_HEADS,
             D_MODEL, D_MODEL)
IN_COLS = sum(COL_SIZES)


def rms_norm(x, g):
    xf = x.astype(jnp.float32)
    y = xf * lax.rsqrt(jnp.mean(xf * xf, axis=-1, keepdims=True) + RMS_EPS)
    return (y * g.astype(jnp.float32)).astype(x.dtype)

def layer_norm(x, g, b):
    xf = x.astype(jnp.float32)
    mu = jnp.mean(xf, axis=-1, keepdims=True)
    var = jnp.mean(jnp.square(xf - mu), axis=-1, keepdims=True)
    y = (xf - mu) * lax.rsqrt(var + LN_EPS)
    return (y * g.astype(jnp.float32) + b.astype(jnp.float32)).astype(x.dtype)

def conv_module(u_val, u_gate, conv_w, conv_b, ln_g, ln_b, w_proj):
    a = u_val * jax.nn.sigmoid(u_gate)
    a = lax.conv_general_dilated(
        a, conv_w[:, None, :].astype(a.dtype), window_strides=(1,),
        padding=[(CONV_KERNEL - 1, 0)],
        dimension_numbers=('NWC', 'WIO', 'NWC'),
        feature_group_count=CONV_WIDTH) + conv_b
    a = jax.nn.silu(layer_norm(a, ln_g, ln_b))
    return a @ w_proj

def forgetting_attention(q, k, v, f_logit):
    B, S = q.shape[0], q.shape[1]
    n_blocks = S // Q_BLOCK
    log_f = jax.nn.log_sigmoid(f_logit.astype(jnp.float32))
    F = jnp.cumsum(log_f, axis=1).transpose(0, 2, 1)
    kh = k.transpose(0, 2, 1, 3)
    vh = v.transpose(0, 2, 1, 3)
    q_blocks = q.transpose(0, 2, 1, 3).reshape(B, N_HEADS, n_blocks, Q_BLOCK, HEAD_DIM).transpose(2, 0, 1, 3, 4)
    F_blocks = F.reshape(B, N_HEADS, n_blocks, Q_BLOCK).transpose(2, 0, 1, 3)
    k_pos = jnp.arange(S)
    scale = HEAD_DIM ** -0.5

    def one_block(args):
        qi, Fi, bi = args
        q_pos = bi * Q_BLOCK + jnp.arange(Q_BLOCK)
        s = jnp.einsum('bhqd,bhkd->bhqk', qi, kh).astype(jnp.float32) * scale
        s = s + Fi[..., :, None] - F[:, :, None, :]
        s = jnp.where(k_pos[None, :] <= q_pos[:, None], s, -jnp.inf)
        p = jax.nn.softmax(s, axis=-1)
        return jnp.einsum('bhqk,bhkd->bhqd', p.astype(vh.dtype), vh)

    out = lax.map(one_block, (q_blocks, F_blocks, jnp.arange(n_blocks)))
    return out.transpose(1, 0, 3, 2, 4).reshape(B, S, ATTN_WIDTH)

def moe_ffn(h, w_router, b_router, w1, b1, w2, b2):
    B, S, D = h.shape
    T = B * S
    A = T * TOP_K
    hf = h.reshape(T, D)
    logits = (hf @ w_router + b_router).astype(jnp.float32)
    top_v, top_e = lax.top_k(logits, TOP_K)
    gates = jax.nn.softmax(top_v, axis=-1)

    flat_e = top_e.reshape(A).astype(jnp.int32)
    flat_tok = (jnp.arange(A, dtype=jnp.int32) // TOP_K)
    flat_gate = gates.reshape(A)
    order = jnp.argsort(flat_e)
    se, stok, sg = flat_e[order], flat_tok[order], flat_gate[order]
    counts = jnp.bincount(flat_e, length=N_EXPERTS)
    padded = (counts + MOE_BLOCK - 1) // MOE_BLOCK * MOE_BLOCK
    pend = jnp.cumsum(padded)
    pstart = pend - padded
    ustart = jnp.cumsum(counts) - counts
    dest = pstart[se] + jnp.arange(A, dtype=jnp.int32) - ustart[se]
    P = A + N_EXPERTS * MOE_BLOCK
    n_blocks = P // MOE_BLOCK
    tok_buf = jnp.zeros((P,), jnp.int32).at[dest].set(stok)
    gate_buf = jnp.zeros((P,), jnp.float32).at[dest].set(sg)
    block_e = jnp.clip(jnp.searchsorted(pend, jnp.arange(n_blocks) * MOE_BLOCK, side='right'), 0, N_EXPERTS - 1)
    xb = hf[tok_buf].reshape(n_blocks, MOE_BLOCK, D)

    def expert_block(args):
        xi, e = args
        hc = xi @ w1[e] + b1[e]
        g, u = hc[:, :D_EXPERT], hc[:, D_EXPERT:]
        g = jnp.minimum(g, SWIGLU_LIMIT)
        u = jnp.clip(u, -SWIGLU_LIMIT, SWIGLU_LIMIT)
        hm = (u + 1.0) * (g * jax.nn.sigmoid(SWIGLU_ALPHA * g))
        return hm @ w2[e] + b2[e]

    yb = lax.map(expert_block, (xb, block_e)).reshape(P, D)
    y = jax.ops.segment_sum(yb.astype(jnp.float32) * gate_buf[:, None], tok_buf, num_segments=T)
    return y.astype(h.dtype).reshape(B, S, D)

def first_inputs(seed: int = 0) -> dict:
    key = jax.random.key(seed)
    ks = jax.random.split(key, 24)
    f32 = jnp.float32
    L, D = DEPTH, D_MODEL

    def nrm(k, shape, fan_in, mult=1.0):
        return jax.random.normal(k, shape, f32) * (mult * fan_in ** -0.5)

    return {
        "x": jax.random.normal(ks[0], (BATCH, SEQ, D), f32),
        "c": jax.random.normal(ks[1], (BATCH, D), f32),
        "w_ada": nrm(ks[2], (L, D, N_MOD * D), D, 0.5),
        "b_ada": 0.02 * jax.random.normal(ks[3], (L, N_MOD * D), f32),
        "norm1_g": 1.0 + 0.05 * jax.random.normal(ks[4], (L, D), f32),
        "w_in": nrm(ks[5], (L, D, IN_COLS), D),
        "b_forget": jax.random.uniform(ks[6], (L, N_HEADS), f32, 1.0, 4.0),
        "conv_w": nrm(ks[7], (L, CONV_KERNEL, CONV_WIDTH), CONV_KERNEL),
        "conv_b": 0.02 * jax.random.normal(ks[8], (L, CONV_WIDTH), f32),
        "conv_ln_g": 1.0 + 0.05 * jax.random.normal(ks[9], (L, CONV_WIDTH), f32),
        "conv_ln_b": 0.02 * jax.random.normal(ks[10], (L, CONV_WIDTH), f32),
        "w_conv_out": nrm(ks[11], (L, CONV_WIDTH, D), CONV_WIDTH),
        "w_attn_out": nrm(ks[12], (L, ATTN_WIDTH, D), ATTN_WIDTH),
        "w_out": nrm(ks[13], (L, D, D), D),
        "norm2_g": 1.0 + 0.05 * jax.random.normal(ks[14], (L, D), f32),
        "w_router": nrm(ks[15], (L, D, N_EXPERTS), D),
        "b_router": 0.01 * jax.random.normal(ks[16], (L, N_EXPERTS), f32),
        "w_exp_in": nrm(ks[17], (L, N_EXPERTS, D, 2 * D_EXPERT), D),
        "b_exp_in": 0.02 * jax.random.normal(ks[18], (L, N_EXPERTS, 2 * D_EXPERT), f32),
        "w_exp_out": nrm(ks[19], (L, N_EXPERTS, D_EXPERT, D), D_EXPERT),
        "b_exp_out": 0.02 * jax.random.normal(ks[20], (L, N_EXPERTS, D), f32),
        "final_g": 1.0 + 0.05 * jax.random.normal(ks[21], (D,), f32),
    }

def first_block(x, c, w_ada, b_ada, norm1_g, w_in, b_forget, conv_w, conv_b, conv_ln_g, conv_ln_b,
              w_conv_out, w_attn_out, w_out, norm2_g, w_router, b_router, w_exp_in, b_exp_in,
              w_exp_out, b_exp_out, final_g):
    B, S, D = x.shape
    offs = np.cumsum(COL_SIZES)[:-1].tolist()
    for l in range(DEPTH):
        mod = (jax.nn.silu(c) @ w_ada[l] + b_ada[l]).reshape(B, N_MOD, D)
        sh1, sc1, g1, sh2, sc2, g2 = (mod[:, i, None, :] for i in range(N_MOD))

        h = rms_norm(x, norm1_g[l]) * (1.0 + sc1) + sh1
        z = h @ w_in[l]
        u_val, u_gate, q, k, v, f_logit, gate_c, gate_a = jnp.split(z, offs, axis=-1)
        conv_out = conv_module(u_val, u_gate, conv_w[l], conv_b[l], conv_ln_g[l], conv_ln_b[l], w_conv_out[l])
        attn = forgetting_attention(q.reshape(B, S, N_HEADS, HEAD_DIM),
                                    k.reshape(B, S, N_HEADS, HEAD_DIM),
                                    v.reshape(B, S, N_HEADS, HEAD_DIM),
                                    f_logit + b_forget[l])
        attn_out = attn @ w_attn_out[l]
        mixed = jax.nn.sigmoid(gate_c) * conv_out + jax.nn.sigmoid(gate_a) * attn_out
        x = x + g1 * (mixed @ w_out[l])

        h2 = rms_norm(x, norm2_g[l]) * (1.0 + sc2) + sh2
        x = x + g2 * moe_ffn(h2, w_router[l], b_router[l], w_exp_in[l], b_exp_in[l], w_exp_out[l], b_exp_out[l])
    return rms_norm(x, final_g)


DEPTH_2 = 2

N_Q_HEADS = 8
N_KV_HEADS = 2
Q_PER_KV = N_Q_HEADS // N_KV_HEADS
WINDOW = 128
ATTN_BLOCK = 128
ATTN_Q_WIDTH = N_Q_HEADS * HEAD_DIM
ATTN_KV_WIDTH = N_KV_HEADS * HEAD_DIM
N_RET_HEADS = 8
RET_KEY_DIM = 32
RET_VAL_DIM = 64
RET_CHUNK = 128
RET_QK_WIDTH = N_RET_HEADS * RET_KEY_DIM
RET_V_WIDTH = N_RET_HEADS * RET_VAL_DIM
D_FF_DENSE = 2816
N_EXPERTS_2 = 8
TOP_K_2 = 2
D_FF_EXPERT = 1408
N_DENSE_LAYERS = (DEPTH_2 + 1) // 2
N_MOE_LAYERS = DEPTH_2 // 2
IN_SIZES = (ATTN_Q_WIDTH, ATTN_KV_WIDTH, ATTN_KV_WIDTH,
            RET_QK_WIDTH, RET_QK_WIDTH, RET_V_WIDTH, RET_V_WIDTH, RET_V_WIDTH,
            2 * D_MODEL)
IN_WIDTH = sum(IN_SIZES)
DEEPNORM_ALPHA = (2 * DEPTH_2) ** 0.25
DEEPNORM_BETA = (8 * DEPTH_2) ** -0.25
GN_EPS = 1e-5
NEG_INF = -1e30


def layer_norm_2(x, g, b):
    xf = x.astype(jnp.float32)
    mu = jnp.mean(xf, axis=-1, keepdims=True)
    var = jnp.mean(jnp.square(xf - mu), axis=-1, keepdims=True)
    return ((xf - mu) * lax.rsqrt(var + LN_EPS)).astype(x.dtype) * g + b

def split_columns(proj, sizes):
    parts, start = [], 0
    for size in sizes:
        parts.append(proj[..., start:start + size])
        start += size
    return parts

def alibi_slopes(n_heads):
    return jnp.exp2(-8.0 * jnp.arange(1, n_heads + 1, dtype=jnp.float32) / n_heads)

def windowed_gqa(q, k, v, sink_logits):
    B, S, _ = q.shape
    C = ATTN_BLOCK
    nb = S // C
    qb = q.reshape(B, nb, C, N_KV_HEADS, Q_PER_KV, HEAD_DIM)
    pad = ((0, 0), (C, C), (0, 0))
    kp = jnp.pad(k, pad).reshape(B, nb + 2, C, N_KV_HEADS, HEAD_DIM)
    vp = jnp.pad(v, pad).reshape(B, nb + 2, C, N_KV_HEADS, HEAD_DIM)
    kw = jnp.concatenate([kp[:, :-2], kp[:, 1:-1], kp[:, 2:]], axis=2)
    vw = jnp.concatenate([vp[:, :-2], vp[:, 1:-1], vp[:, 2:]], axis=2)
    scores = jnp.einsum('bnqgrd,bnkgd->bngrqk', qb, kw,
                        preferred_element_type=jnp.float32) * (HEAD_DIM ** -0.5)
    qi = jnp.arange(C)
    kj = jnp.arange(3 * C)
    dist = jnp.abs(qi[:, None] - kj[None, :] + C)
    key_pos = (jnp.arange(nb)[:, None] - 1) * C + kj[None, :]
    valid = (dist <= WINDOW)[None] & ((key_pos >= 0) & (key_pos < S))[:, None, :]
    slopes = alibi_slopes(N_Q_HEADS).reshape(N_KV_HEADS, Q_PER_KV)
    scores = scores - slopes[:, :, None, None] * dist.astype(jnp.float32)
    scores = jnp.where(valid[None, :, None, None], scores, NEG_INF)
    sink = jnp.broadcast_to(
        sink_logits.astype(jnp.float32).reshape(N_KV_HEADS, Q_PER_KV)[:, :, None, None],
        scores.shape[:-1] + (1,))
    probs = jax.nn.softmax(jnp.concatenate([scores, sink], axis=-1), axis=-1)[..., :-1]
    out = jnp.einsum('bngrqk,bnkgd->bnqgrd', probs.astype(v.dtype), vw)
    return out.reshape(B, S, ATTN_Q_WIDTH)

def head_group_norm(y):
    mu = jnp.mean(y, axis=-1, keepdims=True)
    var = jnp.mean(jnp.square(y - mu), axis=-1, keepdims=True)
    return (y - mu) * lax.rsqrt(var + GN_EPS)

def retention_one_direction(q, k, v, log_gamma, include_diag):
    B, S, H, dk = q.shape
    dv = v.shape[-1]
    C = RET_CHUNK
    nc = S // C
    qc = q.reshape(B, nc, C, H, dk)
    kc = k.reshape(B, nc, C, H, dk)
    vc = v.reshape(B, nc, C, H, dv)
    pos_i = jnp.arange(C)
    diff_i = pos_i[:, None] - pos_i[None, :]
    mask = (diff_i >= 0) if include_diag else (diff_i > 0)
    pos = pos_i.astype(jnp.float32)
    diff = jnp.maximum(diff_i, 0).astype(jnp.float32)
    intra_decay = jnp.where(mask[None], jnp.exp(diff[None] * log_gamma[:, None, None]), 0.0)
    q_decay = jnp.exp((pos + 1.0)[None] * log_gamma[:, None])
    k_decay = jnp.exp((C - 1.0 - pos)[None] * log_gamma[:, None])
    chunk_decay = jnp.exp(C * log_gamma)
    qk = jnp.einsum('bnqhd,bnkhd->bnhqk', qc, kc) * intra_decay
    intra = jnp.einsum('bnhqk,bnkhe->bnqhe', qk, vc)
    chunk_kv = jnp.einsum('bnkhd,hk,bnkhe->bnhde', kc, k_decay, vc)

    def step(state, kv):
        return chunk_decay[None, :, None, None] * state + kv, state

    init = jnp.zeros((B, H, dk, dv), jnp.float32)
    _, prev = lax.scan(step, init, jnp.moveaxis(chunk_kv, 1, 0))
    prev = jnp.moveaxis(prev, 0, 1)
    cross = jnp.einsum('bnqhd,bnhde,hq->bnqhe', qc, prev, q_decay)
    return (intra + cross).reshape(B, S, H, dv)

def bidirectional_retention(q, k, v, g_f, g_b, decay_fwd, decay_bwd):
    B, S, _ = q.shape
    qh = q.reshape(B, S, N_RET_HEADS, RET_KEY_DIM).astype(jnp.float32)
    kh = k.reshape(B, S, N_RET_HEADS, RET_KEY_DIM).astype(jnp.float32) * (RET_KEY_DIM ** -0.5)
    vh = v.reshape(B, S, N_RET_HEADS, RET_VAL_DIM).astype(jnp.float32)
    lg_f = jax.nn.log_sigmoid(decay_fwd.astype(jnp.float32))
    lg_b = jax.nn.log_sigmoid(decay_bwd.astype(jnp.float32))
    y_f = retention_one_direction(qh, kh, vh, lg_f, True)
    y_b = jnp.flip(retention_one_direction(jnp.flip(qh, 1), jnp.flip(kh, 1), jnp.flip(vh, 1),
                                           lg_b, False), axis=1)
    n_f = head_group_norm(y_f).reshape(B, S, RET_V_WIDTH).astype(g_f.dtype)
    n_b = head_group_norm(y_b).reshape(B, S, RET_V_WIDTH).astype(g_b.dtype)
    return jax.nn.silu(g_f) * n_f + jax.nn.silu(g_b) * n_b

def hybrid_mixer(h, w_in, b_gate, sink_logits, decay_fwd, decay_bwd, w_o_attn, w_o_ret, w_out):
    q_a, k_a, v_a, q_r, k_r, v_r, g_f, g_b, gate_logits = split_columns(h @ w_in, IN_SIZES)
    y_attn = windowed_gqa(q_a, k_a, v_a, sink_logits) @ w_o_attn
    y_ret = bidirectional_retention(q_r, k_r, v_r, g_f, g_b, decay_fwd, decay_bwd) @ w_o_ret
    gates = jax.nn.sigmoid(gate_logits + b_gate)
    merged = gates[..., :D_MODEL] * y_attn + gates[..., D_MODEL:] * y_ret
    return merged @ w_out

def swiglu(x, w1, w3, w2):
    return (jax.nn.silu(x @ w1) * (x @ w3)) @ w2

def moe_swiglu(x, router_w, router_b, w1, w3, w2):
    logits = (x @ router_w).astype(jnp.float32) + router_b.astype(jnp.float32)
    top_vals, top_idx = lax.top_k(logits, TOP_K_2)
    top_w = jax.nn.softmax(top_vals, axis=-1)
    gate = jnp.sum(jax.nn.one_hot(top_idx, N_EXPERTS_2, dtype=jnp.float32) * top_w[..., None], axis=-2)
    gate = gate.astype(x.dtype)
    out = jnp.zeros_like(x)
    for e in range(N_EXPERTS_2):
        out = out + gate[..., e:e + 1] * swiglu(x, w1[e], w3[e], w2[e])
    return out

def second_inputs(seed: int = 0) -> dict:
    key = jax.random.key(seed)
    ks = jax.random.split(key, 24)
    f32 = jnp.float32
    beta = DEEPNORM_BETA

    def normal(k, shape, scale):
        return jax.random.normal(k, shape, f32) * scale

    col_mult = (1.0, 1.0, beta, 1.0, 1.0, beta, 1.0, 1.0, 1.0)
    col_scale = jnp.concatenate([jnp.full((s,), c, f32) for s, c in zip(IN_SIZES, col_mult)])
    base_gamma = 1.0 - jnp.exp2(-5.0 - jnp.arange(N_RET_HEADS, dtype=f32))
    base_logit = jnp.log(base_gamma) - jnp.log1p(-base_gamma)
    return {
        'x': normal(ks[0], (BATCH, SEQ, D_MODEL), 1.0),
        'ln_emb_g': 1.0 + normal(ks[1], (D_MODEL,), 0.02),
        'ln_emb_b': normal(ks[2], (D_MODEL,), 0.02),
        'w_in': normal(ks[3], (DEPTH_2, D_MODEL, IN_WIDTH), D_MODEL ** -0.5) * col_scale,
        'b_gate': normal(ks[4], (DEPTH_2, 2 * D_MODEL), 0.02),
        'sink_logits': normal(ks[5], (DEPTH_2, N_Q_HEADS), 0.5),
        'decay_fwd': base_logit + normal(ks[6], (DEPTH_2, N_RET_HEADS), 0.1),
        'decay_bwd': base_logit + normal(ks[7], (DEPTH_2, N_RET_HEADS), 0.1),
        'w_o_attn': normal(ks[8], (DEPTH_2, ATTN_Q_WIDTH, D_MODEL), beta * ATTN_Q_WIDTH ** -0.5),
        'w_o_ret': normal(ks[9], (DEPTH_2, RET_V_WIDTH, D_MODEL), beta * RET_V_WIDTH ** -0.5),
        'w_out': normal(ks[10], (DEPTH_2, D_MODEL, D_MODEL), beta * D_MODEL ** -0.5),
        'ln1_g': 1.0 + normal(ks[11], (DEPTH_2, D_MODEL), 0.02),
        'ln1_b': normal(ks[12], (DEPTH_2, D_MODEL), 0.02),
        'ffn_w1': normal(ks[13], (N_DENSE_LAYERS, D_MODEL, D_FF_DENSE), beta * D_MODEL ** -0.5),
        'ffn_w3': normal(ks[14], (N_DENSE_LAYERS, D_MODEL, D_FF_DENSE), beta * D_MODEL ** -0.5),
        'ffn_w2': normal(ks[15], (N_DENSE_LAYERS, D_FF_DENSE, D_MODEL), beta * D_FF_DENSE ** -0.5),
        'router_w': normal(ks[16], (N_MOE_LAYERS, D_MODEL, N_EXPERTS_2), D_MODEL ** -0.5),
        'router_b': normal(ks[17], (N_MOE_LAYERS, N_EXPERTS_2), 0.01),
        'moe_w1': normal(ks[18], (N_MOE_LAYERS, N_EXPERTS_2, D_MODEL, D_FF_EXPERT), beta * D_MODEL ** -0.5),
        'moe_w3': normal(ks[19], (N_MOE_LAYERS, N_EXPERTS_2, D_MODEL, D_FF_EXPERT), beta * D_MODEL ** -0.5),
        'moe_w2': normal(ks[20], (N_MOE_LAYERS, N_EXPERTS_2, D_FF_EXPERT, D_MODEL), beta * D_FF_EXPERT ** -0.5),
        'ln2_g': 1.0 + normal(ks[21], (DEPTH_2, D_MODEL), 0.02),
        'ln2_b': normal(ks[22], (DEPTH_2, D_MODEL), 0.02),
    }

def second_block(x, ln_emb_g, ln_emb_b, w_in, b_gate, sink_logits, decay_fwd, decay_bwd,
              w_o_attn, w_o_ret, w_out, ln1_g, ln1_b, ffn_w1, ffn_w3, ffn_w2,
              router_w, router_b, moe_w1, moe_w3, moe_w2, ln2_g, ln2_b):
    x = layer_norm_2(x, ln_emb_g, ln_emb_b)
    for layer in range(DEPTH_2):
        mix = hybrid_mixer(x, w_in[layer], b_gate[layer], sink_logits[layer],
                           decay_fwd[layer], decay_bwd[layer],
                           w_o_attn[layer], w_o_ret[layer], w_out[layer])
        x = layer_norm_2(DEEPNORM_ALPHA * x + mix, ln1_g[layer], ln1_b[layer])
        i = layer // 2
        if layer % 2 == 0:
            ffn = swiglu(x, ffn_w1[i], ffn_w3[i], ffn_w2[i])
        else:
            ffn = moe_swiglu(x, router_w[i], router_b[i], moe_w1[i], moe_w3[i], moe_w2[i])
        x = layer_norm_2(DEEPNORM_ALPHA * x + ffn, ln2_g[layer], ln2_b[layer])
    return x


def setup_inputs(seed=0):
    out = dict(first_inputs(seed))
    for name, value in second_inputs(seed + 1).items():
        if name != "x":
            out[name + "_2"] = value
    return out


def reference(
    x, c, w_ada, b_ada, norm1_g, w_in, b_forget, conv_w, conv_b, conv_ln_g, conv_ln_b,
    w_conv_out, w_attn_out, w_out, norm2_g, w_router, b_router, w_exp_in, b_exp_in, w_exp_out,
    b_exp_out, final_g, ln_emb_g_2, ln_emb_b_2, w_in_2, b_gate_2, sink_logits_2, decay_fwd_2,
    decay_bwd_2, w_o_attn_2, w_o_ret_2, w_out_2, ln1_g_2, ln1_b_2, ffn_w1_2, ffn_w3_2, ffn_w2_2,
    router_w_2, router_b_2, moe_w1_2, moe_w3_2, moe_w2_2, ln2_g_2, ln2_b_2,
):
    x = first_block(
        x, c, w_ada, b_ada, norm1_g, w_in, b_forget, conv_w, conv_b, conv_ln_g, conv_ln_b,
        w_conv_out, w_attn_out, w_out, norm2_g, w_router, b_router, w_exp_in, b_exp_in,
        w_exp_out, b_exp_out, final_g,
    )
    return second_block(
        x, ln_emb_g_2, ln_emb_b_2, w_in_2, b_gate_2, sink_logits_2, decay_fwd_2, decay_bwd_2,
        w_o_attn_2, w_o_ret_2, w_out_2, ln1_g_2, ln1_b_2, ffn_w1_2, ffn_w3_2, ffn_w2_2,
        router_w_2, router_b_2, moe_w1_2, moe_w3_2, moe_w2_2, ln2_g_2, ln2_b_2,
    )


_drawn_inputs = setup_inputs


def setup_inputs(seed=0):
    import zlib

    import numpy as np

    out = dict(_drawn_inputs(seed))
    spreads = {}
    factors = {'norm1_g': 3.457,
     'conv_b': 6.108,
     'conv_ln_g': 4.371,
     'conv_ln_b': 18.8,
     'b_router': 4.195,
     'b_exp_in': 8.0,
     'b_exp_out': 8.0,
     'ln_emb_g_2': 2.73,
     'ln_emb_b_2': 2.752,
     'b_gate_2': 49.21,
     'sink_logits_2': 44.916,
     'decay_fwd_2': 21.584,
     'w_o_attn_2': 3.243,
     'router_b_2': 59.167}
    for name, (base, spread) in spreads.items():
        noise = np.random.default_rng([zlib.crc32(name.encode()), seed]).standard_normal(out[name].shape)
        drawn = base * np.exp(spread * noise) if base else spread * noise
        out[name] = jnp.asarray(drawn.astype(out[name].dtype))
    for name, factor in factors.items():
        out[name] = (out[name] * factor).astype(out[name].dtype)
    return out
```

```python
from contextlib import ExitStack

import numpy as np
import concourse.bass as bass
from concourse import mybir

F32 = mybir.dt.float32
I32 = mybir.dt.int32
ALU = mybir.AluOpType
ACT = mybir.ActivationFunctionType
AX = mybir.AxisListType.X

P = 128
T = 256
D = 1024
KT = D // P
CW = 512
TAPS = 31
HEADS = 8
HD = 64
CHUNK = 128
EPS = 1e-5
NEG = -1e30
FAR = 1e34
ALPHA = (2 * 2) ** 0.25
RK = 32
RSCALE = RK ** -0.5
QSCALE = HD ** -0.5
NG = 12
RING = 15
SLOT = 2048
SLOPES = [2.0 ** -(h + 1) for h in range(HEADS)]

V_C, V_BADA, V_N1G, V_N2G, V_FG, V_CB, V_CLG, V_CLB, V_EG, V_EB = 0, 8, 56, 64, 72, 80, 84, 88, 92, 100
V_LN1G, V_LN1B, V_LN2G, V_LN2B, V_BG = 128, 144, 160, 176, 192
V_CONVW, V_B1 = 256, 384
R_SINK, R_DECAY, R_BR1, R_BR2, R_N = 0, 16, 48, 80, 88


class Linear:

    def __init__(self, name, slots, jobs_per_slot, evac, k_major=0):
        self.name, self.slots, self.per, self.evac, self.k_major = name, slots, jobs_per_slot, evac, k_major


def plan():
    order = [Linear("ada0", 8, 1, "dve", 1),
             Linear("uqkv", 10, 1, "act"), Linear("forget", 0, 1, "act"),
             Linear("gates", 8, 1, "act"),
             Linear("ada1", 8, 1, "dve", 1), Linear("ada2", 8, 1, "dve", 1),
             Linear("conv_out", 2, 2, "dve"), Linear("attn_out", 2, 2, "dve"),
             Linear("w_out", 4, 1, "dve")]
    for l in range(2):
        order += [Linear(f"qa{l}", 2, 1, "act"), Linear(f"kva{l}", 1, 2, "act"),
                  Linear(f"ret{l}", 4, 1, "act"), Linear(f"gg{l}", 12, 1, "act"),
                  Linear(f"wo_attn{l}", 2, 2, "dve"), Linear(f"wo_ret{l}", 2, 2, "dve"),
                  Linear(f"w_out{l}", 4, 1, "dve")]
        if l == 0:
            order += [Linear("ffn1", 11, 1, "act"), Linear("ffn3", 11, 1, "dve"),
                      Linear("ffn2", 11, 1, "dve", 2)]
    slot = group = job = 0
    evacs = {"act": 0, "dve": 0}
    lins, job_evac = {}, []
    for lin in order:
        if lin.name == "qa0":
            slot_b = slot
        jobs = lin.k_major or max(1, lin.slots) * lin.per
        groups = lin.slots if lin.k_major else max(1, lin.slots) * lin.per
        lin.slot0, lin.group0, lin.job0, lin.jobs, lin.groups = slot, group, job, jobs, groups
        slot, group, job = slot + lin.slots, group + groups, job + jobs
        for _ in range(jobs):
            evacs[lin.evac] += 1
            job_evac.append((lin.evac, evacs[lin.evac]))
        lins[lin.name] = lin
    free_at = []
    for lin in order:
        for s in range(lin.slots):
            free_at.append(lin.group0 + (s + 1) * (1 if lin.k_major else lin.per))
    return lins, job_evac, free_at, slot_b, slot


class Chain:

    def __init__(self, eng, sem):
        self.eng, self.sem, self.base, self.n = eng, sem, 0, 0

    def link(self, ins):
        self.n += 1
        ins.then_inc(self.sem, 1)
        self.eng.wait_ge(self.sem, self.base + self.n)

    def enter(self, base):
        self.base, self.n = base, 0


def build_two_blocks(nc, A, out):
    lins, job_evac, free_at, N_A, N_SLOTS = plan()
    ctx = ExitStack()
    with ctx:
        sems = {}

        def sem(name):
            if name not in sems:
                sems[name] = ctx.enter_context(nc.semaphore(name))
            return sems[name]

        def sb(name, shape, dt=F32):
            return ctx.enter_context(nc.sbuf_tensor(name, shape, dt))

        W = sb("W", [P, 24 * 1408])
        Z = sb("Z", [P, 38 * T])
        X = sb("X", [P, KT, T])
        H = sb("H", [P, KT, T])
        SQ = sb("SQ", [P, KT * T])
        VEC = sb("VEC", [P, 7 * P])
        IDENT = sb("IDENT", [P, P])
        ONES = sb("ONES", [P, P])
        BLK = sb("BLK", [P, P])
        BEFORE = sb("BEFORE", [P, P])
        DIST = sb("DIST", [P, 2, T])
        LAGS = sb("LAGS", [P, 4, P])
        MOD = sb("MOD", [P, 48])
        ROWS = sb("ROWS", [1, R_N])
        ROWB = sb("ROWB", [P, R_N])
        WR1 = sb("WR1", [P, KT, 32])
        WR2 = sb("WR2", [P, KT, 8])
        LG = sb("LG", [P, 32])
        GS = sb("GS", [P, 3 * KT])
        CSIL = sb("CSIL", [P, KT])
        BFG = sb("BFG", [8, 1])
        IOTAP = sb("IOTAP", [P, 1])
        ST = sb("ST", [P, 2, 8])
        PS = ctx.enter_context(nc.psum_tensor("PS", [P, 8, 512], F32))

        SCR = W[:, RING * SLOT:RING * SLOT + 3072]

        def z(a, b):
            return Z[:, a * T:b * T].rearrange("p (k t) -> p k t", t=T)

        def slot(n):
            r = (n if n < N_A else n - N_A) % RING
            return W[:, r * SLOT:(r + 1) * SLOT], r

        XT = H[:, :, :].rearrange("p k t -> p (k t)").rearrange("p (a d) -> p a d", a=2)
        VROWS = SQ[:, 0:7 * P].rearrange("p (a c) -> p a c", c=P)
        CONV_IN = SCR[:, 0:4 * 286].rearrange("p (j t) -> p j t", t=286)
        SEL = SCR[:, 1144:2168].rearrange("p (h m) -> p h m", m=P)
        CAUSAL = SCR[:, 2168:2296]
        NEGF = SCR[:, 2296:2552]
        WF = SCR[:, 2552:2616].rearrange("p (k n) -> p k n", n=8)
        PROB = SQ[:, 0:1024].rearrange("p (b a k) -> p b a k", b=2, a=2)
        PROBT = SQ[:, 1024:2048].rearrange("p (b k) -> p b k", b=2)
        DEC = SCR[:, 0:1024].rearrange("p (b f) -> p b f", b=2)
        RA = SCR[:, 1024:3072].rearrange("p (b d s t) -> p b d s t", b=2, d=2, s=2)
        UV, UG, Q1, K1, GC, GA = 0, 4, 8, 12, 20, 28
        VT1 = Z[:, 16 * T:20 * T].rearrange("p (a n) -> p a n", a=2)
        QA, KA, QR, KR, GF, GB, G2A, G2R = 0, 4, 5, 7, 14, 18, 22, 30
        VR = Z[:, 9 * T:13 * T].rearrange("p (a n) -> p a n", a=2)
        VA = Z[:, 13 * T:14 * T].rearrange("p (a n) -> p a n", a=2)

        at = [0]

        def zs(n):
            at[0] += n
            return Z[:, at[0] - n:at[0]]

        HT = zs(2048).rearrange("p (a d) -> p a d", a=2)
        Y = zs(2048).rearrange("p (k t) -> p k t", t=T)
        XG = zs(1024).rearrange("p (k c) -> p k c", c=CHUNK)
        HM = zs(11 * CHUNK).rearrange("p (k c) -> p k c", c=CHUNK)
        PART = zs(2048)
        GT = zs(T)
        PICK = zs(2 * CHUNK).rearrange("p (a c) -> p a c", c=CHUNK)
        PICKG = zs(2 * CHUNK).rearrange("p (a c) -> p a c", c=CHUNK)
        IOTA = zs(T)
        YS = SQ[:, 0:1024]
        TAB = SQ[0:1, 1024:1024 + 2 * P + 34].bitcast(I32)
        at = [1024 + 2 * P + 34]

        def qs(n):
            at[0] += n
            return SQ[:, at[0] - n:at[0]]

        B1C = qs(16)
        LOG = qs(80).rearrange("p (a e) -> p a e", e=40)
        LOGR = qs(80).rearrange("p (a e) -> p a e", e=40)
        MASK = qs(64).rearrange("p (a e) -> p a e", e=32)
        GATE = qs(64).rearrange("p (a e) -> p a e", e=32)
        RANK = qs(64).rearrange("p (a e) -> p a e", e=32)
        TOP8 = qs(16).rearrange("p (a e) -> p a e", e=8)
        NTOP, GSUM = qs(2), qs(2)
        NCH, CUM, START, LE, LEN_, ONE32 = qs(32), qs(32), qs(32), qs(32), qs(32), qs(32)
        TCOL, FREE = qs(2), qs(1)
        BOUT = SCR[0:32, 0:1024]

        def bc(ap, n):
            return ap.unsqueeze(1).broadcast_to([P, n, ap.shape[1]])

        def bl(ap, n):
            return ap.unsqueeze(2).broadcast_to([P, ap.shape[1], n])

        def ps(b, n=512, p0=0, p1=P, c0=0):
            return PS[p0:p1, b, c0:c0 + n]

        def ps2(b):
            return PS[:, b, :].rearrange("p (a t) -> p a t", a=2)

        w_in, w_in2 = A["w_in"], A["w_in_2"]

        def cols(w, c0, n, buf, k=KT):
            return [(buf[:, 0:k * n].rearrange("p (k n) -> p k n", k=k),
                     w[:, c0:c0 + n].rearrange("(k p) n -> p k n", p=P))]

        def rows(w, k0, nk, c0, n, buf):
            return [(buf[:, 0:nk * n].rearrange("p (k n) -> p k n", k=nk),
                     w[k0 * P:(k0 + nk) * P, c0:c0 + n].rearrange("(k p) n -> p k n", p=P))]

        def transfers(name, s, buf):
            l = int(name[-1]) if name[-1].isdigit() else 0
            if name.startswith("ada"):
                return rows(A["w_ada"][0], s, 1, 2048 * l, 2048, buf)
            if name == "uqkv":
                return cols(w_in[0], 256 * s, 256, buf)
            if name == "gates":
                return cols(w_in[0], 5 * CW + HEADS + 256 * s, 256, buf)
            if name in ("conv_out", "attn_out"):
                return cols(A["w_" + name][0], 512 * s, 512, buf, 4)
            if name == "w_out":
                return cols(A["w_out"][0], 256 * s, 256, buf)
            if name.startswith("qa"):
                src = w_in2[l][:, 0:512].rearrange("(k p) (g c) -> p k g c", p=P, g=2)
                dst = buf.rearrange("p (k g c) -> p k g c", k=KT, g=4)
                return [(dst[:, :, 2 * i + g, :], src[:, :, g, (2 * s + i) * HD:(2 * s + i + 1) * HD])
                        for i in range(2) for g in range(2)]
            if name.startswith("kva"):
                return cols(w_in2[l], 512, 256, buf)
            if name.startswith("ret"):
                return cols(w_in2[l], 768 + 256 * s, 256, buf)
            if name.startswith("gg"):
                return cols(w_in2[l], 1792 + 256 * s, 256, buf)
            if name.startswith("wo_attn"):
                src = A["w_o_attn_2"][l][:, 512 * s:512 * (s + 1)].rearrange("(g i r) n -> g r i n", g=2, i=4)
                return [(buf[64 * g:64 * (g + 1), :].rearrange("p (k n) -> p k n", k=4), src[g]) for g in range(2)]
            if name.startswith("wo_ret"):
                return cols(A["w_o_ret_2"][l], 512 * s, 512, buf, 4)
            if name.startswith("w_out"):
                return cols(A["w_out_2"][l], 256 * s, 256, buf)
            if name == "ffn1":
                return cols(A["ffn_w1_2"][0], 256 * s, 256, buf)
            if name == "ffn3":
                return cols(A["ffn_w3_2"][0], 256 * s, 256, buf)
            return rows(A["ffn_w2_2"][0], 2 * s, 2, 0, 1024, buf)

        arrive, total = [], [0] * RING
        for lin in lins.values():
            for s in range(lin.slots):
                n = lin.slot0 + s
                if n == N_A:
                    moe1_base = list(total)
                    for g in range(NG):
                        total[g] += 16 * 32
                buf, r = slot(n)
                total[r] += 16 * len(transfers(lin.name, s, buf))
                arrive.append((r, total[r]))
        moe2_base = list(total)

        class Moe:
            pass

        m1, m2 = Moe(), Moe()
        m1.tag, m1.n, m1.top, m1.ht, m1.base, m1.parts, m1.up, m1.out = "m1", 32, 4, 8, moe1_base, 2, 2, 4
        m2.tag, m2.n, m2.top, m2.ht, m2.base, m2.parts, m2.up, m2.out = "m2", 8, 2, 11, moe2_base, 3, 3, 0

        def msem(m, name):
            return sem(f"{m.tag}_{name}")

        def group_kts(m, s):
            if s < 8:
                return [s] if m is m1 else [2 * (s % 4), 2 * (s % 4) + 1]
            k = 2 if m is m1 else 3
            return list(range(k * (s - 8), min(k * (s - 7), m.ht)))

        def group_at(m, s):
            if m is m1:
                return s * SLOT
            return s * 2816 if s < 8 else 8 * 2816 + (s - 8) * 3072

        def group_src(m, s, e):
            if m is m1:
                if s < 8:
                    w, k0, nk, n = A["w_exp_in"], s, 1, 2048
                else:
                    w, k0, nk, n = A["w_exp_out"], 2 * (s - 8), 2, 1024
            else:
                ks = group_kts(m, s)
                w = A["moe_w1_2"] if s < 4 else A["moe_w3_2"] if s < 8 else A["moe_w2_2"]
                k0, nk, n = ks[0], len(ks), 1408 if s < 8 else 1024
            src = w[0, bass.ds(e, 1), k0 * P:(k0 + nk) * P, :].rearrange("a (k p) n -> p (a k) n", p=P)
            dst = W[:, group_at(m, s):group_at(m, s) + nk * n].rearrange("p (k n) -> p k n", k=nk)
            return dst, src

        block = ctx.enter_context(nc.Block())

        @block.sync
        def _(sp):
            def dense(n0, n1):
                for lin in lins.values():
                    for s in range(lin.slots):
                        n = lin.slot0 + s
                        if not n0 <= n < n1:
                            continue
                        buf, r = slot(n)
                        if n - n0 >= RING:
                            sp.wait_ge(sem("lin_done"), free_at[n - RING])
                        elif n0 and r < NG:
                            sp.wait_ge(msem(m1, "group_done"), m1.last * NG + (r + 1))
                        elif n0:
                            last = max(k for k in range(N_A) if k % RING == r)
                            sp.wait_ge(sem("lin_done"), free_at[last])
                        for dst, src in transfers(lin.name, s, buf):
                            sp.dma_start(dst, src).then_inc(sem(f"arrived{r}"), 16)

            def experts(m, n0, n1):
                for s in range(NG):
                    lo, hi = group_at(m, s), group_at(m, s) + int(np.prod(group_src(m, s, 0)[0].shape[1:]))
                    over = [k for k in range(max(n0, n1 - RING), n1)
                            if slot(k)[1] * SLOT < hi and (slot(k)[1] + 1) * SLOT > lo]
                    need = free_at[max(over)] if over else 0
                    if hi > RING * SLOT:
                        need = free_at[n1 - 1]
                    sp.wait_ge(sem("lin_done"), need)
                    dst, src = group_src(m, s, 0)
                    sp.dma_start(dst, src).then_inc(sem(f"arrived{s}"), 16)
                sp.wait_ge(msem(m, "tables"), 1)
                m.last = sp.value_load(TAB[0:1, 2 * P + 33:2 * P + 34], min_val=0, max_val=47)
                with sp.Fori(1, m.n) as e:
                    before = sp.value_load(TAB[0:1, bass.ds(e + 2 * P, 1)], min_val=0, max_val=47)
                    for s in range(NG):
                        sp.wait_ge(msem(m, "group_done"), before * NG + (s + 1))
                        dst, src = group_src(m, s, e)
                        sp.dma_start(dst, src).then_inc(sem(f"arrived{s}"), 16)

            dense(0, N_A)
            experts(m1, 0, N_A)
            dense(N_A, N_SLOTS)
            experts(m2, N_A, N_SLOTS)
            sp.wait_ge(sem("out_staged"), 4)
            sp.dma_start(out[0].rearrange("(a p) d -> p a d", p=P), XT).then_inc(sem("stored"), 16)
            sp.wait_ge(sem("stored"), 16)

        @block.gpsimd
        def _(pool):
            ch = Chain(pool, sem("pool_step"))
            ch.link(pool.memset(IDENT[:, :], 0.0))
            ch.link(pool.affine_select(out=IDENT[:, :], in_=IDENT[:, :], compare_op=ALU.not_equal, fill=1.0,
                                       base=0, pattern=[[-1, P]], channel_multiplier=1))
            pool.memset(ONES[:, :], 1.0).then_inc(sem("ident_ready"), 1)
            ch.link(pool.memset(BLK[:, :], 0.0))
            ch.link(pool.memset(BLK[0:64, 0:64], 1.0))
            ch.link(pool.memset(BLK[64:128, 64:128], 1.0))
            ch.link(pool.memset(BEFORE[:, :], 1.0))
            ch.link(pool.affine_select(out=BEFORE[:, :], in_=BEFORE[:, :], compare_op=ALU.is_gt, fill=0.0,
                                       base=0, pattern=[[1, P]], channel_multiplier=-1))
            ch.link(pool.memset(SEL, 0.0))
            ch.link(pool.affine_select(out=SEL, in_=SEL, compare_op=ALU.not_equal, fill=1.0,
                                       base=0, pattern=[[-1, HEADS], [0, P]], channel_multiplier=1))
            ch.link(pool.memset(CAUSAL, 0.0))
            ch.link(pool.affine_select(out=CAUSAL, in_=CAUSAL, compare_op=ALU.is_ge, fill=NEG,
                                       base=0, pattern=[[-1, P]], channel_multiplier=1))
            ch.link(pool.memset(NEGF, 0.0))
            ch.link(pool.memset(CONV_IN[:, :, 0:TAPS - 1], 0.0))
            ch.link(pool.iota(IOTAP[:, :], pattern=[[0, 1]], base=0, channel_multiplier=1,
                              allow_small_or_imprecise_dtypes=True))
            for i, (base, step) in enumerate(((0, 1), (P, 1), (P, -1), (0, -1))):
                ch.link(pool.iota(LAGS[:, i, :], pattern=[[step, P]], base=base, channel_multiplier=-step,
                                  allow_small_or_imprecise_dtypes=True))
            ch.link(pool.iota(DIST[:, :, :], pattern=[[P, 2], [-1, T]], base=0, channel_multiplier=1,
                              allow_small_or_imprecise_dtypes=True))
            pool.wait_ge(sem("dist_abs"), 1)
            ch.link(pool.affine_select(out=DIST[:, :, :], in_=DIST[:, :, :], compare_op=ALU.is_ge, fill=FAR,
                                       base=P, pattern=[[-P, 2], [1, T]], channel_multiplier=-1))
            pool.affine_select(out=DIST[:, :, :], in_=DIST[:, :, :], compare_op=ALU.is_ge, fill=FAR,
                               base=P, pattern=[[P, 2], [-1, T]], channel_multiplier=1)\
                .then_inc(sem("dist_ready"), 1)

            def decay_masks(l):
                for h in range(HEADS):
                    n = l * HEADS + h
                    pool.wait_ge(sem("decay_exp"), n + 1)
                    dec = DEC[:, h % 2, :]
                    ch.link(pool.affine_select(out=dec[:, 0:P], in_=dec[:, 0:P], compare_op=ALU.is_ge, fill=0.0,
                                               base=0, pattern=[[1, P]], channel_multiplier=-1))
                    pool.affine_select(out=dec[:, 3 * P:], in_=dec[:, 3 * P:], compare_op=ALU.is_gt, fill=0.0,
                                       base=0, pattern=[[-1, P]], channel_multiplier=1)\
                        .then_inc(sem("decay_masked"), 1)

            def slot_iota(m):
                pool.wait_ge(sem("moe_scratch_free"), 1 if m is m1 else 2)
                pool.iota(IOTA, pattern=[[1, T]], base=0, channel_multiplier=0,
                          allow_small_or_imprecise_dtypes=True).then_inc(msem(m, "iota"), 1)

            slot_iota(m1)
            decay_masks(0)
            decay_masks(1)
            slot_iota(m2)

        @block.tensor
        def _(pe):
            norm = [0]

            def bank_free(job):
                if job >= 2:
                    e, c = job_evac[job - 2]
                    pe.wait_ge(sem("evac_" + e), c)
                else:
                    pe.wait_ge(sem("init_act"), 1)

            def weights(n):
                r, c = arrive[n]
                pe.wait_ge(sem(f"arrived{r}"), c)
                return slot(n)[0]

            def feature_job(lin, s, x, nk=KT, cols_=256, part=0, width=256):
                job = lin.job0 + s * lin.per + part
                w = weights(lin.slot0 + s).rearrange("p (k n) -> p k n", k=nk)
                bank_free(job)
                for j in range(width // P):
                    for k in range(nk):
                        c = part * width + j * P
                        mm = pe.matmul(ps(job % 2, T, c0=j * T), w[:, k, c:c + P], x[:, k, :],
                                       start=(k == 0), stop=(k == nk - 1))
                mm.then_inc(sem("lin_done"), 1)

            def token_job(lin, s, x, c0, width, part=0):
                job = lin.job0 + s * lin.per + part
                w = weights(lin.slot0 + s).rearrange("p (k n) -> p k n", k=KT)
                bank_free(job)
                for a in range(2):
                    for k in range(KT):
                        mm = pe.matmul(ps(job % 2, width, c0=a * width), x[:, k, a * P:(a + 1) * P],
                                       w[:, k, c0:c0 + width], start=(k == 0), stop=(k == KT - 1))
                mm.then_inc(sem("lin_done"), 1)

            def ada(l):
                lin = lins[f"ada{l}"]
                bank_free(lin.job0)
                for s in range(KT):
                    w = weights(lin.slot0 + s)
                    for j in range(16):
                        mm = pe.matmul(PS[:, lin.job0 % 2, j:j + 1], w[:, j * P:(j + 1) * P], CSIL[:, s:s + 1],
                                       start=(s == 0 and j == 0), stop=(s == KT - 1), skip_group_check=True)
                    mm.then_inc(sem("lin_done"), 1)

            def norm_sum(src, nk, col=0):
                norm[0] += 1
                pe.wait_ge(sem("norm_in"), norm[0])
                for k in range(nk):
                    mm = pe.matmul(ps(4, T, c0=col), ONES[:, :], src[:, k, :], start=(k == 0), stop=(k == nk - 1))
                mm.then_inc(sem("norm_sum"), 1)

            SQV = SQ[:, :].rearrange("p (k t) -> p k t", t=T)

            def rms():
                norm_sum(SQV, KT)

            def layer_norm(src, nk=KT):
                norm_sum(src, nk)
                norm_sum(SQV, nk, T)

            pe.wait_ge(sem("ident_ready"), 1)
            pe.wait_ge(sem("ld_vec"), 16 * 17)
            for i, r in enumerate([108, 96, 124] + [P] * 4):
                tr = pe.transpose(PS[:, i // 4, (i % 4) * P:(i % 4) * P + r], VROWS[0:r, i, :], IDENT[0:r, 0:r])
            tr.then_inc(sem("vec_turned"), 1)
            pe.wait_ge(sem("ld_rows"), 16 * 5)
            pe.matmul(ps(3, R_N), ONES[0:1, :], ROWS[0:1, :], start=True, stop=True).then_inc(sem("rows_spread"), 1)
            pe.wait_ge(sem("ld_x"), 16)
            for k in range(KT):
                for a in range(2):
                    tr = pe.transpose(PS[:, 4 + k // 2, (k % 2) * T + a * P:(k % 2) * T + (a + 1) * P],
                                      XT[:, a, k * P:(k + 1) * P], IDENT[:, :])
            tr.then_inc(sem("x_turned"), 1)

            ada(0)
            pe.wait_ge(sem("x_ready"), 1)
            rms()
            pe.wait_ge(sem("h_ready"), 1)
            lin = lins["uqkv"]
            for s in range(8):
                feature_job(lin, s, H)
            for s in range(8, 10):
                token_job(lin, s, H, 0, 256)
            job = lins["forget"].job0
            pe.wait_ge(sem("ld_small"), 16 * 4)
            bank_free(job)
            for k in range(KT):
                mm = pe.matmul(PS[0:8, job % 2, 0:T], WF[:, k, :], H[:, k, :], start=(k == 0), stop=(k == KT - 1))
            mm.then_inc(sem("lin_done"), 1)

            def scores1(h):
                r = (h % 2) * HD
                q, k = Z[r:r + HD, (Q1 + h // 2) * T:(Q1 + h // 2 + 1) * T], Z[r:r + HD, (K1 + h // 2) * T:(K1 + h // 2 + 1) * T]
                b = 4 + h % 2
                if h >= 2:
                    pe.wait_ge(sem("exp_done"), h - 1)
                else:
                    pe.wait_ge(sem("negf_ready"), 1)
                pe.matmul(ps(b, P), q[:, 0:P], k[:, 0:P], start=True, stop=False)
                pe.matmul(ps(b, P), SEL[:, h, :], NEGF[:, 0:P], start=False, stop=False)
                pe.matmul(ps(b, P), IDENT[:, :], CAUSAL, start=False, stop=True)
                pe.matmul(ps(b, T, c0=P), q[:, P:T], k[:, :], start=True, stop=False)
                pe.matmul(ps(b, T, c0=P), SEL[:, h, :], NEGF, start=False, stop=True)
                pe.matmul(ps(b, P, c0=2 * P), IDENT[:, :], CAUSAL, start=False, stop=True,
                          skip_group_check=True).then_inc(sem("scores_ready"), 1)

            def turn_probs(n, h, blocks):
                pe.wait_ge(sem("probs_ready"), n + 1)
                if n >= 1:
                    pe.wait_ge(sem("probs_copied"), n)
                for i, (qa, ka) in enumerate(blocks):
                    tr = pe.transpose(ps(6, P, c0=i * P), PROB[:, n % 2, qa, ka * P:(ka + 1) * P], IDENT[:, :])
                tr.then_inc(sem("probs_turned"), 1)

            def values(n, half, pair, last_half, v, blocks):
                pe.wait_ge(sem("probs_copied"), n + 1)
                if half == 0 and pair >= 1:
                    pe.wait_ge(sem("pair_copied"), pair)
                for i, (ka, q0, wd, c) in enumerate(blocks):
                    mm = pe.matmul(ps(7, wd, HD * half, HD * half + HD, (pair % 2) * T + q0),
                                   v[:, ka, :], PROBT[:, n % 2, c:c + wd], start=(i == 0),
                                   stop=True, skip_group_check=True)
                mm.then_inc(sem("values_done"), 1)

            lin = lins["gates"]
            for i in range(10):
                if i < 8:
                    feature_job(lin, i, H)
                    if i == 0:
                        for n in range(10):
                            pass
                        pe.wait_ge(sem("evac_act"), lins["uqkv"].jobs)
                    scores1(i)
                if 1 <= i < 9:
                    turn_probs(i - 1, i - 1, ((0, 0), (1, 0), (1, 1)))
                if i >= 2:
                    h = i - 2
                    values(h, h % 2, h // 2, h % 2, VT1[:, :, h * HD:(h + 1) * HD], ((0, 0, T, 0), (1, P, P, T)))
            ada(1)
            ada(2)
            layer_norm(z(UV, UV + 4), 4)
            pe.wait_ge(sem("conv_ready"), 1)
            for s in range(2):
                for part in range(2):
                    feature_job(lins["conv_out"], s, z(UV, UV + 4), 4, 512, part)
            pe.wait_ge(sem("pair_copied"), 4)
            for s in range(2):
                for part in range(2):
                    feature_job(lins["attn_out"], s, z(UG, UG + 4), 4, 512, part)
            pe.wait_ge(sem("mix_ready"), 1)
            for s in range(4):
                feature_job(lins["w_out"], s, z(GC, GC + 8))
            rms()
            pe.wait_ge(sem("h_ready"), 2)

            def experts(m, x, wr, hr_name, hr_n):
                E = m.n
                pe.wait_ge(sem("moe_scratch_free"), 1 if m is m1 else 2)
                for a in range(2):
                    for k in range(KT):
                        tr = pe.transpose(ps(4 + 2 * a + k // 4, P, c0=(k % 4) * P), x[:, k, a * P:(a + 1) * P], IDENT[:, :])
                tr.then_inc(msem(m, "x_turned"), 1)
                for a in range(2):
                    for k in range(KT):
                        mm = pe.matmul(ps(0, E, c0=a * E), x[:, k, a * P:(a + 1) * P], wr[:, k, :],
                                       start=(k == 0), stop=(k == KT - 1))
                mm.then_inc(msem(m, "logits"), 1)
                pe.wait_ge(msem(m, "mask"), 1)
                for a in range(2):
                    pe.matmul(ps(1, E), ONES[:, :], MASK[:, a, 0:E], start=(a == 0), stop=(a == 1))
                pe.matmul(ps(1, E, c0=64), BEFORE[:, :], MASK[:, 0, 0:E], start=True, stop=True)
                pe.matmul(ps(1, E, c0=96), ONES[:, :], MASK[:, 0, 0:E], start=True, stop=False)
                pe.matmul(ps(1, E, c0=96), BEFORE[:, :], MASK[:, 1, 0:E], start=False, stop=True)\
                    .then_inc(msem(m, "counts"), 1)
                pe.wait_ge(msem(m, "table_cols"), 1)
                for j in range(2):
                    mm = pe.matmul(ps(2, P, 0, 1, j * P), TCOL[:, j:j + 1], IDENT[:, :], start=True, stop=True)
                mm.then_inc(msem(m, "table_rows"), 1)
                pe.wait_ge(msem(m, "tables"), 1)
                count = pe.value_load(TAB[0:1, 2 * P + 32:2 * P + 33], min_val=m.n, max_val=48)

                def gather(g1, last=None):
                    pe.wait_ge(msem(m, "pick"), g1)
                    for k in range(KT):
                        if last is not None and k % 4 == 0:
                            pe.wait_ge(msem(m, "added"), last * 4 + (3 + k // 4))
                        for a in range(2):
                            mm = pe.matmul(ps(6 + k // 4, CHUNK, c0=(k % 4) * CHUNK), HT[:, a, k * P:(k + 1) * P],
                                           PICK[:, a, :], start=(a == 0), stop=(a == 1))
                    mm.then_inc(msem(m, "gathered"), 1)

                def turn(g):
                    pe.wait_ge(msem(m, "pickg"), g + 1)
                    pe.nop(nofuse=True)
                    for a in range(2):
                        tr = pe.transpose(ps(6, P, c0=a * P), PICKG[:, a, :], IDENT[:, :])
                    tr.then_inc(msem(m, "turned"), 1)

                def scatter(g):
                    pe.wait_ge(msem(m, "turned_copied"), g + 1)
                    pe.wait_ge(msem(m, "ys_dve"), g + 1)
                    pe.wait_ge(msem(m, "ys_act"), g + 1)
                    for q in range(4):
                        if q >= 2:
                            pe.wait_ge(msem(m, "added"), g * 4 + (q - 1))
                        for j in range(2):
                            k = 2 * q + j
                            mm = pe.matmul(ps(6 + q % 2, T, c0=j * T), YS[:, k * P:(k + 1) * P], GT,
                                           start=True, stop=True)
                        mm.then_inc(msem(m, "scattered"), 1)

                def first_product(g, e, s):
                    pe.wait_ge(sem(f"arrived{s}"), e * 16 + (m.base[s] + 16))
                    halves = (0, 1) if m is m1 else (s // 4,)
                    n = SLOT if m is m1 else 1408
                    for i, k in enumerate(group_kts(m, s)):
                        for half in halves:
                            for j in range(m.ht):
                                w0 = group_at(m, s) + i * n + (half if m is m1 else 0) * 1024 + j * P
                                mm = pe.matmul(ps(m.up * half + j // 4, CHUNK, c0=(j % 4) * CHUNK), W[:, w0:w0 + P],
                                               XG[:, k, :], start=(k == 0 and j % 4 == 0), stop=(k == KT - 1),
                                               skip_group_check=True)
                    mm.then_inc(msem(m, "group_done"), 1)

                def second_product(g, e, s):
                    pe.wait_ge(sem(f"arrived{s}"), e * 16 + (m.base[s] + 16))
                    for i, k in enumerate(group_kts(m, s)):
                        if m is m1 and k % 4 == 0:
                            pe.wait_ge(msem(m, "hm"), g * 2 + (k // 4 + 1))
                        elif k == 0:
                            pe.wait_ge(msem(m, "hm"), g * 3 + 3)
                        elif k == 8:
                            pe.wait_ge(msem(m, "hm"), g * 3 + 4)
                        for half in range(2):
                            w0 = group_at(m, s) + i * D + half * 512
                            mm = pe.matmul(ps(m.out + half), HM[:, k, :], W[:, w0:w0 + 512],
                                           start=(k == 0), stop=(k == m.ht - 1), skip_group_check=True)
                    mm.then_inc(msem(m, "group_done"), 1)

                if m is m1:
                    pe.wait_ge(msem(m, "gates"), 1)
                    for a in range(2):
                        tr = pe.transpose(ps(3, P, 0, 32, a * P), GATE[:, a, :], IDENT[:, :])
                    tr.then_inc(sem("gates_turned"), 1)
                    pe.wait_ge(sem("gates_copied"), 1)
                    pe.wait_ge(sem("ld_bout"), 16)
                    for k in range(KT):
                        mm = pe.matmul(ps(4 + k // 2, T, c0=(k % 2) * T), BOUT[:, k * P:(k + 1) * P], GT[0:32, :],
                                       start=True, stop=True)
                    mm.then_inc(sem("bias_sum"), 1)
                    pe.wait_ge(sem("bias_copied"), 1)
                pe.wait_ge(msem(m, "ht_act"), 1)
                pe.wait_ge(msem(m, "ht_dve"), 1)
                gather(1)
                with pe.Fori(0, count) as g:
                    e = pe.value_load(TAB[0:1, bass.ds(g, 1)], min_val=0, max_val=m.n - 1)
                    pe.wait_ge(msem(m, "xg"), g + 1)
                    if m is m2:
                        pe.wait_ge(msem(m, "ys_dve"), g + 1)
                        pe.wait_ge(msem(m, "ys_act"), g + 1)
                    for s in range(2):
                        first_product(g, e, s)
                    turn(g)
                    for s in range(2, 4):
                        first_product(g, e, s)
                    scatter(g)
                    for s in range(4, 8):
                        first_product(g, e, s)
                    gather(g + 2, g)
                    for s in range(8, NG):
                        second_product(g, e, s)
                pe.wait_ge(msem(m, "xg"), count + 1)
                turn(count)
                scatter(count)

            experts(m1, H, WR1, "h_ready", 2)

            rms()
            layer_norm(X)

            def mixer2(l):
                pe.wait_ge(sem("x2_ready"), 2 * l + 1)
                for s in range(2):
                    feature_job(lins[f"qa{l}"], s, X)
                lin = lins[f"kva{l}"]
                feature_job(lin, 0, X, width=P)
                token_job(lin, 0, X, P, P, part=1)
                lin = lins[f"ret{l}"]
                for s in range(2):
                    feature_job(lin, s, X)
                for s in range(2, 4):
                    token_job(lin, s, X, 0, 256)

                def scores2(i):
                    g, q = i % 2, i // 2
                    n = HEADS * (l + 1) + i
                    r = g * HD
                    pe.wait_ge(sem("exp_done"), n - 1)
                    for a in range(2):
                        mm = pe.matmul(ps(4 + g, T, c0=a * T), Z[r:r + HD, (QA + q) * T + a * P:(QA + q) * T + (a + 1) * P],
                                       Z[r:r + HD, KA * T:(KA + 1) * T], start=True, stop=True)
                    mm.then_inc(sem("scores_ready"), 1)

                def ret_scores(h):
                    r = (h % 4) * RK
                    n = HEADS * l + h
                    if n:
                        pe.wait_ge(sem("ret_weighted"), n)
                    for a in range(2):
                        k0, q0 = (KR + h // 4) * T + a * P, (QR + h // 4) * T
                        mm = pe.matmul(ps(2, T, c0=a * T), Z[r:r + RK, k0:k0 + P], Z[r:r + RK, q0:q0 + T],
                                       start=True, stop=True, tile_position=(r, 0))
                    mm.then_inc(sem("ret_scores"), 1)

                def ret_values(h):
                    n = HEADS * l + h
                    r = (h % 2) * HD
                    pe.wait_ge(sem("ret_weighted"), n + 1)
                    if h % 2 == 0 and n:
                        pe.wait_ge(sem("ret_copied"), n // 2)
                    a = RA[:, h % 2]
                    v = VR[:, :, h * HD:(h + 1) * HD]
                    pe.matmul(ps(3, T, r, r + HD, 0), v[:, 0, :], a[:, 0, 0, :], start=True, stop=True, skip_group_check=True)
                    pe.matmul(ps(3, P, r, r + HD, P), v[:, 1, :], a[:, 0, 1, P:T], start=False, stop=True, skip_group_check=True)
                    pe.matmul(ps(3, T, r, r + HD, T), v[:, 1, :], a[:, 1, 1, :], start=True, stop=True, skip_group_check=True)
                    pe.matmul(ps(3, P, r, r + HD, T), v[:, 0, :], a[:, 1, 0, 0:P], start=False, stop=True,
                              skip_group_check=True).then_inc(sem("ret_values"), 1)

                lin = lins[f"gg{l}"]
                pe.wait_ge(sem("pair_copied"), 4 * (l + 1))
                for i in range(12):
                    feature_job(lin, i, X)
                    if i == 0:
                        e, c = job_evac[lin.job0 - 1]
                        pe.wait_ge(sem("evac_" + e), c)
                    if i < 8:
                        scores2(i)
                        ret_scores(i)
                    n = HEADS * (l + 1) + i
                    if 1 <= i < 9:
                        turn_probs(n - 1, 0, ((0, 0), (1, 0), (0, 1), (1, 1)))
                        ret_values(i - 1)
                    if 2 <= i < 10:
                        i2 = i - 2
                        g, q = i2 % 2, i2 // 2
                        values(n - 2, g, 4 * (l + 1) + q, g, VA[:, :, g * HD:(g + 1) * HD], ((0, 0, T, 0), (1, 0, T, T)))

                def head_sums(src):
                    norm[0] += 1
                    pe.wait_ge(sem("norm_in"), norm[0])
                    for k in range(KT):
                        mm = pe.matmul(ps(4 + k // 2, T, c0=(k % 2) * T), BLK[:, :], src[:, k, :], start=True, stop=True)
                    mm.then_inc(sem("norm_sum"), 1)

                head_sums(H)
                pe.wait_ge(sem("pair_copied"), 4 * (l + 2))
                lin = lins[f"wo_attn{l}"]
                for part in range(2):
                    feature_job(lin, 0, z(QA, QA + 4), 4, 512, part)
                head_sums(SQV)
                for part in range(2):
                    feature_job(lin, 1, z(QA, QA + 4), 4, 512, part)
                pe.wait_ge(sem("ret_out"), l + 1)
                for s in range(2):
                    for part in range(2):
                        feature_job(lins[f"wo_ret{l}"], s, z(QR, QR + 4), 4, 512, part)
                pe.wait_ge(sem("mix_ready"), l + 2)
                for s in range(4):
                    feature_job(lins[f"w_out{l}"], s, z(G2A, G2A + 8))
                layer_norm(X)
                pe.wait_ge(sem("x2_ready"), 2 * l + 2)

            mixer2(0)
            for s in range(11):
                feature_job(lins["ffn1"], s, X)
            for s in range(11):
                feature_job(lins["ffn3"], s, X)
            lin = lins["ffn2"]
            for s in range(11):
                w = weights(lin.slot0 + s).rearrange("p (k n) -> p k n", k=2)
                e, c = job_evac[lins["ffn3"].job0 + s]
                pe.wait_ge(sem("evac_" + e), max(c, job_evac[lin.job0 - 1][1] if s == 0 else 0))
                for i in range(2):
                    for j in range(KT):
                        k = 2 * s + i
                        mm = pe.matmul(ps(j // 2, T, c0=(j % 2) * T), w[:, i, j * P:(j + 1) * P],
                                       Z[:, k * T:(k + 1) * T], start=(k == 0 and j % 2 == 0), stop=(k == 21),
                                       skip_group_check=True)
                mm.then_inc(sem("lin_done"), 1)
            layer_norm(X)
            mixer2(1)
            experts(m2, X, WR2, "x2_ready", 4)
            layer_norm(X)

            pe.wait_ge(sem("x2_ready"), 5)
            for a in range(2):
                for k in range(KT):
                    tr = pe.transpose(ps(4 + 2 * a + k // 4, P, c0=(k % 4) * P), X[:, k, a * P:(a + 1) * P], IDENT[:, :])
            tr.then_inc(sem("out_turned"), 1)

        @block.scalar
        def _(act):
            ch = Chain(act, sem("act_step"))

            def rows_of(name, pat="l (r c) -> (l r) c"):
                return A[name].rearrange(pat, c=P)

            vec = [("c", 0, V_C, 8), ("b_ada", 0, V_BADA, 48), ("norm1_g", 0, V_N1G, 8), ("norm2_g", 0, V_N2G, 8),
                   ("final_g", 0, V_FG, 8), ("conv_b", 0, V_CB, 4), ("conv_ln_g", 0, V_CLG, 4),
                   ("conv_ln_b", 0, V_CLB, 4), ("ln_emb_g_2", 0, V_EG, 8), ("ln_emb_b_2", 0, V_EB, 8),
                   ("ln1_g_2", 1, 0, 16), ("ln1_b_2", 1, 16, 16), ("ln2_g_2", 1, 32, 16), ("ln2_b_2", 1, 48, 16),
                   ("b_gate_2", 1, 64, 32)]
            for name, tile, r, n in vec:
                src = rows_of(name, "(r c) -> r c" if len(A[name].shape) == 1 else "l (r c) -> (l r) c")
                act.dma_start(VROWS[r:r + n, tile, :], src).then_inc(sem("ld_vec"), 16)
            act.dma_start(VROWS[0:124, 2, :], A["conv_w"][0].rearrange("k (j c) -> (k j) c", c=P)).then_inc(sem("ld_vec"), 16)
            act.dma_start(VROWS[:, 3:7, :], A["b_exp_in"][0].rearrange("(t a) (j c) -> (a j) t c", t=4, c=P))\
                .then_inc(sem("ld_vec"), 16)
            act.dma_start(XT, A["x"][0].rearrange("(a p) d -> p a d", p=P)).then_inc(sem("ld_x"), 16)
            for name, c0, n in (("sink_logits_2", R_SINK, 16), ("decay_fwd_2", R_DECAY, 16), ("decay_bwd_2", R_DECAY + 16, 16),
                                ("b_router", R_BR1, 32), ("router_b_2", R_BR2, 8)):
                act.dma_start(ROWS[0:1, c0:c0 + n], A[name].rearrange("l h -> (l h)").unsqueeze(0)).then_inc(sem("ld_rows"), 16)
            act.dma_start(WF, w_in[0][:, 5 * CW:5 * CW + HEADS].rearrange("(k p) n -> p k n", p=P)).then_inc(sem("ld_small"), 16)
            act.dma_start(WR1[:, :, :], A["w_router"][0].rearrange("(k p) n -> p k n", p=P)).then_inc(sem("ld_small"), 16)
            act.dma_start(WR2[:, :, :], A["router_w_2"][0].rearrange("(k p) n -> p k n", p=P)).then_inc(sem("ld_small"), 16)
            act.dma_start(BFG[:, :], A["b_forget"].rearrange("l h -> h l")).then_inc(sem("ld_small"), 16)

            def linear_ready(lin, s, part=0):
                g = lin.group0 + (lin.groups if lin.k_major else s * lin.per + part + 1)
                act.wait_ge(sem("lin_done"), g)
                return (lin.job0 + s * lin.per + part) % 2

            sq = [0]

            def root():
                sq[0] += 1
                act.wait_ge(sem("root_in"), sq[0])
                act.activation(SQ[:, 0:T], SQ[:, 0:T], ACT.Sqrt).then_inc(sem("root_out"), 1)

            act.wait_ge(sem("vec_turned"), 1)
            V = PS[:, 0:3, :].rearrange("p b n -> p (b n)")
            act.activation(VEC[:, 0:108], V[:, 0:108], ACT.Copy)
            act.activation(VEC[:, P:P + 96], V[:, P:P + 96], ACT.Copy)
            act.activation(VEC[:, 2 * P:2 * P + 124], V[:, 2 * P:2 * P + 124], ACT.Copy)
            act.activation(VEC[:, 3 * P:4 * P], V[:, 3 * P:4 * P], ACT.Copy)
            ch.link(act.activation(VEC[:, 4 * P:7 * P], V[:, 4 * P:7 * P], ACT.Copy))
            act.wait_ge(sem("rows_spread"), 1)
            ch.link(act.activation(ROWB[:, :], ps(3, R_N), ACT.Copy))
            act.activation(CSIL[:, :], VEC[:, V_C:V_C + 8], ACT.Silu).then_inc(sem("init_act"), 1)
            act.wait_ge(sem("logsig_in"), 1)
            act.activation(SQ[:, 32:64], SQ[:, 0:32], ACT.Exp, scale=-1.0).then_inc(sem("logsig_exp"), 1)
            root()

            lin = lins["uqkv"]
            dst = [z(UV, UV + 2), z(UV + 2, UV + 4), z(UG, UG + 2), z(UG + 2, UG + 4),
                   z(Q1, Q1 + 2), z(Q1 + 2, Q1 + 4), z(K1, K1 + 2), z(K1 + 2, K1 + 4),
                   VT1[:, :, 0:256], VT1[:, :, 256:512]]
            for s in range(10):
                b = linear_ready(lin, s)
                act.activation(dst[s], ps2(b), ACT.Sigmoid if s in (2, 3) else ACT.Copy).then_inc(sem("evac_act"), 1)
            b = linear_ready(lins["forget"], 0)
            act.wait_ge(sem("ld_small"), 16 * 4)
            act.activation(SQ[0:8, 0:T], PS[0:8, b, 0:T], ACT.Identity, bias=BFG[:, 0:1]).then_inc(sem("evac_act"), 1)
            act.wait_ge(sem("logsig_in"), 2)
            act.activation(SQ[0:8, 2 * T:3 * T], SQ[0:8, T:2 * T], ACT.Exp, scale=-1.0).then_inc(sem("logsig_exp"), 1)

            lin = lins["gates"]
            for i in range(10):
                if i < 8:
                    b = linear_ready(lin, i)
                    act.activation(z(GC + 2 * i, GC + 2 * i + 2), ps2(b), ACT.Sigmoid).then_inc(sem("evac_act"), 1)
                    h = i
                    act.wait_ge(sem("max_ready"), h + 1)
                    b = 4 + h % 2
                    st = ST[:, h % 2, :]
                    if h >= 2:
                        act.wait_ge(sem("probs_turned"), h - 1)
                    act.activation(PROB[:, h % 2, 0, 0:P], ps(b, P), ACT.Exp, bias=st[:, 2:3], scale=QSCALE,
                                   accum_out=st[:, 4:5])
                    act.activation(PROB[:, h % 2, 1, :], ps(b, T, c0=P), ACT.Exp, bias=st[:, 3:4], scale=QSCALE,
                                   accum_out=st[:, 5:6]).then_inc(sem("exp_done"), 1)
                if 1 <= i < 9:
                    n = i - 1
                    act.wait_ge(sem("probs_turned"), n + 1)
                    if n >= 2:
                        act.wait_ge(sem("values_done"), n - 1)
                    act.activation(PROBT[:, n % 2, 0:3 * P], ps(6, 3 * P), ACT.Copy).then_inc(sem("probs_copied"), 1)

            root()
            act.wait_ge(sem("conv_normed"), 1)
            for j in range(4):
                a = act.activation(Z[:, (UV + j) * T:(UV + j + 1) * T], Z[:, (UV + j) * T:(UV + j + 1) * T], ACT.Silu,
                                   bias=VEC[:, V_CLB + j:V_CLB + j + 1], scale=VEC[:, V_CLG + j:V_CLG + j + 1])
            a.then_inc(sem("conv_ready"), 1)
            act.dma_start(BOUT, A["b_exp_out"][0]).then_inc(sem("ld_bout"), 16)
            root()

            def experts(m):
                act.wait_ge(msem(m, "x_turned"), 1)
                act.activation(HT[:, 0, :], PS[:, 4:6, :].rearrange("p b n -> p (b n)"), ACT.Copy).then_inc(msem(m, "ht_act"), 1)
                act.wait_ge(msem(m, "top"), 1)
                for a in range(2):
                    e = act.activation(GATE[:, a, 0:m.n], LOG[:, a, 0:m.n], ACT.Exp, bias=NTOP[:, a:a + 1])
                e.then_inc(msem(m, "gate_exp"), 1)
                act.wait_ge(msem(m, "tables"), 1)
                count = act.value_load(TAB[0:1, 2 * P + 32:2 * P + 33], min_val=m.n, max_val=48)

                if m is m1:
                    act.wait_ge(sem("gates_turned"), 1)
                    act.activation(GT[0:32, :], ps(3, T, 0, 32), ACT.Copy).then_inc(sem("gates_copied"), 1)

                def gathered(g1):
                    act.wait_ge(msem(m, "gathered"), g1)
                    act.activation(XG.rearrange("p k c -> p (k c)"), PS[:, 6:8, :].rearrange("p b n -> p (b n)"), ACT.Copy)\
                        .then_inc(msem(m, "xg"), 1)

                def turned(g):
                    act.wait_ge(msem(m, "turned"), g + 1)
                    act.activation(GT, ps(6, T), ACT.Copy).then_inc(msem(m, "turned_copied"), 1)

                act.wait_ge(msem(m, "ys_dve"), 1)
                act.activation(YS[:, 512:1024], YS[:, 0:512], ACT.Copy).then_inc(msem(m, "ys_act"), 1)
                gathered(1)
                with act.Fori(0, count) as g:
                    turned(g)
                    if m is m1:
                        for i in range(2):
                            act.wait_ge(msem(m, "gate_part"), g * 2 + (i + 1))
                            act.activation(PART[:, 1024 + i * 512:1536 + i * 512], PART[:, i * 512:i * 512 + 512],
                                           ACT.Sigmoid, scale=1.702).then_inc(msem(m, "sig"), 1)
                    else:
                        act.wait_ge(msem(m, "group_done"), g * NG + 8)
                        act.wait_ge(msem(m, "hm"), g * 3 + 1)
                        for i in range(3):
                            n = min(512, 1408 - i * 512)
                            act.activation(PART[:, i * 512:i * 512 + n], ps(i, n), ACT.Silu).then_inc(msem(m, "sig"), 1)
                    gathered(g + 2)
                    act.wait_ge(msem(m, "group_done"), g * NG + NG)
                    act.activation(YS[:, 512:1024], ps(m.out + 1), ACT.Copy).then_inc(msem(m, "ys_act"), 1)
                turned(count)

            experts(m1)
            root()
            root()

            def mixer2(l):
                def copy(lin, s, dst, f=ACT.Copy, part=0):
                    b = linear_ready(lin, s, part)
                    act.activation(dst, ps2(b), f).then_inc(sem("evac_act"), 1)

                for s in range(2):
                    copy(lins[f"qa{l}"], s, z(QA + 2 * s, QA + 2 * s + 2))
                b = linear_ready(lins[f"kva{l}"], 0, 0)
                act.activation(Z[:, KA * T:(KA + 1) * T], ps(b, T), ACT.Copy).then_inc(sem("evac_act"), 1)
                b = linear_ready(lins[f"kva{l}"], 0, 1)
                act.activation(VA, PS[:, b, 0:T].rearrange("p (a n) -> p a n", a=2), ACT.Copy).then_inc(sem("evac_act"), 1)
                lin = lins[f"ret{l}"]
                copy(lin, 0, z(QR, QR + 2))
                copy(lin, 1, z(KR, KR + 2))
                copy(lin, 2, VR[:, :, 0:256])
                copy(lin, 3, VR[:, :, 256:512])
                lin = lins[f"gg{l}"]
                for i in range(12):
                    if i < 4:
                        copy(lin, i, z(GF + 2 * i, GF + 2 * i + 2), ACT.Silu)
                    else:
                        b = linear_ready(lin, i)
                        for j in range(2):
                            t = 2 * (i - 4) + j
                            a = act.activation(Z[:, (G2A + t) * T:(G2A + t + 1) * T], ps(b, T, c0=j * T), ACT.Sigmoid,
                                               bias=VEC[:, V_BG + 16 * l + t:V_BG + 16 * l + t + 1])
                        a.then_inc(sem("evac_act"), 1)
                    if i < 8:
                        h = 4 * (i % 2) + i // 2
                        n = HEADS * (l + 1) + i
                        rn = HEADS * l + i
                        if i >= 2:
                            act.wait_ge(sem("ret_weighted"), rn - 1)
                        for d in range(2):
                            c = 16 * d + HEADS * l + i
                            for j in range(2):
                                a = act.activation(DEC[:, i % 2, (2 * d + j) * P:(2 * d + j + 1) * P], LAGS[:, 2 * d + j, :],
                                                   ACT.Exp, scale=LG[:, c:c + 1])
                        a.then_inc(sem("decay_exp"), 1)
                        st = ST[:, i % 2, :]
                        act.wait_ge(sem("max_ready"), n + 1)
                        act.activation(st[:, 6:8], st[:, 2:4], ACT.Exp, bias=ROWB[:, R_SINK + HEADS * l + h:R_SINK + HEADS * l + h + 1])
                        for a_ in range(2):
                            a = act.activation(PROB[:, i % 2, a_, :], PROB[:, i % 2, a_, :], ACT.Exp, bias=st[:, 2 + a_:3 + a_],
                                               scale=QSCALE, accum_out=st[:, 4 + a_:5 + a_])
                        a.then_inc(sem("exp_done"), 1)
                    if 1 <= i < 9:
                        n = HEADS * (l + 1) + i - 1
                        act.wait_ge(sem("probs_turned"), n + 1)
                        act.wait_ge(sem("values_done"), n - 1)
                        act.activation(PROBT[:, n % 2, :], ps(6), ACT.Copy).then_inc(sem("probs_copied"), 1)
                        if i % 2 == 0:
                            pr = i // 2 - 1
                            act.wait_ge(sem("ret_values"), HEADS * l + i)
                            for d in range(2):
                                a = act.activation(H[:, 4 * d + pr, :], ps(3, T, c0=d * T), ACT.Copy)
                            a.then_inc(sem("ret_copied"), 1)
                sq[0] += 1
                act.wait_ge(sem("root_in"), sq[0])
                act.activation(SQ[:, :], SQ[:, :], ACT.Sqrt).then_inc(sem("root_out"), 1)
                root()

            mixer2(0)
            for s in range(11):
                b = linear_ready(lins["ffn1"], s)
                act.activation(z(2 * s, 2 * s + 2), ps2(b), ACT.Silu).then_inc(sem("evac_act"), 1)
            root()
            mixer2(1)
            experts(m2)
            root()
            act.wait_ge(sem("out_turned"), 1)
            for b in range(4):
                act.activation(XT[:, b // 2, (b % 2) * 512:(b % 2) * 512 + 512], ps(4 + b), ACT.Copy)\
                    .then_inc(sem("out_staged"), 1)

        @block.vector
        def _(dve):
            ch = Chain(dve, sem("dve_step"))
            link = ch.link
            norm, rt = [0], [0]
            SQV = SQ[:, :].rearrange("p (k t) -> p k t", t=T)

            def log_sigmoid(y, t, n, k):
                link(dve.scalar_tensor_tensor(out=t[0], in0=y, scalar=-1.0, in1=y, op0=ALU.mult, op1=ALU.max))
                dve.tensor_scalar(t[0], t[0], 0.0, None, ALU.max).then_inc(sem("logsig_in"), 1)
                dve.wait_ge(sem("logsig_exp"), k)
                link(dve.tensor_scalar(t[2], t[1], 2.0, None, ALU.add))
                link(dve.reciprocal(t[2], t[2]))
                link(dve.tensor_tensor(t[1], t[1], t[2], ALU.mult))
                link(dve.tensor_tensor(t[2], t[1], t[1], ALU.mult))
                link(dve.tensor_scalar(t[3], t[2], 1.0 / 17.0, None, ALU.mult))
                for c in (15, 13, 11, 9, 7, 5, 3):
                    link(dve.scalar_tensor_tensor(out=t[3], in0=t[3], scalar=1.0 / c, in1=t[2], op0=ALU.add, op1=ALU.mult))
                link(dve.scalar_tensor_tensor(out=t[3], in0=t[3], scalar=1.0, in1=t[1], op0=ALU.add, op1=ALU.mult))
                link(dve.tensor_scalar(t[2], y, 0.0, None, ALU.min))
                link(dve.scalar_tensor_tensor(out=t[4], in0=t[3], scalar=-2.0, in1=t[2], op0=ALU.mult, op1=ALU.add))

            def sums():
                norm[0] += 1
                dve.wait_ge(sem("norm_sum"), norm[0])

            def reciprocal_root(sum_, n, w=T):
                for o, s in sum_:
                    i = dve.tensor_scalar(o, s, 1.0 / n, EPS, ALU.mult, ALU.add)
                i.then_inc(sem("root_in"), 1)
                rt[0] += 1
                dve.wait_ge(sem("root_out"), rt[0])
                link(dve.reciprocal(SQ[:, 0:w], SQ[:, 0:w]))

            def rms(src, dst, gain, bias):
                dve.tensor_tensor(SQV, src, src, ALU.mult).then_inc(sem("norm_in"), 1)
                sums()
                reciprocal_root([(SQ[:, 0:T], ps(4, T))], D)
                link(dve.tensor_tensor(dst, src, bc(SQ[:, 0:T], KT), ALU.mult))
                return affine(dst, gain, bias)

            def affine(dst, gain, bias):
                for k in range(dst.shape[1]):
                    if bias is None:
                        i = dve.tensor_scalar(dst[:, k, :], dst[:, k, :], gain[:, k:k + 1], None, ALU.mult)
                    else:
                        i = dve.tensor_scalar(dst[:, k, :], dst[:, k, :], gain[:, k:k + 1], bias[:, k:k + 1], ALU.mult, ALU.add)
                return i

            def centre(x, nk, n):
                sums()
                link(dve.scalar_tensor_tensor(out=x, in0=bc(ps(4, T), nk), scalar=-1.0 / n, in1=x,
                                              op0=ALU.mult, op1=ALU.add))
                dve.tensor_tensor(SQV[:, 0:nk, :], x, x, ALU.mult).then_inc(sem("norm_in"), 1)
                sums()
                reciprocal_root([(SQ[:, 0:T], ps(4, T, c0=T))], n)
                return dve.tensor_tensor(x, x, bc(SQ[:, 0:T], nk), ALU.mult)

            def layer_norm(x, g, b, ready):
                link(centre(x, KT, D))
                affine(x, g, b).then_inc(sem(ready), 1)

            def linear_ready(lin, s, part=0):
                g = lin.group0 + (lin.groups if lin.k_major else s * lin.per + part + 1)
                dve.wait_ge(sem("lin_done"), g)
                return (lin.job0 + s * lin.per + part) % 2

            dve.wait_ge(sem("pool_step"), 18)
            link(dve.tensor_scalar(LAGS[:, 0, :], LAGS[:, 0, :], 0.0, None, ALU.max))
            link(dve.tensor_scalar(LAGS[:, 3, :], LAGS[:, 3, :], 0.0, None, ALU.max))
            dve.wait_ge(sem("pool_step"), 19)
            dve.scalar_tensor_tensor(out=DIST[:, :, :], in0=DIST[:, :, :], scalar=-1.0, in1=DIST[:, :, :],
                                     op0=ALU.mult, op1=ALU.max).then_inc(sem("dist_abs"), 1)
            dve.wait_ge(sem("init_act"), 1)
            log_sigmoid(ROWB[:, R_DECAY:R_DECAY + 32],
                        [SQ[:, 0:32], SQ[:, 32:64], SQ[:, 64:96], SQ[:, 96:128], LG[:, :]], 32, 1)
            dve.wait_ge(sem("x_turned"), 1)
            for b in range(4):
                i = dve.tensor_copy(X[:, 2 * b:2 * b + 2, :], ps2(4 + b))
            i.then_inc(sem("x_ready"), 1)
            dve.wait_ge(sem("x_ready"), 1)

            def ada(l):
                b = linear_ready(lins[f"ada{l}"], 0)
                dve.tensor_tensor(MOD[:, 16 * l:16 * l + 16], ps(b, 16), VEC[:, V_BADA + 16 * l:V_BADA + 16 * l + 16],
                                  ALU.add).then_inc(sem("evac_dve"), 1)
                dve.wait_ge(sem("evac_dve"), l + 1)

            ada(0)
            link(dve.scalar_tensor_tensor(out=GS[:, 0:8], in0=MOD[:, 8:16], scalar=1.0, in1=VEC[:, V_N1G:V_N1G + 8],
                                          op0=ALU.add, op1=ALU.mult))
            rms(X[:, :, :], H[:, :, :], GS[:, 0:8], MOD[:, 0:8]).then_inc(sem("h_ready"), 1)

            dve.wait_ge(sem("evac_act"), 4)
            link(dve.tensor_tensor(CONV_IN[:, :, TAPS - 1:], z(UV, UV + 4), z(UG, UG + 4), ALU.mult))
            conv = [0]

            def taps(n):
                for k in range(conv[0], min(conv[0] + n, TAPS)):
                    for j in range(4):
                        o = Z[:, (UV + j) * T:(UV + j + 1) * T]
                        w = VEC[:, V_CONVW + 4 * k + j:V_CONVW + 4 * k + j + 1]
                        if k == 0:
                            i = dve.tensor_scalar(o, CONV_IN[:, j, 0:T], w, VEC[:, V_CB + j:V_CB + j + 1], ALU.mult, ALU.add)
                        else:
                            dve.wait_ge(sem("tap"), 4 * (k - 1) + j + 1)
                            i = dve.scalar_tensor_tensor(out=o, in0=CONV_IN[:, j, k:k + T], scalar=w, in1=o,
                                                         op0=ALU.mult, op1=ALU.add)
                        i.then_inc(sem("tap"), 1)
                conv[0] = min(conv[0] + n, TAPS)

            taps(9)
            dve.wait_ge(sem("evac_act"), 11)
            R = [SQ[0:8, i * T:(i + 1) * T] for i in range(8)]
            log_sigmoid(R[0], R[1:6], 256, 2)
            link(dve.memset(R[6], 1.0))
            link(dve.tensor_tensor_scan(R[7], R[6], R[5], 0.0, ALU.mult, ALU.add))
            dve.tensor_scalar(NEGF[0:8, :], R[7], -1.0 / QSCALE, None, ALU.mult).then_inc(sem("negf_ready"), 1)

            def normalise(n, widths):
                st = ST[:, n % 2, :]
                link(dve.reciprocal(st[:, 0:2], st[:, 4:6]))
                for a in range(2):
                    o = PROB[:, n % 2, a, 0:widths[a]]
                    i = dve.tensor_scalar(o, o, st[:, a:a + 1], None, ALU.mult)
                i.then_inc(sem("probs_ready"), 1)

            for i in range(10):
                if i < 8:
                    h = i
                    st = ST[:, h % 2, :]
                    dve.wait_ge(sem("scores_ready"), h + 1)
                    dve.reduce_max(st[:, 0:1], ps(4 + h % 2, P), AX)
                    link(dve.reduce_max(st[:, 1:2], ps(4 + h % 2, T, c0=P), AX))
                    dve.tensor_scalar(st[:, 2:4], st[:, 0:2], -QSCALE, None, ALU.mult).then_inc(sem("max_ready"), 1)
                    taps(2)
                    dve.wait_ge(sem("exp_done"), h + 1)
                    normalise(h, (P, T))
                if i >= 2 and i % 2 == 1:
                    p = (i - 3) // 2
                    dve.wait_ge(sem("values_done"), 2 * p + 2)
                    dve.tensor_copy(Z[:, (UG + p) * T:(UG + p + 1) * T], ps(7, T, c0=(p % 2) * T)).then_inc(sem("pair_copied"), 1)
            taps(TAPS)
            dve.wait_ge(sem("tap"), 4 * TAPS)
            link(dve.tensor_copy(GS[:, 16:17], GS[:, 0:1]))
            dve.tensor_copy(GS[:, 17:18], GS[:, 0:1]).then_inc(sem("norm_in"), 1)
            ada(1)
            ada(2)
            centre(z(UV, UV + 4), 4, CW).then_inc(sem("conv_normed"), 1)

            def gated(lin, g0, acc=None):
                for s in range(2):
                    for part in range(2):
                        b = linear_ready(lin, s, part)
                        t = 4 * s + 2 * part
                        o = z(g0 + t, g0 + t + 2)
                        i = dve.tensor_tensor(o, ps2(b), o, ALU.mult)
                        i.then_inc(sem("evac_dve"), 1)

            gated(lins["conv_out"], GC)
            gated(lins["attn_out"], GA)
            dve.wait_ge(sem("evac_dve"), job_evac[lins["attn_out"].job0 + 3][1])
            dve.tensor_tensor(z(GC, GC + 8), z(GC, GC + 8), z(GA, GA + 8), ALU.add).then_inc(sem("mix_ready"), 1)
            lin = lins["w_out"]
            for s in range(4):
                b = linear_ready(lin, s)
                for j in range(2):
                    k = 2 * s + j
                    i = dve.scalar_tensor_tensor(out=X[:, k, :], in0=ps(b, T, c0=j * T), scalar=MOD[:, 16 + k:17 + k],
                                                 in1=X[:, k, :], op0=ALU.mult, op1=ALU.add)
                i.then_inc(sem("evac_dve"), 1)
            dve.wait_ge(sem("evac_dve"), job_evac[lin.job0 + 3][1])
            link(dve.scalar_tensor_tensor(out=GS[:, 8:16], in0=MOD[:, 32:40], scalar=1.0, in1=VEC[:, V_N2G:V_N2G + 8],
                                          op0=ALU.add, op1=ALU.mult))
            rms(X[:, :, :], H[:, :, :], GS[:, 8:16], MOD[:, 24:32]).then_inc(sem("h_ready"), 1)

            def experts(m, br):
                E, top = m.n, m.top
                dve.wait_ge(sem("h_ready") if m is m1 else sem("x2_ready"), 2 if m is m1 else 4)
                if m is m2:
                    link(dve.memset(Y, 0.0))
                link(dve.memset(LOG[:, :, E:E + 8], NEG))
                link(dve.memset(ONE32, 1.0))
                dve.memset(YS[:, 0:512], 0.0).then_inc(msem(m, "ys_dve"), 1)
                dve.memset(PICKG, 0.0).then_inc(msem(m, "pickg"), 1)
                if m is m2:
                    dve.memset(PART[:, 0:1], 0.0).then_inc(msem(m, "hm"), 1)
                for name in ("ys_dve", "pickg") + (("hm",) if m is m2 else ()):
                    dve.wait_ge(msem(m, name), 1)
                dve.memset(FREE, 0.0).then_inc(sem("moe_scratch_free"), 1)
                dve.wait_ge(sem("moe_scratch_free"), 1 if m is m1 else 2)
                dve.wait_ge(msem(m, "x_turned"), 1)
                dve.tensor_copy(HT[:, 1, :], PS[:, 6:8, :].rearrange("p b n -> p (b n)")).then_inc(msem(m, "ht_dve"), 1)
                dve.wait_ge(msem(m, "logits"), 1)
                link(dve.tensor_tensor(LOG[:, :, 0:E], PS[:, 0, 0:2 * E].rearrange("p (a e) -> p a e", a=2),
                                       bc(ROWB[:, br:br + E], 2), ALU.add))
                for a in range(2):
                    link(dve.max(TOP8[:, a, :], LOG[:, a, 0:E]))
                link(dve.tensor_scalar(NTOP, TOP8[:, :, 0], -1.0, None, ALU.mult))
                dve.memset(TOP8[:, :, top:8], NEG).then_inc(msem(m, "top"), 1)
                dve.wait_ge(msem(m, "top"), 1)
                for a in range(2):
                    link(dve.match_replace(LOGR[:, a, 0:E + 8], TOP8[:, a, :], LOG[:, a, 0:E + 8], 3e38))
                dve.tensor_tensor(MASK[:, :, 0:E], LOGR[:, :, 0:E], LOG[:, :, 0:E], ALU.not_equal).then_inc(msem(m, "mask"), 1)
                dve.wait_ge(msem(m, "mask"), 1)
                dve.wait_ge(msem(m, "gate_exp"), 1)
                link(dve.tensor_tensor(GATE[:, :, 0:E], GATE[:, :, 0:E], MASK[:, :, 0:E], ALU.mult))
                link(dve.reduce_sum(GSUM, GATE[:, :, 0:E], AX))
                link(dve.reciprocal(GSUM, GSUM))
                dve.tensor_tensor(GATE[:, :, 0:E], GATE[:, :, 0:E], bl(GSUM, E), ALU.mult).then_inc(msem(m, "gates"), 1)
                dve.wait_ge(msem(m, "gates"), 1)
                dve.wait_ge(msem(m, "counts"), 1)
                n = ps(1, E)
                link(dve.tensor_scalar(NCH[:, 0:E], n, float(CHUNK), 1.0, ALU.is_gt, ALU.add))
                link(dve.tensor_tensor_scan(CUM[:, 0:E], ONE32[:, 0:E], NCH[:, 0:E], 0.0, ALU.mult, ALU.add))
                link(dve.tensor_tensor(START[:, 0:E], CUM[:, 0:E], NCH[:, 0:E], ALU.subtract))
                for a in range(2):
                    link(dve.scalar_tensor_tensor(out=RANK[:, a, 0:E], in0=ps(1, E, c0=64 + 32 * a), scalar=1.0,
                                                  in1=MASK[:, a, 0:E], op0=ALU.add, op1=ALU.mult))
                link(dve.tensor_scalar(RANK[:, :, 0:E], RANK[:, :, 0:E], -1.0, None, ALU.add))
                link(dve.tensor_scalar(LE[:, 0:E], CUM[:, 0:E], IOTAP[:, 0:1], None, ALU.is_le))
                link(dve.tensor_tensor(LEN_[:, 0:E], LE[:, 0:E], NCH[:, 0:E], ALU.mult))
                link(dve.reduce_sum(TCOL[:, 0:1], LE[:, 0:E], AX))
                link(dve.reduce_sum(TCOL[:, 1:2], LEN_[:, 0:E], AX))
                link(dve.tensor_scalar(TCOL[:, 0:1], TCOL[:, 0:1], float(E - 1), None, ALU.min))
                link(dve.tensor_tensor(TCOL[:, 1:2], IOTAP[:, 0:1], TCOL[:, 1:2], ALU.subtract))
                dve.tensor_scalar(TCOL[:, 1:2], TCOL[:, 1:2], 1.0, float(CHUNK), ALU.min, ALU.mult)\
                    .then_inc(msem(m, "table_cols"), 1)
                dve.wait_ge(msem(m, "table_rows"), 1)
                link(dve.tensor_copy(TAB[0:1, 0:2 * P], ps(2, 2 * P, 0, 1)))
                link(dve.tensor_scalar(TAB[0:1, 2 * P:2 * P + E], START[0:1, 0:E], -1.0, None, ALU.add))
                link(dve.tensor_scalar(TAB[0:1, 2 * P + 33:2 * P + 34], CUM[0:1, E - 1:E], -1.0, None, ALU.add))
                dve.tensor_copy(TAB[0:1, 2 * P + 32:2 * P + 33], CUM[0:1, E - 1:E]).then_inc(msem(m, "tables"), 1)
                dve.wait_ge(msem(m, "tables"), 1)
                count = dve.value_load(TAB[0:1, 2 * P + 32:2 * P + 33], min_val=m.n, max_val=48)
                dve.wait_ge(msem(m, "iota"), 1)
                if m is m1:
                    dve.wait_ge(sem("bias_sum"), 1)
                    dve.tensor_copy(Y.rearrange("p k t -> p (k t)"), PS[:, 4:8, :].rearrange("p b n -> p (b n)"))\
                        .then_inc(sem("bias_copied"), 1)
                    dve.wait_ge(sem("bias_copied"), 1)

                def pick(e, c):
                    for a in range(2):
                        i = dve.tensor_scalar(PICK[:, a, :], IOTA[:, bass.ds(c, CHUNK)], RANK[:, a, bass.ds(e, 1)], None,
                                              ALU.is_equal)
                    i.then_inc(msem(m, "pick"), 1)

                def pick_gated(e, c):
                    for a in range(2):
                        i = dve.tensor_scalar(PICKG[:, a, :], IOTA[:, bass.ds(c, CHUNK)], RANK[:, a, bass.ds(e, 1)],
                                              GATE[:, a, bass.ds(e, 1)], ALU.is_equal, ALU.mult)
                    i.then_inc(msem(m, "pickg"), 1)

                def add(g):
                    for q in range(4):
                        dve.wait_ge(msem(m, "scattered"), g * 4 + (q + 1))
                        o = Y[:, 2 * q:2 * q + 2, :]
                        dve.tensor_tensor(o, o, ps2(6 + q % 2), ALU.add).then_inc(msem(m, "added"), 1)

                pick(0, 0)
                mch = Chain(dve, msem(m, "dve_step"))
                with dve.Fori(0, count) as g:
                    e = dve.value_load(TAB[0:1, bass.ds(g, 1)], min_val=0, max_val=m.n - 1)
                    c = dve.value_load(TAB[0:1, bass.ds(g + P, 1)], min_val=0, max_val=CHUNK)
                    mch.enter(g * 7)
                    dve.wait_ge(msem(m, "turned"), g + 1)
                    pick_gated(e, c)
                    if m is m1:
                        mch.link(dve.tensor_copy(B1C, VEC[:, bass.ds(e * 16 + V_B1, 16)]))
                    e1 = dve.value_load(TAB[0:1, bass.ds(g + 1, 1)], min_val=0, max_val=m.n - 1)
                    c1 = dve.value_load(TAB[0:1, bass.ds(g + (P + 1), 1)], min_val=0, max_val=CHUNK)
                    dve.wait_ge(msem(m, "gathered"), g + 1)
                    pick(e1, c1)
                    add(g)
                    dve.wait_ge(msem(m, "group_done"), g * NG + 8)
                    if m is m1:
                        def tiles(ap):
                            return ap.rearrange("p (k c) -> p k c", c=CHUNK)

                        def gate_part(i):
                            ga = tiles(PART[:, i * 512:(i + 1) * 512])
                            mch.link(dve.tensor_tensor(ga, tiles(ps(i)), bl(B1C[:, 4 * i:4 * i + 4], CHUNK), ALU.add))
                            dve.tensor_scalar(ga, ga, 7.0, None, ALU.min).then_inc(msem(m, "gate_part"), 1)

                        def up_part(i):
                            up = HM[:, 4 * i:4 * i + 4, :]
                            mch.link(dve.tensor_tensor(up, tiles(ps(2 + i)), bl(B1C[:, 8 + 4 * i:12 + 4 * i], CHUNK), ALU.add))
                            mch.link(dve.tensor_scalar(up, up, 7.0, -7.0, ALU.min, ALU.max))
                            dve.wait_ge(msem(m, "gate_part"), g * 2 + (i + 1))
                            dve.scalar_tensor_tensor(out=up, in0=up, scalar=1.0, in1=tiles(PART[:, i * 512:(i + 1) * 512]),
                                                     op0=ALU.add, op1=ALU.mult).then_inc(msem(m, "up_part"), 1)
                            dve.wait_ge(msem(m, "up_part"), g * 2 + (i + 1))
                            dve.wait_ge(msem(m, "sig"), g * 2 + (i + 1))
                            dve.tensor_tensor(up, up, tiles(PART[:, 1024 + i * 512:1536 + i * 512]), ALU.mult)\
                                .then_inc(msem(m, "hm"), 1)

                        for i in range(2):
                            gate_part(i)
                            up_part(i)
                        assert mch.n == 7
                    else:
                        for i in range(3):
                            n = min(512, 1408 - i * 512)
                            dve.wait_ge(msem(m, "sig"), g * 3 + (i + 1))
                            dve.tensor_tensor(HM.rearrange("p k c -> p (k c)")[:, i * 512:i * 512 + n], ps(3 + i, n),
                                              PART[:, i * 512:i * 512 + n], ALU.mult).then_inc(msem(m, "hm"), 1)
                    dve.wait_ge(msem(m, "group_done"), g * NG + NG)
                    dve.tensor_copy(YS[:, 0:512], ps(m.out)).then_inc(msem(m, "ys_dve"), 1)
                add(count)
                dve.wait_ge(msem(m, "added"), count * 4 + 4)

            experts(m1, R_BR1)
            for k in range(KT):
                i = dve.scalar_tensor_tensor(out=X[:, k, :], in0=Y[:, k, :], scalar=MOD[:, 40 + k:41 + k], in1=X[:, k, :],
                                             op0=ALU.mult, op1=ALU.add)
            link(i)
            i = rms(X[:, :, :], X[:, :, :], VEC[:, V_FG:V_FG + 8], None)
            i.then_inc(sem("norm_in"), 1)
            dve.wait_ge(sem("norm_in"), norm[0] + 1)
            layer_norm(X[:, :, :], VEC[:, V_EG:V_EG + 8], VEC[:, V_EB:V_EB + 8], "x2_ready")

            def vcols(c, l):
                return VEC[:, c + 8 * l:c + 8 * l + 8]

            def residual(lin, ready):
                for s in range(4):
                    b = linear_ready(lin, s)
                    o = X[:, 2 * s:2 * s + 2, :]
                    dve.scalar_tensor_tensor(out=o, in0=o, scalar=ALPHA, in1=ps2(b), op0=ALU.mult, op1=ALU.add)\
                        .then_inc(sem("evac_dve"), 1)
                dve.wait_ge(sem("evac_dve"), job_evac[lin.job0 + lin.jobs - 1][1])

            def x_in():
                dve.tensor_copy(GS[:, 16:17], GS[:, 0:1]).then_inc(sem("norm_in"), 1)

            def mixer2(l):
                dve.wait_ge(sem("dist_ready"), 1)
                for i in range(12):
                    n = HEADS * (l + 1) + i
                    if i < 8:
                        h = 4 * (i % 2) + i // 2
                        st = ST[:, i % 2, :]
                        dve.wait_ge(sem("scores_ready"), n + 1)
                        dve.wait_ge(sem("probs_turned"), n - 1)
                        pr = PROB[:, i % 2]
                        link(dve.scalar_tensor_tensor(out=pr, in0=DIST[:, :, :], scalar=-SLOPES[h] / QSCALE, in1=ps2(4 + i % 2),
                                                      op0=ALU.mult, op1=ALU.add))
                        link(dve.reduce_max(st[:, 0:2], pr, AX))
                        sk = ROWB[:, R_SINK + HEADS * l + h:R_SINK + HEADS * l + h + 1]
                        link(dve.tensor_scalar(st[:, 0:2], st[:, 0:2], QSCALE, sk, ALU.mult, ALU.max))
                        dve.tensor_scalar(st[:, 2:4], st[:, 0:2], -1.0, None, ALU.mult).then_inc(sem("max_ready"), 1)
                        rn = HEADS * l + i
                        dve.wait_ge(sem("ret_scores"), rn + 1)
                        dve.wait_ge(sem("decay_masked"), rn + 1)
                        if i >= 2:
                            dve.wait_ge(sem("ret_values"), rn - 1)
                        dec, ra = DEC[:, i % 2, :], RA[:, i % 2]
                        for o, p_, d_ in ((ra[:, 0, 0, :], ps(2, T), dec[:, 0:T]),
                                          (ra[:, 0, 1, P:T], ps(2, P, c0=3 * P), dec[:, 0:P]),
                                          (ra[:, 1, 1, :], ps(2, T, c0=T), dec[:, T:2 * T]),
                                          (ra[:, 1, 0, 0:P], ps(2, P), dec[:, 3 * P:4 * P])):
                            j = dve.scalar_tensor_tensor(out=o, in0=p_, scalar=RSCALE, in1=d_, op0=ALU.mult, op1=ALU.mult)
                        j.then_inc(sem("ret_weighted"), 1)
                        dve.wait_ge(sem("exp_done"), n + 1)
                        link(dve.tensor_tensor(st[:, 4:6], st[:, 4:6], st[:, 6:8], ALU.add))
                        normalise(i, (T, T))
                    if 3 <= i < 11 and i % 2 == 1:
                        p = (i - 3) // 2
                        dve.wait_ge(sem("values_done"), HEADS * (l + 1) + 2 * p + 2)
                        dve.tensor_copy(Z[:, (QA + p) * T:(QA + p + 1) * T], ps(7, T, c0=(p % 2) * T))\
                            .then_inc(sem("pair_copied"), 1)
                dve.wait_ge(sem("ret_copied"), 4 * (l + 1))
                x_in()
                sums()
                for b in range(4):
                    o = H[:, 2 * b:2 * b + 2, :]
                    i = dve.scalar_tensor_tensor(out=o, in0=ps2(4 + b), scalar=-1.0 / HD, in1=o, op0=ALU.mult, op1=ALU.add)
                link(i)
                dve.tensor_tensor(SQV, H[:, :, :], H[:, :, :], ALU.mult).then_inc(sem("norm_in"), 1)

                def gated(lin, g0, js):
                    for j in js:
                        b = linear_ready(lin, j // 2, j % 2)
                        o = z(g0 + 2 * j, g0 + 2 * j + 2)
                        dve.tensor_tensor(o, ps2(b), o, ALU.mult).then_inc(sem("evac_dve"), 1)

                lin = lins[f"wo_attn{l}"]
                gated(lin, G2A, (0, 1))
                sums()
                reciprocal_root([(SQV[:, 2 * b:2 * b + 2, :], ps2(4 + b)) for b in range(4)], HD, KT * T)
                gated(lin, G2A, (2, 3))
                link(dve.tensor_tensor(H[:, :, :], H[:, :, :], SQV, ALU.mult))
                link(dve.tensor_tensor(H[:, :, :], H[:, :, :], z(GF, GF + 8), ALU.mult))
                dve.tensor_tensor(z(QR, QR + 4), H[:, 0:4, :], H[:, 4:8, :], ALU.add).then_inc(sem("ret_out"), 1)
                lin = lins[f"wo_ret{l}"]
                gated(lin, G2R, range(4))
                dve.wait_ge(sem("evac_dve"), job_evac[lin.job0 + 3][1])
                dve.tensor_tensor(z(G2A, G2A + 8), z(G2A, G2A + 8), z(G2R, G2R + 8), ALU.add).then_inc(sem("mix_ready"), 1)
                residual(lins[f"w_out{l}"], 0)
                x_in()
                layer_norm(X[:, :, :], vcols(V_LN1G, l), vcols(V_LN1B, l), "x2_ready")

            mixer2(0)
            for s in range(11):
                b = linear_ready(lins["ffn3"], s)
                o = z(2 * s, 2 * s + 2)
                dve.tensor_tensor(o, ps2(b), o, ALU.mult).then_inc(sem("evac_dve"), 1)
            dve.wait_ge(sem("lin_done"), lins["ffn2"].group0 + 11)
            for b in (2, 3, 0, 1):
                o = X[:, 2 * b:2 * b + 2, :]
                i = dve.scalar_tensor_tensor(out=o, in0=o, scalar=ALPHA, in1=ps2(b), op0=ALU.mult, op1=ALU.add)
                if b in (0, 1):
                    i.then_inc(sem("evac_dve"), 1)
            dve.wait_ge(sem("evac_dve"), job_evac[lins["ffn2"].job0 + 1][1])
            x_in()
            layer_norm(X[:, :, :], vcols(V_LN2G, 0), vcols(V_LN2B, 0), "x2_ready")
            mixer2(1)
            experts(m2, R_BR2)
            link(dve.scalar_tensor_tensor(out=X[:, :, :], in0=X[:, :, :], scalar=ALPHA, in1=Y, op0=ALU.mult, op1=ALU.add))
            x_in()
            layer_norm(X[:, :, :], vcols(V_LN2G, 1), vcols(V_LN2B, 1), "x2_ready")


INPUTS = ["x", "c", "w_ada", "b_ada", "norm1_g", "w_in", "b_forget", "conv_w", "conv_b", "conv_ln_g", "conv_ln_b",
          "w_conv_out", "w_attn_out", "w_out", "norm2_g", "w_router", "b_router", "w_exp_in", "b_exp_in", "w_exp_out",
          "b_exp_out", "final_g", "ln_emb_g_2", "ln_emb_b_2", "w_in_2", "b_gate_2", "sink_logits_2", "decay_fwd_2",
          "decay_bwd_2", "w_o_attn_2", "w_o_ret_2", "w_out_2", "ln1_g_2", "ln1_b_2", "ffn_w1_2", "ffn_w3_2",
          "ffn_w2_2", "router_w_2", "router_b_2", "moe_w1_2", "moe_w3_2", "moe_w2_2", "ln2_g_2", "ln2_b_2"]


def kernel(**inputs):
    import numpy as _np
    import concourse.bacc as _bacc
    from concourse import mybir as _mybir
    from concourse.bass_utils import run_bass_kernel_spmd as _run

    nc = _bacc.Bacc("TRN2", target_bir_lowering=False, num_devices=1)
    arrays, aps = {}, {}
    for name in INPUTS:
        a = _np.ascontiguousarray(inputs[name])
        arrays[f"in_{name}"] = a
        aps[name] = nc.dram_tensor(f"in_{name}", a.shape, _mybir.dt.from_np(a.dtype), kind="ExternalInput").ap()
    out = nc.dram_tensor("out_0", (1, T, D), _mybir.dt.float32, kind="ExternalOutput").ap()
    build_two_blocks(nc, aps, out)
    r = _run(nc, [arrays], core_ids=[0])
    return r.results[0]["out_0"]
```

```python
from contextlib import ExitStack

import numpy as np
import concourse.bass as bass
from concourse import mybir

F32 = mybir.dt.float32
F32R = mybir.dt.float32r
I32 = mybir.dt.int32
ALU = mybir.AluOpType
ACT = mybir.ActivationFunctionType
AX = mybir.AxisListType.X

P = 128
T = 256
D = 1024
KT = D // P
CW = 512
TAPS = 31
HEADS = 8
HD = 64
CHUNK = 128
HALF = 64
EPS = 1e-5
NEG = -1e30
FAR = 1e34
ALPHA = (2 * 2) ** 0.25
RK = 32
RSCALE = RK ** -0.5
QSCALE = HD ** -0.5
NG = 12
RAW_N, SPLIT_N = 6, 4
RING = 15
SLOT = 2048
SLOPES = [2.0 ** -(h + 1) for h in range(HEADS)]

V_C, V_BADA, V_N1G, V_N2G, V_FG, V_CB, V_CLG, V_CLB, V_EG, V_EB = 0, 8, 56, 64, 72, 80, 84, 88, 92, 100
V_LN1G, V_LN1B, V_LN2G, V_LN2B, V_BG = 128, 144, 160, 176, 192
V_CONVW, V_B1 = 256, 384
R_SINK, R_DECAY, R_BR1, R_BR2, R_N = 0, 16, 48, 80, 88


class Linear:

    def __init__(self, name, slots, jobs_per_slot, evac, k_major=0):
        self.name, self.slots, self.per, self.evac, self.k_major = name, slots, jobs_per_slot, evac, k_major
        self.is_ada = name.startswith("ada")


def plan():
    order = [Linear("ada0", 8, 1, "dve", 1), Linear("uqkv_a", 4, 1, "act"),
             Linear("ada1", 8, 1, "dve", 1), Linear("uqkv_b", 6, 1, "act"), Linear("forget", 0, 1, "act"),
             Linear("ada2", 8, 1, "dve", 1), Linear("gates", 8, 1, "act"),
             Linear("conv_out", 2, 2, "dve"), Linear("attn_out", 2, 2, "dve"),
             Linear("w_out", 4, 1, "dve")]
    for l in range(2):
        order += [Linear(f"qa{l}", 2, 1, "act"), Linear(f"kva{l}", 1, 2, "act"),
                  Linear(f"ret{l}", 4, 1, "act"), Linear(f"gg{l}", 12, 1, "act"),
                  Linear(f"wo_attn{l}", 2, 2, "dve"), Linear(f"wo_ret{l}", 2, 2, "dve"),
                  Linear(f"w_out{l}", 4, 1, "dve")]
        if l == 0:
            order += [Linear("ffn1", 11, 1, "act"), Linear("ffn3", 11, 1, "dve"),
                      Linear("ffn2", 11, 1, "dve", 2)]
    group = job = 0
    evacs = {"act": 0, "dve": 0}
    lins, job_evac = {}, []
    for lin in order:
        jobs = lin.k_major or max(1, lin.slots) * lin.per
        groups = 1 if lin.is_ada else lin.slots if lin.k_major else max(1, lin.slots) * lin.per
        lin.group0, lin.job0, lin.jobs, lin.groups, lin.at = group, job, jobs, groups, []
        group, job = group + groups, job + jobs
        for _ in range(jobs):
            evacs[lin.evac] += 1
            job_evac.append((lin.evac, evacs[lin.evac]))
        lins[lin.name] = lin
    stream = [("ada0", s) for s in range(8)]
    for name, n, ada in (("uqkv_a", 4, "ada1"), ("uqkv_b", 6, "ada2")):
        for s in range(n):
            stream.append((name, s))
            stream += [(ada, k) for k in range(min(2 * s, 8), min(2 * s + 2, 8))]
    done = {name for name, _ in stream}
    for lin in order:
        if lin.name == "qa0":
            n_block1 = len(stream)
        if lin.name not in done:
            stream += [(lin.name, s) for s in range(lin.slots)]
    free_at = []
    for n, (name, s) in enumerate(stream):
        lin = lins[name]
        assert len(lin.at) == s
        lin.at.append(n)
        if lin.is_ada:
            free_at.append(("ada_used", 8 * int(name[-1]) + s + 1))
        else:
            free_at.append(("lin_done", lin.group0 + (s + 1) * (1 if lin.k_major else lin.per)))
    return lins, job_evac, stream, free_at, n_block1


class Chain:

    def __init__(self, eng, sem):
        self.eng, self.sem, self.base, self.n = eng, sem, 0, 0

    def link(self, ins):
        self.n += 1
        ins.then_inc(self.sem, 1)
        self.eng.wait_ge(self.sem, self.base + self.n)

    def enter(self, base):
        self.base, self.n = base, 0


def build_two_blocks(nc, A, out):
    lins, job_evac, stream, free_at, N_A = plan()
    N_SLOTS = len(stream)
    ctx = ExitStack()
    with ctx:
        sems = {}

        def sem(name):
            if name not in sems:
                sems[name] = ctx.enter_context(nc.semaphore(name))
            return sems[name]

        def sb(name, shape, dt=F32):
            return ctx.enter_context(nc.sbuf_tensor(name, shape, dt))

        with nc.sbuf_tensor("W", [P, 24 * 1408], F32) as W:
            pass
        RAW = sb("RAW", [P, RAW_N, SLOT])
        WHI = sb("WHI", [P, SPLIT_N, SLOT], F32R)
        WLO = sb("WLO", [P, SPLIT_N, SLOT], F32R)
        X2 = sb("X2", [P, KT, 2 * HALF], F32R)
        HM2 = sb("HM2", [P, KT, 2 * HALF], F32R)
        sb("W_REST", [P, 24 * 1408 - (RAW_N + 2 * SPLIT_N) * SLOT - 4 * KT * HALF])
        Z = sb("Z", [P, 38 * T])
        X = sb("X", [P, KT, T])
        H = sb("H", [P, KT, T])
        SQ = sb("SQ", [P, KT * T])
        VEC = sb("VEC", [P, 7 * P])
        IDENT = sb("IDENT", [P, P])
        ONES = sb("ONES", [P, P])
        BLK = sb("BLK", [P, P])
        BEFORE = sb("BEFORE", [P, P])
        DIST = sb("DIST", [P, 2, T])
        LAGS = sb("LAGS", [P, 4, P])
        MOD = sb("MOD", [P, 48])
        ROWS = sb("ROWS", [1, R_N])
        ROWB = sb("ROWB", [P, R_N])
        WR1 = sb("WR1", [P, KT, 32])
        WR2 = sb("WR2", [P, KT, 8])
        LG = sb("LG", [P, 32])
        GS = sb("GS", [P, 3 * KT])
        CSIL = sb("CSIL", [P, KT])
        BFG = sb("BFG", [8, 1])
        IOTAP = sb("IOTAP", [P, 1])
        ST = sb("ST", [P, 2, 8])
        PS = ctx.enter_context(nc.psum_tensor("PS", [P, 8, 512], F32))

        SCR = W[:, RING * SLOT:RING * SLOT + 3072]

        def z(a, b):
            return Z[:, a * T:b * T].rearrange("p (k t) -> p k t", t=T)

        def slot(n):
            r = (n if n < N_A else n - N_A) % RING
            return W[:, r * SLOT:(r + 1) * SLOT], r

        XT = H[:, :, :].rearrange("p k t -> p (k t)").rearrange("p (a d) -> p a d", a=2)
        VROWS = SQ[:, 0:7 * P].rearrange("p (a c) -> p a c", c=P)
        CONV_IN = SCR[:, 0:4 * 286].rearrange("p (j t) -> p j t", t=286)
        SEL = SCR[:, 1144:2168].rearrange("p (h m) -> p h m", m=P)
        CAUSAL = SCR[:, 2168:2296]
        NEGF = SCR[:, 2296:2552]
        WF = SCR[:, 2552:2616].rearrange("p (k n) -> p k n", n=8)
        PROB = SQ[:, 0:1024].rearrange("p (b a k) -> p b a k", b=2, a=2)
        PROBT = SQ[:, 1024:2048].rearrange("p (b k) -> p b k", b=2)
        DEC = SCR[:, 0:1024].rearrange("p (b f) -> p b f", b=2)
        RA = SCR[:, 1024:3072].rearrange("p (b d s t) -> p b d s t", b=2, d=2, s=2)
        UV, UG, Q1, K1, GC, GA = 0, 4, 8, 12, 20, 28
        VT1 = Z[:, 16 * T:20 * T].rearrange("p (a n) -> p a n", a=2)
        ADA = Z[:, GA * T:(GA + 8) * T]
        QA, KA, QR, KR, GF, GB, G2A, G2R = 0, 4, 5, 7, 14, 18, 22, 30
        VR = Z[:, 9 * T:13 * T].rearrange("p (a n) -> p a n", a=2)
        VA = Z[:, 13 * T:14 * T].rearrange("p (a n) -> p a n", a=2)

        at = [0]

        def zs(n):
            at[0] += n
            return Z[:, at[0] - n:at[0]]

        HT = zs(2048).rearrange("p (a d) -> p a d", a=2)
        Y = zs(2048).rearrange("p (k t) -> p k t", t=T)
        XG = zs(1024).rearrange("p (k c) -> p k c", c=CHUNK)
        HM = zs(11 * CHUNK).rearrange("p (k c) -> p k c", c=CHUNK)
        PART = zs(2048)
        GT = zs(T)
        PICK = zs(2 * CHUNK).rearrange("p (a c) -> p a c", c=CHUNK)
        PICKG = zs(2 * CHUNK).rearrange("p (a c) -> p a c", c=CHUNK)
        IOTA = zs(T)
        HS = PART
        GPART, UPART = XG[:, 0:4, :].rearrange("p k (a c) -> p (k a) c", a=2), XG[:, 4:8, :].rearrange("p k (a c) -> p (k a) c", a=2)
        SIG = HM[:, 0:4, :].rearrange("p k (a c) -> p (k a) c", a=2)
        STACK = HM[:, 4, 0:HALF]
        YS = SQ[:, 0:1024]
        TAB = SQ[0:1, 1024:1024 + 2 * P + 34].bitcast(I32)
        at = [1024 + 2 * P + 34]

        def qs(n):
            at[0] += n
            return SQ[:, at[0] - n:at[0]]

        B1C = qs(16)
        LOG = qs(80).rearrange("p (a e) -> p a e", e=40)
        LOGR = qs(80).rearrange("p (a e) -> p a e", e=40)
        MASK = qs(64).rearrange("p (a e) -> p a e", e=32)
        GATE = qs(64).rearrange("p (a e) -> p a e", e=32)
        RANK = qs(64).rearrange("p (a e) -> p a e", e=32)
        TOP8 = qs(16).rearrange("p (a e) -> p a e", e=8)
        NTOP, GSUM = qs(2), qs(2)
        NCH, CUM, START, LE, LEN_, ONE32 = qs(32), qs(32), qs(32), qs(32), qs(32), qs(32)
        TCOL, FREE = qs(2), qs(1)
        BOUT = SCR[0:32, 0:1024]

        def bc(ap, n):
            return ap.unsqueeze(1).broadcast_to([P, n, ap.shape[1]])

        def bl(ap, n):
            return ap.unsqueeze(2).broadcast_to([P, ap.shape[1], n])

        def ps(b, n=512, p0=0, p1=P, c0=0):
            return PS[p0:p1, b, c0:c0 + n]

        def ps2(b):
            return PS[:, b, :].rearrange("p (a t) -> p a t", a=2)

        w_in, w_in2 = A["w_in"], A["w_in_2"]

        def cols(w, c0, n, buf, k=KT):
            return [(buf[:, 0:k * n].rearrange("p (k n) -> p k n", k=k),
                     w[:, c0:c0 + n].rearrange("(k p) n -> p k n", p=P))]

        def rows(w, k0, nk, c0, n, buf):
            return [(buf[:, 0:nk * n].rearrange("p (k n) -> p k n", k=nk),
                     w[k0 * P:(k0 + nk) * P, c0:c0 + n].rearrange("(k p) n -> p k n", p=P))]

        def transfers(name, s, buf):
            l = int(name[-1]) if name[-1].isdigit() else 0
            if name.startswith("ada"):
                return rows(A["w_ada"][0], s, 1, 2048 * l, 2048, buf)
            if name.startswith("uqkv"):
                return cols(w_in[0], 256 * (s + (4 if name == "uqkv_b" else 0)), 256, buf)
            if name == "gates":
                return cols(w_in[0], 5 * CW + HEADS + 256 * s, 256, buf)
            if name in ("conv_out", "attn_out"):
                return cols(A["w_" + name][0], 512 * s, 512, buf, 4)
            if name == "w_out":
                return cols(A["w_out"][0], 256 * s, 256, buf)
            if name.startswith("qa"):
                src = w_in2[l][:, 0:512].rearrange("(k p) (g c) -> p k g c", p=P, g=2)
                dst = buf.rearrange("p (k g c) -> p k g c", k=KT, g=4)
                return [(dst[:, :, 2 * i + g, :], src[:, :, g, (2 * s + i) * HD:(2 * s + i + 1) * HD])
                        for i in range(2) for g in range(2)]
            if name.startswith("kva"):
                return cols(w_in2[l], 512, 256, buf)
            if name.startswith("ret"):
                return cols(w_in2[l], 768 + 256 * s, 256, buf)
            if name.startswith("gg"):
                return cols(w_in2[l], 1792 + 256 * s, 256, buf)
            if name.startswith("wo_attn"):
                src = A["w_o_attn_2"][l][:, 512 * s:512 * (s + 1)].rearrange("(g i r) n -> g r i n", g=2, i=4)
                return [(buf[64 * g:64 * (g + 1), :].rearrange("p (k n) -> p k n", k=4), src[g]) for g in range(2)]
            if name.startswith("wo_ret"):
                return cols(A["w_o_ret_2"][l], 512 * s, 512, buf, 4)
            if name.startswith("w_out"):
                return cols(A["w_out_2"][l], 256 * s, 256, buf)
            if name == "ffn1":
                return cols(A["ffn_w1_2"][0], 256 * s, 256, buf)
            if name == "ffn3":
                return cols(A["ffn_w3_2"][0], 256 * s, 256, buf)
            return rows(A["ffn_w2_2"][0], 2 * s, 2, 0, 1024, buf)

        arrive, total = [], [0] * RING
        for n, (name, s) in enumerate(stream):
            buf, r = slot(n)
            total[r] += 16 * len(transfers(name, s, buf))
            arrive.append((r, total[r]))
        moe2_base = list(total)

        class Moe:
            pass

        m1, m2 = Moe(), Moe()
        m1.tag, m1.n, m1.top, m1.ht, m1.slots, m1.free = "m1", 32, 4, 8, HALF, 1
        m2.tag, m2.n, m2.top, m2.ht, m2.slots, m2.free = "m2", 8, 2, 11, CHUNK, 0

        def msem(m, name):
            return sem(f"{m.tag}_{name}")

        def group_kts(m, s):
            if s < 8:
                return [s] if m is m1 else [2 * (s % 4), 2 * (s % 4) + 1]
            k = 2 if m is m1 else 3
            return list(range(k * (s - 8), min(k * (s - 7), m.ht)))

        def lo_engine(s):
            return "pool" if s % 3 == 2 else "dve"

        def los(s):
            return sum(lo_engine(i) == lo_engine(s) for i in range(s + 1))

        LO_DVE, LO_POOL = 8, 4

        def wait_split(eng, g, s):
            n = LO_DVE if lo_engine(s) == "dve" else LO_POOL
            eng.wait_ge(sem("m1_lo_" + lo_engine(s)), g * n + los(s))

        def split_lo(eng, g, s, first=False):
            eng.wait_ge(sem("m1_hi"), g * NG + (s + 1))
            if not first:
                eng.wait_ge(sem("m1_group_done"), g * NG + (s + 1 - SPLIT_N))
            eng.tensor_tensor(WLO[:, s % SPLIT_N, :], RAW[:, s % RAW_N, :], WHI[:, s % SPLIT_N, :].bitcast(F32), ALU.subtract)\
                .then_inc(sem("m1_lo_" + lo_engine(s)), 1)

        def group_at(m, s):
            return s * 2816 if s < 8 else 8 * 2816 + (s - 8) * 3072

        def group_src(m, s, e):
            if m is m1:
                if s < 8:
                    w, k0, nk, n = A["w_exp_in"], s, 1, 2048
                else:
                    w, k0, nk, n = A["w_exp_out"], 2 * (s - 8), 2, 1024
            else:
                ks = group_kts(m, s)
                w = A["moe_w1_2"] if s < 4 else A["moe_w3_2"] if s < 8 else A["moe_w2_2"]
                k0, nk, n = ks[0], len(ks), 1408 if s < 8 else 1024
            src = w[0, bass.ds(e, 1), k0 * P:(k0 + nk) * P, :].rearrange("a (k p) n -> p (a k) n", p=P)
            if m is m1:
                dst = RAW[:, s % RAW_N, :]
            else:
                dst = W[:, group_at(m, s):group_at(m, s) + nk * n]
            return dst.rearrange("p (k n) -> p k n", k=nk), src

        block = ctx.enter_context(nc.Block())

        @block.sync
        def _(sp):
            def wait_free(n):
                name, count = free_at[n]
                sp.wait_ge(sem(name), count)

            def dense(n0, n1):
                for n in range(n0, n1):
                    name, s = stream[n]
                    buf, r = slot(n)
                    if n == 2:
                        sp.wait_ge(sem("ld_vec"), 16 * 17)
                    if n - n0 >= RING:
                        wait_free(n - RING)
                    for dst, src in transfers(name, s, buf):
                        sp.dma_start(dst, src).then_inc(sem(f"arrived{r}"), 16)

            def experts1():
                def group(g, s, e):
                    dst, src = group_src(m1, s, e)
                    sp.dma_start(dst, src).then_inc(sem(f"m1_raw{s % RAW_N}"), 16)

                for s in range(NG):
                    if s < RAW_N:
                        wait_free(max(k for k in range(N_A) if k % RING == s))
                    else:
                        wait_split(sp, 0, s - RAW_N)
                    group(0, s, 0)
                sp.wait_ge(msem(m1, "tables"), 1)
                last = sp.value_load(TAB[0:1, 2 * P + 33:2 * P + 34], min_val=0, max_val=47)
                with sp.Fori(0, last) as before:
                    e = sp.value_load(TAB[0:1, bass.ds(before + 1, 1)], min_val=0, max_val=m1.n - 1)
                    for s in range(NG):
                        wait_split(sp, before + (s >= RAW_N), (s - RAW_N) % NG)
                        group(before + 1, s, e)
                for s in range(SPLIT_N):
                    wait_split(sp, last, s + RAW_N)
                    group(last + 1, s, m1.n - 1)
                sp.wait_ge(sem("m1_bytes_free"), 1)

            def experts(m, n0, n1):
                for s in range(NG):
                    lo, hi = group_at(m, s), group_at(m, s) + int(np.prod(group_src(m, s, 0)[0].shape[1:]))
                    over = [k for k in range(max(n0, n1 - RING), n1)
                            if slot(k)[1] * SLOT < hi and (slot(k)[1] + 1) * SLOT > lo]
                    if hi > RING * SLOT:
                        over = [n1 - 1]
                    if over:
                        wait_free(max(over))
                    dst, src = group_src(m, s, 0)
                    sp.dma_start(dst, src).then_inc(sem(f"arrived{s}"), 16)
                sp.wait_ge(msem(m, "tables"), 1)
                with sp.Fori(1, m.n) as e:
                    before = sp.value_load(TAB[0:1, bass.ds(e + 2 * P, 1)], min_val=0, max_val=47)
                    for s in range(NG):
                        sp.wait_ge(msem(m, "group_done"), before * NG + (s + 1))
                        dst, src = group_src(m, s, e)
                        sp.dma_start(dst, src).then_inc(sem(f"arrived{s}"), 16)

            dense(0, N_A)
            experts1()
            dense(N_A, N_SLOTS)
            experts(m2, N_A, N_SLOTS)
            sp.wait_ge(sem("out_staged"), 4)
            sp.dma_start(out[0].rearrange("(a p) d -> p a d", p=P), XT).then_inc(sem("stored"), 16)
            sp.wait_ge(sem("stored"), 16)

        @block.gpsimd
        def _(pool):
            ch = Chain(pool, sem("pool_step"))
            ch.link(pool.memset(IDENT[:, :], 0.0))
            ch.link(pool.affine_select(out=IDENT[:, :], in_=IDENT[:, :], compare_op=ALU.not_equal, fill=1.0,
                                       base=0, pattern=[[-1, P]], channel_multiplier=1))
            pool.memset(ONES[:, :], 1.0).then_inc(sem("ident_ready"), 1)
            ch.link(pool.memset(BLK[:, :], 0.0))
            ch.link(pool.memset(BLK[0:64, 0:64], 1.0))
            ch.link(pool.memset(BLK[64:128, 64:128], 1.0))
            ch.link(pool.memset(BEFORE[:, :], 1.0))
            ch.link(pool.affine_select(out=BEFORE[:, :], in_=BEFORE[:, :], compare_op=ALU.is_gt, fill=0.0,
                                       base=0, pattern=[[1, P]], channel_multiplier=-1))
            ch.link(pool.memset(SEL, 0.0))
            ch.link(pool.affine_select(out=SEL, in_=SEL, compare_op=ALU.not_equal, fill=1.0,
                                       base=0, pattern=[[-1, HEADS], [0, P]], channel_multiplier=1))
            ch.link(pool.memset(CAUSAL, 0.0))
            ch.link(pool.affine_select(out=CAUSAL, in_=CAUSAL, compare_op=ALU.is_ge, fill=NEG,
                                       base=0, pattern=[[-1, P]], channel_multiplier=1))
            ch.link(pool.memset(NEGF, 0.0))
            ch.link(pool.memset(CONV_IN[:, :, 0:TAPS - 1], 0.0))
            ch.link(pool.iota(IOTAP[:, :], pattern=[[0, 1]], base=0, channel_multiplier=1,
                              allow_small_or_imprecise_dtypes=True))
            for i, (base, step) in enumerate(((0, 1), (P, 1), (P, -1), (0, -1))):
                ch.link(pool.iota(LAGS[:, i, :], pattern=[[step, P]], base=base, channel_multiplier=-step,
                                  allow_small_or_imprecise_dtypes=True))
            ch.link(pool.iota(DIST[:, :, :], pattern=[[P, 2], [-1, T]], base=0, channel_multiplier=1,
                              allow_small_or_imprecise_dtypes=True))
            pool.wait_ge(sem("dist_abs"), 1)
            ch.link(pool.affine_select(out=DIST[:, :, :], in_=DIST[:, :, :], compare_op=ALU.is_ge, fill=FAR,
                                       base=P, pattern=[[-P, 2], [1, T]], channel_multiplier=-1))
            pool.affine_select(out=DIST[:, :, :], in_=DIST[:, :, :], compare_op=ALU.is_ge, fill=FAR,
                               base=P, pattern=[[P, 2], [-1, T]], channel_multiplier=1)\
                .then_inc(sem("dist_ready"), 1)

            def decay_masks(l):
                for h in range(HEADS):
                    n = l * HEADS + h
                    pool.wait_ge(sem("decay_exp"), n + 1)
                    dec = DEC[:, h % 2, :]
                    ch.link(pool.affine_select(out=dec[:, 0:P], in_=dec[:, 0:P], compare_op=ALU.is_ge, fill=0.0,
                                               base=0, pattern=[[1, P]], channel_multiplier=-1))
                    pool.affine_select(out=dec[:, 3 * P:], in_=dec[:, 3 * P:], compare_op=ALU.is_gt, fill=0.0,
                                       base=0, pattern=[[-1, P]], channel_multiplier=1)\
                        .then_inc(sem("decay_masked"), 1)

            def slot_iota(m):
                pool.wait_ge(sem("moe_scratch_free"), 1 if m is m1 else 2)
                pool.iota(IOTA, pattern=[[1, T]], base=0, channel_multiplier=0,
                          allow_small_or_imprecise_dtypes=True).then_inc(msem(m, "iota"), 1)

            slot_iota(m1)
            split_lo(pool, 0, 2, first=True)
            pool.wait_ge(msem(m1, "tables"), 1)
            count = pool.value_load(TAB[0:1, 2 * P + 32:2 * P + 33], min_val=m1.n, max_val=48)
            with pool.Fori(0, count) as g:
                for s in (5, 8, 11):
                    split_lo(pool, g, s)
                split_lo(pool, g + 1, 2)
            decay_masks(0)
            decay_masks(1)
            slot_iota(m2)

        @block.tensor
        def _(pe):
            norm = [0]

            def bank_free(job):
                if job >= 2:
                    e, c = job_evac[job - 2]
                    pe.wait_ge(sem("evac_" + e), c)
                else:
                    pe.wait_ge(sem("init_act"), 1)

            def weights(n):
                r, c = arrive[n]
                pe.wait_ge(sem(f"arrived{r}"), c)
                return slot(n)[0]

            def feature_job(lin, s, x, nk=KT, cols_=256, part=0, width=256):
                job = lin.job0 + s * lin.per + part
                w = weights(lin.at[s]).rearrange("p (k n) -> p k n", k=nk)
                bank_free(job)
                for j in range(width // P):
                    for k in range(nk):
                        c = part * width + j * P
                        mm = pe.matmul(ps(job % 2, T, c0=j * T), w[:, k, c:c + P], x[:, k, :],
                                       start=(k == 0), stop=(k == nk - 1))
                mm.then_inc(sem("lin_done"), 1)

            def token_job(lin, s, x, c0, width, part=0):
                job = lin.job0 + s * lin.per + part
                w = weights(lin.at[s]).rearrange("p (k n) -> p k n", k=KT)
                bank_free(job)
                for a in range(2):
                    for k in range(KT):
                        mm = pe.matmul(ps(job % 2, width, c0=a * width), x[:, k, a * P:(a + 1) * P],
                                       w[:, k, c0:c0 + width], start=(k == 0), stop=(k == KT - 1))
                mm.then_inc(sem("lin_done"), 1)

            def ada(l):
                lin = lins[f"ada{l}"]
                pe.wait_ge(sem("ada_used"), 8 * (l + 1))
                bank_free(lin.job0)
                for j in range(16):
                    mm = pe.matmul(PS[:, lin.job0 % 2, j:j + 1], ADA[:, j * P:(j + 1) * P], ONES[:, 0:1], start=True, stop=True)
                mm.then_inc(sem("lin_done"), 1)

            def norm_sum(src, nk, col=0):
                norm[0] += 1
                pe.wait_ge(sem("norm_in"), norm[0])
                for k in range(nk):
                    mm = pe.matmul(ps(4, T, c0=col), ONES[:, :], src[:, k, :], start=(k == 0), stop=(k == nk - 1))
                mm.then_inc(sem("norm_sum"), 1)

            SQV = SQ[:, :].rearrange("p (k t) -> p k t", t=T)

            def rms():
                norm_sum(SQV, KT)

            def layer_norm(src, nk=KT):
                norm_sum(src, nk)
                norm_sum(SQV, nk, T)

            pe.wait_ge(sem("ident_ready"), 1)
            pe.wait_ge(sem("ld_vec"), 16 * 17)
            for i, r in enumerate([108, 96, 124] + [P] * 4):
                tr = pe.transpose(PS[:, i // 4, (i % 4) * P:(i % 4) * P + r], VROWS[0:r, i, :], IDENT[0:r, 0:r])
            tr.then_inc(sem("vec_turned"), 1)
            pe.wait_ge(sem("ld_rows"), 16 * 5)
            pe.matmul(ps(3, R_N), ONES[0:1, :], ROWS[0:1, :], start=True, stop=True).then_inc(sem("rows_spread"), 1)
            pe.wait_ge(sem("ld_x"), 16)
            for k in range(KT):
                for a in range(2):
                    tr = pe.transpose(PS[:, 4 + k // 2, (k % 2) * T + a * P:(k % 2) * T + (a + 1) * P],
                                      XT[:, a, k * P:(k + 1) * P], IDENT[:, :])
            tr.then_inc(sem("x_turned"), 1)

            ada(0)
            pe.wait_ge(sem("x_ready"), 1)
            rms()
            pe.wait_ge(sem("h_ready"), 1)
            for s in range(4):
                feature_job(lins["uqkv_a"], s, H)
            ada(1)
            for s in range(4):
                feature_job(lins["uqkv_b"], s, H)
            for s in range(4, 6):
                token_job(lins["uqkv_b"], s, H, 0, 256)
            job = lins["forget"].job0
            pe.wait_ge(sem("ld_small"), 16 * 4)
            bank_free(job)
            for k in range(KT):
                mm = pe.matmul(PS[0:8, job % 2, 0:T], WF[:, k, :], H[:, k, :], start=(k == 0), stop=(k == KT - 1))
            mm.then_inc(sem("lin_done"), 1)
            ada(2)

            def scores1(h):
                r = (h % 2) * HD
                q, k = Z[r:r + HD, (Q1 + h // 2) * T:(Q1 + h // 2 + 1) * T], Z[r:r + HD, (K1 + h // 2) * T:(K1 + h // 2 + 1) * T]
                b = 4 + h % 2
                if h >= 2:
                    pe.wait_ge(sem("exp_done"), h - 1)
                else:
                    pe.wait_ge(sem("negf_ready"), 1)
                pe.matmul(ps(b, P), q[:, 0:P], k[:, 0:P], start=True, stop=False)
                pe.matmul(ps(b, P), SEL[:, h, :], NEGF[:, 0:P], start=False, stop=False)
                pe.matmul(ps(b, P), IDENT[:, :], CAUSAL, start=False, stop=True)
                pe.matmul(ps(b, T, c0=P), q[:, P:T], k[:, :], start=True, stop=False)
                pe.matmul(ps(b, T, c0=P), SEL[:, h, :], NEGF, start=False, stop=True)
                pe.matmul(ps(b, P, c0=2 * P), IDENT[:, :], CAUSAL, start=False, stop=True,
                          skip_group_check=True).then_inc(sem("scores_ready"), 1)

            def turn_probs(n, h, blocks):
                pe.wait_ge(sem("probs_ready"), n + 1)
                if n >= 1:
                    pe.wait_ge(sem("probs_copied"), n)
                for i, (qa, ka) in enumerate(blocks):
                    tr = pe.transpose(ps(6, P, c0=i * P), PROB[:, n % 2, qa, ka * P:(ka + 1) * P], IDENT[:, :])
                tr.then_inc(sem("probs_turned"), 1)

            def values(n, half, pair, last_half, v, blocks):
                pe.wait_ge(sem("probs_copied"), n + 1)
                if half == 0 and pair >= 1:
                    pe.wait_ge(sem("pair_copied"), pair)
                for i, (ka, q0, wd, c) in enumerate(blocks):
                    mm = pe.matmul(ps(7, wd, HD * half, HD * half + HD, (pair % 2) * T + q0),
                                   v[:, ka, :], PROBT[:, n % 2, c:c + wd], start=(i == 0),
                                   stop=True, skip_group_check=True)
                mm.then_inc(sem("values_done"), 1)

            lin = lins["gates"]
            for i in range(10):
                if i < 8:
                    feature_job(lin, i, H)
                    if i == 0:
                        pe.wait_ge(sem("evac_act"), 10)
                    scores1(i)
                if 1 <= i < 9:
                    turn_probs(i - 1, i - 1, ((0, 0), (1, 0), (1, 1)))
                if i >= 2:
                    h = i - 2
                    values(h, h % 2, h // 2, h % 2, VT1[:, :, h * HD:(h + 1) * HD], ((0, 0, T, 0), (1, P, P, T)))
            layer_norm(z(UV, UV + 4), 4)
            pe.wait_ge(sem("conv_ready"), 1)
            for s in range(2):
                for part in range(2):
                    feature_job(lins["conv_out"], s, z(UV, UV + 4), 4, 512, part)
            pe.wait_ge(sem("pair_copied"), 4)
            for s in range(2):
                for part in range(2):
                    feature_job(lins["attn_out"], s, z(UG, UG + 4), 4, 512, part)
            pe.wait_ge(sem("mix_ready"), 1)
            for s in range(4):
                feature_job(lins["w_out"], s, z(GC, GC + 8))
            rms()
            pe.wait_ge(sem("h_ready"), 2)

            def experts(m, x, wr, hr_name, hr_n):
                E = m.n
                pe.wait_ge(sem("moe_scratch_free"), 1 if m is m1 else 2)
                for a in range(2):
                    for k in range(KT):
                        tr = pe.transpose(ps(4 + 2 * a + k // 4, P, c0=(k % 4) * P), x[:, k, a * P:(a + 1) * P], IDENT[:, :])
                tr.then_inc(msem(m, "x_turned"), 1)
                for a in range(2):
                    for k in range(KT):
                        mm = pe.matmul(ps(0, E, c0=a * E), x[:, k, a * P:(a + 1) * P], wr[:, k, :],
                                       start=(k == 0), stop=(k == KT - 1))
                mm.then_inc(msem(m, "logits"), 1)
                pe.wait_ge(msem(m, "mask"), 1)
                for a in range(2):
                    pe.matmul(ps(1, E), ONES[:, :], MASK[:, a, 0:E], start=(a == 0), stop=(a == 1))
                pe.matmul(ps(1, E, c0=64), BEFORE[:, :], MASK[:, 0, 0:E], start=True, stop=True)
                pe.matmul(ps(1, E, c0=96), ONES[:, :], MASK[:, 0, 0:E], start=True, stop=False)
                pe.matmul(ps(1, E, c0=96), BEFORE[:, :], MASK[:, 1, 0:E], start=False, stop=True)\
                    .then_inc(msem(m, "counts"), 1)
                pe.wait_ge(msem(m, "table_cols"), 1)
                for j in range(2):
                    mm = pe.matmul(ps(2, P, 0, 1, j * P), TCOL[:, j:j + 1], IDENT[:, :], start=True, stop=True)
                mm.then_inc(msem(m, "table_rows"), 1)
                pe.wait_ge(msem(m, "tables"), 1)
                count = pe.value_load(TAB[0:1, 2 * P + 32:2 * P + 33], min_val=m.n, max_val=48)

                def gather(g1, last=None):
                    pe.wait_ge(msem(m, "pick"), g1)
                    if m is m1 and last is not None:
                        pe.wait_ge(msem(m, "turned_copied"), last + 1)
                    for k in range(KT):
                        if m is m2 and last is not None and k % 4 == 0:
                            pe.wait_ge(msem(m, "added"), last * 4 + (3 + k // 4))
                        for a in range(2):
                            mm = pe.matmul(ps(6 + k // 4, CHUNK, c0=(k % 4) * CHUNK), HT[:, a, k * P:(k + 1) * P],
                                           PICK[:, a, :], start=(a == 0), stop=(a == 1))
                    mm.then_inc(msem(m, "gathered"), 1)

                def turn(g):
                    pe.wait_ge(msem(m, "pickg"), g + 1)
                    if m is m1:
                        pe.wait_ge(msem(m, "added"), g * 4 + m.free)
                    pe.nop(nofuse=True)
                    for a in range(2):
                        tr = pe.transpose(ps(6, P, c0=a * P), PICKG[:, a, :], IDENT[:, :])
                    tr.then_inc(msem(m, "turned"), 1)

                def scatter(g, qs_=range(4)):
                    pe.wait_ge(msem(m, "turned_copied"), g + 1)
                    pe.wait_ge(msem(m, "ys_dve"), g + 1)
                    pe.wait_ge(msem(m, "ys_act"), g + 1)
                    for q in qs_:
                        if q >= 2:
                            pe.wait_ge(msem(m, "added"), g * 4 + (q - 1 + m.free))
                        for j in range(2):
                            k = 2 * q + j
                            mm = pe.matmul(ps(6 + q % 2, T, c0=j * T), YS[:, k * P:(k + 1) * P], GT,
                                           start=True, stop=True)
                        mm.then_inc(msem(m, "scattered"), 1)

                def split_product(g, s):
                    wait_split(pe, g, s)
                    per = SLOT // 512 if s < 8 else 2
                    for i, k in enumerate(group_kts(m, s)):
                        x, b0 = (X2, 0) if s < 8 else (HM2, 4)
                        for part in (WHI, WLO):
                            for j in range(per):
                                c = (i * per + j) * 512
                                mm = pe.matmul(ps(b0 + j), x[:, k, :], part[:, s % SPLIT_N, c:c + 512],
                                               start=(k == 0 and part is WHI), stop=(k == KT - 1 and part is WLO),
                                               skip_group_check=True)
                    mm.then_inc(msem(m, "group_done"), 1)

                def turn_hidden(g):
                    pe.wait_ge(msem(m, "ys_dve"), g + 1)
                    pe.wait_ge(msem(m, "ys_act"), g + 1)
                    for half, copied in ((0, "hs_act"), (1, "hs_dve")):
                        pe.wait_ge(msem(m, copied), g + 1)
                        for j in range(KT):
                            f = (half * KT + j) * P
                            mm = pe.matmul(ps(4 + half, HALF, c0=j * HALF), HS[:, f:f + P], STACK, start=True, stop=True)
                        mm.then_inc(msem(m, "hidden_turned"), 1)

                def first_product(g, e, s):
                    pe.wait_ge(sem(f"arrived{s}"), e * 16 + (moe2_base[s] + 16))
                    for i, k in enumerate(group_kts(m, s)):
                        for j in range(m.ht):
                            w0 = group_at(m, s) + i * 1408 + j * P
                            mm = pe.matmul(ps(3 * (s // 4) + j // 4, CHUNK, c0=(j % 4) * CHUNK), W[:, w0:w0 + P],
                                           XG[:, k, :], start=(k == 0 and j % 4 == 0), stop=(k == KT - 1),
                                           skip_group_check=True)
                    mm.then_inc(msem(m, "group_done"), 1)

                def second_product(g, e, s):
                    pe.wait_ge(sem(f"arrived{s}"), e * 16 + (moe2_base[s] + 16))
                    for i, k in enumerate(group_kts(m, s)):
                        if k == 0:
                            pe.wait_ge(msem(m, "hm"), g * 3 + 3)
                        elif k == 8:
                            pe.wait_ge(msem(m, "hm"), g * 3 + 4)
                        for half in range(2):
                            w0 = group_at(m, s) + i * D + half * 512
                            mm = pe.matmul(ps(half), HM[:, k, :], W[:, w0:w0 + 512],
                                           start=(k == 0), stop=(k == m.ht - 1), skip_group_check=True)
                    mm.then_inc(msem(m, "group_done"), 1)

                if m is m1:
                    pe.wait_ge(msem(m, "gates"), 1)
                    for a in range(2):
                        tr = pe.transpose(ps(3, P, 0, 32, a * P), GATE[:, a, :], IDENT[:, :])
                    tr.then_inc(sem("gates_turned"), 1)
                    pe.wait_ge(sem("gates_copied"), 1)
                    pe.wait_ge(sem("ld_bout"), 16)
                    for k in range(KT):
                        mm = pe.matmul(ps(4 + k // 2, T, c0=(k % 2) * T), BOUT[:, k * P:(k + 1) * P], GT[0:32, :],
                                       start=True, stop=True)
                    mm.then_inc(sem("bias_sum"), 1)
                    pe.wait_ge(sem("bias_copied"), 1)
                pe.wait_ge(msem(m, "ht_act"), 1)
                pe.wait_ge(msem(m, "ht_dve"), 1)
                gather(1)
                if m is m1:
                    pe.wait_ge(sem("stack_ready"), 1)
                    with pe.Fori(0, count) as g:
                        pe.wait_ge(msem(m, "x_hi"), g + 1)
                        pe.wait_ge(msem(m, "x_lo"), g + 1)
                        for s in range(2):
                            split_product(g, s)
                        turn(g)
                        for s in range(2, 8):
                            split_product(g, s)
                        gather(g + 2, g)
                        turn_hidden(g)
                        pe.wait_ge(msem(m, "x_hi"), g + 2)
                        pe.wait_ge(msem(m, "x_lo"), g + 2)
                        scatter(g, (0, 1))
                        pe.wait_ge(msem(m, "hm"), g + 1)
                        for s in range(8, 10):
                            split_product(g, s)
                        scatter(g, (2, 3))
                        for s in range(10, NG):
                            split_product(g, s)
                    pe.wait_ge(msem(m, "x_hi"), count + 1)
                    pe.wait_ge(msem(m, "x_lo"), count + 1)
                else:
                    with pe.Fori(0, count) as g:
                        e = pe.value_load(TAB[0:1, bass.ds(g, 1)], min_val=0, max_val=m.n - 1)
                        pe.wait_ge(msem(m, "xg"), g + 1)
                        pe.wait_ge(msem(m, "ys_dve"), g + 1)
                        pe.wait_ge(msem(m, "ys_act"), g + 1)
                        for s in range(2):
                            first_product(g, e, s)
                        turn(g)
                        for s in range(2, 4):
                            first_product(g, e, s)
                        scatter(g)
                        for s in range(4, 8):
                            first_product(g, e, s)
                        gather(g + 2, g)
                        for s in range(8, NG):
                            second_product(g, e, s)
                    pe.wait_ge(msem(m, "xg"), count + 1)
                turn(count)
                scatter(count)

            experts(m1, H, WR1, "h_ready", 2)

            rms()
            layer_norm(X)

            def mixer2(l):
                pe.wait_ge(sem("x2_ready"), 2 * l + 1)
                for s in range(2):
                    feature_job(lins[f"qa{l}"], s, X)
                lin = lins[f"kva{l}"]
                feature_job(lin, 0, X, width=P)
                token_job(lin, 0, X, P, P, part=1)
                lin = lins[f"ret{l}"]
                for s in range(2):
                    feature_job(lin, s, X)
                for s in range(2, 4):
                    token_job(lin, s, X, 0, 256)

                def scores2(i):
                    g, q = i % 2, i // 2
                    n = HEADS * (l + 1) + i
                    r = g * HD
                    pe.wait_ge(sem("exp_done"), n - 1)
                    for a in range(2):
                        mm = pe.matmul(ps(4 + g, T, c0=a * T), Z[r:r + HD, (QA + q) * T + a * P:(QA + q) * T + (a + 1) * P],
                                       Z[r:r + HD, KA * T:(KA + 1) * T], start=True, stop=True)
                    mm.then_inc(sem("scores_ready"), 1)

                def ret_scores(h):
                    r = (h % 4) * RK
                    n = HEADS * l + h
                    if n:
                        pe.wait_ge(sem("ret_weighted"), n)
                    for a in range(2):
                        k0, q0 = (KR + h // 4) * T + a * P, (QR + h // 4) * T
                        mm = pe.matmul(ps(2, T, c0=a * T), Z[r:r + RK, k0:k0 + P], Z[r:r + RK, q0:q0 + T],
                                       start=True, stop=True, tile_position=(r, 0))
                    mm.then_inc(sem("ret_scores"), 1)

                def ret_values(h):
                    n = HEADS * l + h
                    r = (h % 2) * HD
                    pe.wait_ge(sem("ret_weighted"), n + 1)
                    if h % 2 == 0 and n:
                        pe.wait_ge(sem("ret_copied"), n // 2)
                    a = RA[:, h % 2]
                    v = VR[:, :, h * HD:(h + 1) * HD]
                    pe.matmul(ps(3, T, r, r + HD, 0), v[:, 0, :], a[:, 0, 0, :], start=True, stop=True, skip_group_check=True)
                    pe.matmul(ps(3, P, r, r + HD, P), v[:, 1, :], a[:, 0, 1, P:T], start=False, stop=True, skip_group_check=True)
                    pe.matmul(ps(3, T, r, r + HD, T), v[:, 1, :], a[:, 1, 1, :], start=True, stop=True, skip_group_check=True)
                    pe.matmul(ps(3, P, r, r + HD, T), v[:, 0, :], a[:, 1, 0, 0:P], start=False, stop=True,
                              skip_group_check=True).then_inc(sem("ret_values"), 1)

                lin = lins[f"gg{l}"]
                pe.wait_ge(sem("pair_copied"), 4 * (l + 1))
                for i in range(12):
                    feature_job(lin, i, X)
                    if i == 0:
                        e, c = job_evac[lin.job0 - 1]
                        pe.wait_ge(sem("evac_" + e), c)
                    if i < 8:
                        scores2(i)
                        ret_scores(i)
                    n = HEADS * (l + 1) + i
                    if 1 <= i < 9:
                        turn_probs(n - 1, 0, ((0, 0), (1, 0), (0, 1), (1, 1)))
                        ret_values(i - 1)
                    if 2 <= i < 10:
                        i2 = i - 2
                        g, q = i2 % 2, i2 // 2
                        values(n - 2, g, 4 * (l + 1) + q, g, VA[:, :, g * HD:(g + 1) * HD], ((0, 0, T, 0), (1, 0, T, T)))

                def head_sums(src):
                    norm[0] += 1
                    pe.wait_ge(sem("norm_in"), norm[0])
                    for k in range(KT):
                        mm = pe.matmul(ps(4 + k // 2, T, c0=(k % 2) * T), BLK[:, :], src[:, k, :], start=True, stop=True)
                    mm.then_inc(sem("norm_sum"), 1)

                head_sums(H)
                pe.wait_ge(sem("pair_copied"), 4 * (l + 2))
                lin = lins[f"wo_attn{l}"]
                for part in range(2):
                    feature_job(lin, 0, z(QA, QA + 4), 4, 512, part)
                head_sums(SQV)
                for part in range(2):
                    feature_job(lin, 1, z(QA, QA + 4), 4, 512, part)
                pe.wait_ge(sem("ret_out"), l + 1)
                for s in range(2):
                    for part in range(2):
                        feature_job(lins[f"wo_ret{l}"], s, z(QR, QR + 4), 4, 512, part)
                pe.wait_ge(sem("mix_ready"), l + 2)
                for s in range(4):
                    feature_job(lins[f"w_out{l}"], s, z(G2A, G2A + 8))
                layer_norm(X)
                pe.wait_ge(sem("x2_ready"), 2 * l + 2)

            mixer2(0)
            for s in range(11):
                feature_job(lins["ffn1"], s, X)
            for s in range(11):
                feature_job(lins["ffn3"], s, X)
            lin = lins["ffn2"]
            for s in range(11):
                w = weights(lin.at[s]).rearrange("p (k n) -> p k n", k=2)
                e, c = job_evac[lins["ffn3"].job0 + s]
                pe.wait_ge(sem("evac_" + e), max(c, job_evac[lin.job0 - 1][1] if s == 0 else 0))
                for i in range(2):
                    for j in range(KT):
                        k = 2 * s + i
                        mm = pe.matmul(ps(j // 2, T, c0=(j % 2) * T), w[:, i, j * P:(j + 1) * P],
                                       Z[:, k * T:(k + 1) * T], start=(k == 0 and j % 2 == 0), stop=(k == 21),
                                       skip_group_check=True)
                mm.then_inc(sem("lin_done"), 1)
            layer_norm(X)
            mixer2(1)
            experts(m2, X, WR2, "x2_ready", 4)
            layer_norm(X)

            pe.wait_ge(sem("x2_ready"), 5)
            for a in range(2):
                for k in range(KT):
                    tr = pe.transpose(ps(4 + 2 * a + k // 4, P, c0=(k % 4) * P), X[:, k, a * P:(a + 1) * P], IDENT[:, :])
            tr.then_inc(sem("out_turned"), 1)

        @block.scalar
        def _(act):
            ch = Chain(act, sem("act_step"))

            def rows_of(name, pat="l (r c) -> (l r) c"):
                return A[name].rearrange(pat, c=P)

            vec = [("c", 0, V_C, 8), ("b_ada", 0, V_BADA, 48), ("norm1_g", 0, V_N1G, 8), ("norm2_g", 0, V_N2G, 8),
                   ("final_g", 0, V_FG, 8), ("conv_b", 0, V_CB, 4), ("conv_ln_g", 0, V_CLG, 4),
                   ("conv_ln_b", 0, V_CLB, 4), ("ln_emb_g_2", 0, V_EG, 8), ("ln_emb_b_2", 0, V_EB, 8),
                   ("ln1_g_2", 1, 0, 16), ("ln1_b_2", 1, 16, 16), ("ln2_g_2", 1, 32, 16), ("ln2_b_2", 1, 48, 16),
                   ("b_gate_2", 1, 64, 32)]
            for name, tile, r, n in vec:
                src = rows_of(name, "(r c) -> r c" if len(A[name].shape) == 1 else "l (r c) -> (l r) c")
                act.dma_start(VROWS[r:r + n, tile, :], src).then_inc(sem("ld_vec"), 16)
            act.dma_start(VROWS[0:124, 2, :], A["conv_w"][0].rearrange("k (j c) -> (k j) c", c=P)).then_inc(sem("ld_vec"), 16)
            act.dma_start(VROWS[:, 3:7, :], A["b_exp_in"][0].rearrange("(t a) (j c) -> (a j) t c", t=4, c=P))\
                .then_inc(sem("ld_vec"), 16)
            act.dma_start(XT, A["x"][0].rearrange("(a p) d -> p a d", p=P)).then_inc(sem("ld_x"), 16)
            for name, c0, n in (("sink_logits_2", R_SINK, 16), ("decay_fwd_2", R_DECAY, 16), ("decay_bwd_2", R_DECAY + 16, 16),
                                ("b_router", R_BR1, 32), ("router_b_2", R_BR2, 8)):
                act.dma_start(ROWS[0:1, c0:c0 + n], A[name].rearrange("l h -> (l h)").unsqueeze(0)).then_inc(sem("ld_rows"), 16)
            act.dma_start(WF, w_in[0][:, 5 * CW:5 * CW + HEADS].rearrange("(k p) n -> p k n", p=P)).then_inc(sem("ld_small"), 16)
            act.dma_start(WR1[:, :, :], A["w_router"][0].rearrange("(k p) n -> p k n", p=P)).then_inc(sem("ld_small"), 16)
            act.dma_start(WR2[:, :, :], A["router_w_2"][0].rearrange("(k p) n -> p k n", p=P)).then_inc(sem("ld_small"), 16)
            act.dma_start(BFG[:, :], A["b_forget"].rearrange("l h -> h l")).then_inc(sem("ld_small"), 16)

            def linear_ready(lin, s, part=0):
                g = lin.group0 + (lin.groups if lin.k_major else s * lin.per + part + 1)
                act.wait_ge(sem("lin_done"), g)
                return (lin.job0 + s * lin.per + part) % 2

            sq = [0]

            def root():
                sq[0] += 1
                act.wait_ge(sem("root_in"), sq[0])
                act.activation(SQ[:, 0:T], SQ[:, 0:T], ACT.Sqrt).then_inc(sem("root_out"), 1)

            act.wait_ge(sem("vec_turned"), 1)
            V = PS[:, 0:3, :].rearrange("p b n -> p (b n)")
            act.activation(VEC[:, 0:108], V[:, 0:108], ACT.Copy)
            act.activation(VEC[:, P:P + 96], V[:, P:P + 96], ACT.Copy)
            act.activation(VEC[:, 2 * P:2 * P + 124], V[:, 2 * P:2 * P + 124], ACT.Copy)
            act.activation(VEC[:, 3 * P:4 * P], V[:, 3 * P:4 * P], ACT.Copy)
            ch.link(act.activation(VEC[:, 4 * P:7 * P], V[:, 4 * P:7 * P], ACT.Copy))
            act.wait_ge(sem("rows_spread"), 1)
            ch.link(act.activation(ROWB[:, :], ps(3, R_N), ACT.Copy))
            act.activation(CSIL[:, :], VEC[:, V_C:V_C + 8], ACT.Silu).then_inc(sem("init_act"), 1)
            act.wait_ge(sem("logsig_in"), 1)
            act.activation(SQ[:, 32:64], SQ[:, 0:32], ACT.Exp, scale=-1.0).then_inc(sem("logsig_exp"), 1)
            root()

            dst = [z(UV, UV + 2), z(UV + 2, UV + 4), z(UG, UG + 2), z(UG + 2, UG + 4),
                   z(Q1, Q1 + 2), z(Q1 + 2, Q1 + 4), z(K1, K1 + 2), z(K1 + 2, K1 + 4),
                   VT1[:, :, 0:256], VT1[:, :, 256:512]]
            for s in range(10):
                b = linear_ready(lins["uqkv_a"], s) if s < 4 else linear_ready(lins["uqkv_b"], s - 4)
                act.activation(dst[s], ps2(b), ACT.Sigmoid if s in (2, 3) else ACT.Copy).then_inc(sem("evac_act"), 1)
            b = linear_ready(lins["forget"], 0)
            act.wait_ge(sem("ld_small"), 16 * 4)
            act.activation(SQ[0:8, 0:T], PS[0:8, b, 0:T], ACT.Identity, bias=BFG[:, 0:1]).then_inc(sem("evac_act"), 1)
            act.wait_ge(sem("logsig_in"), 2)
            act.activation(SQ[0:8, 2 * T:3 * T], SQ[0:8, T:2 * T], ACT.Exp, scale=-1.0).then_inc(sem("logsig_exp"), 1)

            lin = lins["gates"]
            for i in range(10):
                if i < 8:
                    b = linear_ready(lin, i)
                    act.activation(z(GC + 2 * i, GC + 2 * i + 2), ps2(b), ACT.Sigmoid).then_inc(sem("evac_act"), 1)
                    h = i
                    act.wait_ge(sem("max_ready"), h + 1)
                    b = 4 + h % 2
                    st = ST[:, h % 2, :]
                    if h >= 2:
                        act.wait_ge(sem("probs_turned"), h - 1)
                    act.activation(PROB[:, h % 2, 0, 0:P], ps(b, P), ACT.Exp, bias=st[:, 2:3], scale=QSCALE,
                                   accum_out=st[:, 4:5])
                    act.activation(PROB[:, h % 2, 1, :], ps(b, T, c0=P), ACT.Exp, bias=st[:, 3:4], scale=QSCALE,
                                   accum_out=st[:, 5:6]).then_inc(sem("exp_done"), 1)
                if 1 <= i < 9:
                    n = i - 1
                    act.wait_ge(sem("probs_turned"), n + 1)
                    if n >= 2:
                        act.wait_ge(sem("values_done"), n - 1)
                    act.activation(PROBT[:, n % 2, 0:3 * P], ps(6, 3 * P), ACT.Copy).then_inc(sem("probs_copied"), 1)

            root()
            act.wait_ge(sem("conv_normed"), 1)
            for j in range(4):
                a = act.activation(Z[:, (UV + j) * T:(UV + j + 1) * T], Z[:, (UV + j) * T:(UV + j + 1) * T], ACT.Silu,
                                   bias=VEC[:, V_CLB + j:V_CLB + j + 1], scale=VEC[:, V_CLG + j:V_CLG + j + 1])
            a.then_inc(sem("conv_ready"), 1)
            act.dma_start(BOUT, A["b_exp_out"][0]).then_inc(sem("ld_bout"), 16)
            root()

            def experts(m):
                act.wait_ge(msem(m, "x_turned"), 1)
                act.activation(HT[:, 0, :], PS[:, 4:6, :].rearrange("p b n -> p (b n)"), ACT.Copy).then_inc(msem(m, "ht_act"), 1)

                def split_hi(g, s, first=False):
                    act.wait_ge(sem(f"m1_raw{s % RAW_N}"), g * 32 + 16 * (s // RAW_N + 1))
                    if not first:
                        act.wait_ge(msem(m, "group_done"), g * NG + (s + 1 - SPLIT_N))
                    act.activation(WHI[:, s % SPLIT_N, :], RAW[:, s % RAW_N, :], ACT.Copy).then_inc(sem("m1_hi"), 1)

                if m is m1:
                    act.wait_ge(sem("lin_done"), free_at[N_A - 1][1])
                    for s in range(2):
                        split_hi(0, s, first=True)
                act.wait_ge(msem(m, "top"), 1)
                for a in range(2):
                    e = act.activation(GATE[:, a, 0:m.n], LOG[:, a, 0:m.n], ACT.Exp, bias=NTOP[:, a:a + 1])
                e.then_inc(msem(m, "gate_exp"), 1)
                if m is m1:
                    for s in range(2, SPLIT_N):
                        split_hi(0, s, first=True)
                act.wait_ge(msem(m, "tables"), 1)
                count = act.value_load(TAB[0:1, 2 * P + 32:2 * P + 33], min_val=m.n, max_val=48)

                if m is m1:
                    act.wait_ge(sem("gates_turned"), 1)
                    act.activation(GT[0:32, :], ps(3, T, 0, 32), ACT.Copy).then_inc(sem("gates_copied"), 1)

                def gathered(g1):
                    act.wait_ge(msem(m, "gathered"), g1)
                    act.activation(XG.rearrange("p k c -> p (k c)"), PS[:, 6:8, :].rearrange("p b n -> p (b n)"), ACT.Copy)\
                        .then_inc(msem(m, "xg"), 1)

                def turned(g):
                    act.wait_ge(msem(m, "turned"), g + 1)
                    act.activation(GT, ps(6, T), ACT.Copy).then_inc(msem(m, "turned_copied"), 1)

                act.wait_ge(msem(m, "ys_dve"), 1)
                act.activation(YS[:, 512:1024], YS[:, 0:512], ACT.Copy).then_inc(msem(m, "ys_act"), 1)
                if m is m1:
                    def tokens_hi(g1):
                        act.wait_ge(msem(m, "gathered"), g1)
                        for b in range(2):
                            i = act.activation(X2[:, 4 * b:4 * b + 4, 0:HALF], ps(6 + b).rearrange("p (k c) -> p k c", k=4)[:, :, 0:HALF],
                                               ACT.Copy)
                        i.then_inc(msem(m, "x_hi"), 1)

                    tokens_hi(1)
                    with act.Fori(0, count) as g:
                        split_hi(g, 4)
                        turned(g)
                        for s in range(5, 11):
                            split_hi(g, s)
                        act.wait_ge(msem(m, "group_done"), g * NG + 8)
                        act.activation(HS[:, 0:1024], PS[:, 0:2, :].rearrange("p b n -> p (b n)"), ACT.Copy)\
                            .then_inc(msem(m, "hs_act"), 1)
                        tokens_hi(g + 2)
                        split_hi(g, 11)
                        act.wait_ge(msem(m, "gate_part"), g + 1)
                        act.activation(SIG, GPART, ACT.Sigmoid, scale=1.702).then_inc(msem(m, "sig"), 1)
                        for s in range(3):
                            split_hi(g + 1, s)
                        act.wait_ge(msem(m, "group_done"), g * NG + NG)
                        act.activation(YS[:, 512:1024], ps(5), ACT.Copy).then_inc(msem(m, "ys_act"), 1)
                        split_hi(g + 1, 3)
                else:
                    gathered(1)
                    with act.Fori(0, count) as g:
                        turned(g)
                        act.wait_ge(msem(m, "group_done"), g * NG + 8)
                        act.wait_ge(msem(m, "hm"), g * 3 + 1)
                        for i in range(3):
                            n = min(512, 1408 - i * 512)
                            act.activation(PART[:, i * 512:i * 512 + n], ps(i, n), ACT.Silu).then_inc(msem(m, "sig"), 1)
                        gathered(g + 2)
                        act.wait_ge(msem(m, "group_done"), g * NG + NG)
                        act.activation(YS[:, 512:1024], ps(1), ACT.Copy).then_inc(msem(m, "ys_act"), 1)
                turned(count)

            experts(m1)
            root()
            root()

            def mixer2(l):
                def copy(lin, s, dst, f=ACT.Copy, part=0):
                    b = linear_ready(lin, s, part)
                    act.activation(dst, ps2(b), f).then_inc(sem("evac_act"), 1)

                for s in range(2):
                    copy(lins[f"qa{l}"], s, z(QA + 2 * s, QA + 2 * s + 2))
                b = linear_ready(lins[f"kva{l}"], 0, 0)
                act.activation(Z[:, KA * T:(KA + 1) * T], ps(b, T), ACT.Copy).then_inc(sem("evac_act"), 1)
                b = linear_ready(lins[f"kva{l}"], 0, 1)
                act.activation(VA, PS[:, b, 0:T].rearrange("p (a n) -> p a n", a=2), ACT.Copy).then_inc(sem("evac_act"), 1)
                lin = lins[f"ret{l}"]
                copy(lin, 0, z(QR, QR + 2))
                copy(lin, 1, z(KR, KR + 2))
                copy(lin, 2, VR[:, :, 0:256])
                copy(lin, 3, VR[:, :, 256:512])
                lin = lins[f"gg{l}"]
                for i in range(12):
                    if i < 4:
                        copy(lin, i, z(GF + 2 * i, GF + 2 * i + 2), ACT.Silu)
                    else:
                        b = linear_ready(lin, i)
                        for j in range(2):
                            t = 2 * (i - 4) + j
                            a = act.activation(Z[:, (G2A + t) * T:(G2A + t + 1) * T], ps(b, T, c0=j * T), ACT.Sigmoid,
                                               bias=VEC[:, V_BG + 16 * l + t:V_BG + 16 * l + t + 1])
                        a.then_inc(sem("evac_act"), 1)
                    if i < 8:
                        h = 4 * (i % 2) + i // 2
                        n = HEADS * (l + 1) + i
                        rn = HEADS * l + i
                        if i >= 2:
                            act.wait_ge(sem("ret_weighted"), rn - 1)
                        for d in range(2):
                            c = 16 * d + HEADS * l + i
                            for j in range(2):
                                a = act.activation(DEC[:, i % 2, (2 * d + j) * P:(2 * d + j + 1) * P], LAGS[:, 2 * d + j, :],
                                                   ACT.Exp, scale=LG[:, c:c + 1])
                        a.then_inc(sem("decay_exp"), 1)
                        st = ST[:, i % 2, :]
                        act.wait_ge(sem("max_ready"), n + 1)
                        act.activation(st[:, 6:8], st[:, 2:4], ACT.Exp, bias=ROWB[:, R_SINK + HEADS * l + h:R_SINK + HEADS * l + h + 1])
                        for a_ in range(2):
                            a = act.activation(PROB[:, i % 2, a_, :], PROB[:, i % 2, a_, :], ACT.Exp, bias=st[:, 2 + a_:3 + a_],
                                               scale=QSCALE, accum_out=st[:, 4 + a_:5 + a_])
                        a.then_inc(sem("exp_done"), 1)
                    if 1 <= i < 9:
                        n = HEADS * (l + 1) + i - 1
                        act.wait_ge(sem("probs_turned"), n + 1)
                        act.wait_ge(sem("values_done"), n - 1)
                        act.activation(PROBT[:, n % 2, :], ps(6), ACT.Copy).then_inc(sem("probs_copied"), 1)
                        if i % 2 == 0:
                            pr = i // 2 - 1
                            act.wait_ge(sem("ret_values"), HEADS * l + i)
                            for d in range(2):
                                a = act.activation(H[:, 4 * d + pr, :], ps(3, T, c0=d * T), ACT.Copy)
                            a.then_inc(sem("ret_copied"), 1)
                sq[0] += 1
                act.wait_ge(sem("root_in"), sq[0])
                act.activation(SQ[:, :], SQ[:, :], ACT.Sqrt).then_inc(sem("root_out"), 1)
                root()

            mixer2(0)
            for s in range(11):
                b = linear_ready(lins["ffn1"], s)
                act.activation(z(2 * s, 2 * s + 2), ps2(b), ACT.Silu).then_inc(sem("evac_act"), 1)
            root()
            mixer2(1)
            experts(m2)
            root()
            act.wait_ge(sem("out_turned"), 1)
            for b in range(4):
                act.activation(XT[:, b // 2, (b % 2) * 512:(b % 2) * 512 + 512], ps(4 + b), ACT.Copy)\
                    .then_inc(sem("out_staged"), 1)

        @block.vector
        def _(dve):
            ch = Chain(dve, sem("dve_step"))
            link = ch.link
            norm, rt = [0], [0]
            SQV = SQ[:, :].rearrange("p (k t) -> p k t", t=T)

            def log_sigmoid(y, t, n, k):
                link(dve.scalar_tensor_tensor(out=t[0], in0=y, scalar=-1.0, in1=y, op0=ALU.mult, op1=ALU.max))
                dve.tensor_scalar(t[0], t[0], 0.0, None, ALU.max).then_inc(sem("logsig_in"), 1)
                dve.wait_ge(sem("logsig_exp"), k)
                link(dve.tensor_scalar(t[2], t[1], 2.0, None, ALU.add))
                link(dve.reciprocal(t[2], t[2]))
                link(dve.tensor_tensor(t[1], t[1], t[2], ALU.mult))
                link(dve.tensor_tensor(t[2], t[1], t[1], ALU.mult))
                link(dve.tensor_scalar(t[3], t[2], 1.0 / 17.0, None, ALU.mult))
                for c in (15, 13, 11, 9, 7, 5, 3):
                    link(dve.scalar_tensor_tensor(out=t[3], in0=t[3], scalar=1.0 / c, in1=t[2], op0=ALU.add, op1=ALU.mult))
                link(dve.scalar_tensor_tensor(out=t[3], in0=t[3], scalar=1.0, in1=t[1], op0=ALU.add, op1=ALU.mult))
                link(dve.tensor_scalar(t[2], y, 0.0, None, ALU.min))
                link(dve.scalar_tensor_tensor(out=t[4], in0=t[3], scalar=-2.0, in1=t[2], op0=ALU.mult, op1=ALU.add))

            def sums():
                norm[0] += 1
                dve.wait_ge(sem("norm_sum"), norm[0])

            def reciprocal_root(sum_, n, w=T):
                for o, s in sum_:
                    i = dve.tensor_scalar(o, s, 1.0 / n, EPS, ALU.mult, ALU.add)
                i.then_inc(sem("root_in"), 1)
                rt[0] += 1
                dve.wait_ge(sem("root_out"), rt[0])
                link(dve.reciprocal(SQ[:, 0:w], SQ[:, 0:w]))

            def rms(src, dst, gain, bias):
                dve.tensor_tensor(SQV, src, src, ALU.mult).then_inc(sem("norm_in"), 1)
                sums()
                reciprocal_root([(SQ[:, 0:T], ps(4, T))], D)
                link(dve.tensor_tensor(dst, src, bc(SQ[:, 0:T], KT), ALU.mult))
                return affine(dst, gain, bias)

            def affine(dst, gain, bias):
                for k in range(dst.shape[1]):
                    if bias is None:
                        i = dve.tensor_scalar(dst[:, k, :], dst[:, k, :], gain[:, k:k + 1], None, ALU.mult)
                    else:
                        i = dve.tensor_scalar(dst[:, k, :], dst[:, k, :], gain[:, k:k + 1], bias[:, k:k + 1], ALU.mult, ALU.add)
                return i

            def centre(x, nk, n):
                sums()
                link(dve.scalar_tensor_tensor(out=x, in0=bc(ps(4, T), nk), scalar=-1.0 / n, in1=x,
                                              op0=ALU.mult, op1=ALU.add))
                dve.tensor_tensor(SQV[:, 0:nk, :], x, x, ALU.mult).then_inc(sem("norm_in"), 1)
                sums()
                reciprocal_root([(SQ[:, 0:T], ps(4, T, c0=T))], n)
                return dve.tensor_tensor(x, x, bc(SQ[:, 0:T], nk), ALU.mult)

            def layer_norm(x, g, b, ready):
                link(centre(x, KT, D))
                affine(x, g, b).then_inc(sem(ready), 1)

            def linear_ready(lin, s, part=0):
                g = lin.group0 + (lin.groups if lin.k_major else s * lin.per + part + 1)
                dve.wait_ge(sem("lin_done"), g)
                return (lin.job0 + s * lin.per + part) % 2

            dve.wait_ge(sem("pool_step"), 18)
            link(dve.tensor_scalar(LAGS[:, 0, :], LAGS[:, 0, :], 0.0, None, ALU.max))
            link(dve.tensor_scalar(LAGS[:, 3, :], LAGS[:, 3, :], 0.0, None, ALU.max))
            dve.wait_ge(sem("pool_step"), 19)
            dve.scalar_tensor_tensor(out=DIST[:, :, :], in0=DIST[:, :, :], scalar=-1.0, in1=DIST[:, :, :],
                                     op0=ALU.mult, op1=ALU.max).then_inc(sem("dist_abs"), 1)
            dve.wait_ge(sem("init_act"), 1)
            log_sigmoid(ROWB[:, R_DECAY:R_DECAY + 32],
                        [SQ[:, 0:32], SQ[:, 32:64], SQ[:, 64:96], SQ[:, 96:128], LG[:, :]], 32, 1)
            dve.wait_ge(sem("x_turned"), 1)
            for b in range(4):
                i = dve.tensor_copy(X[:, 2 * b:2 * b + 2, :], ps2(4 + b))
            i.then_inc(sem("x_ready"), 1)
            dve.wait_ge(sem("x_ready"), 1)

            def ada_products(l):
                lin = lins[f"ada{l}"]
                for s in range(KT):
                    r, c = arrive[lin.at[s]]
                    dve.wait_ge(sem(f"arrived{r}"), c)
                    w = slot(lin.at[s])[0]
                    if s == 0:
                        i = dve.tensor_scalar(ADA, w, CSIL[:, 0:1], None, ALU.mult)
                    else:
                        dve.wait_ge(sem("ada_used"), 8 * l + s)
                        i = dve.scalar_tensor_tensor(out=ADA, in0=w, scalar=CSIL[:, s:s + 1], in1=ADA, op0=ALU.mult, op1=ALU.add)
                    i.then_inc(sem("ada_used"), 1)

            def ada(l):
                b = linear_ready(lins[f"ada{l}"], 0)
                dve.tensor_tensor(MOD[:, 16 * l:16 * l + 16], ps(b, 16), VEC[:, V_BADA + 16 * l:V_BADA + 16 * l + 16],
                                  ALU.add).then_inc(sem("evac_dve"), 1)
                dve.wait_ge(sem("evac_dve"), l + 1)

            ada_products(0)
            ada(0)
            link(dve.scalar_tensor_tensor(out=GS[:, 0:8], in0=MOD[:, 8:16], scalar=1.0, in1=VEC[:, V_N1G:V_N1G + 8],
                                          op0=ALU.add, op1=ALU.mult))
            rms(X[:, :, :], H[:, :, :], GS[:, 0:8], MOD[:, 0:8]).then_inc(sem("h_ready"), 1)

            ada_products(1)
            ada(1)
            dve.wait_ge(sem("evac_act"), 4)
            link(dve.tensor_tensor(CONV_IN[:, :, TAPS - 1:], z(UV, UV + 4), z(UG, UG + 4), ALU.mult))
            conv = [0]

            def taps(n):
                for k in range(conv[0], min(conv[0] + n, TAPS)):
                    for j in range(4):
                        o = Z[:, (UV + j) * T:(UV + j + 1) * T]
                        w = VEC[:, V_CONVW + 4 * k + j:V_CONVW + 4 * k + j + 1]
                        if k == 0:
                            i = dve.tensor_scalar(o, CONV_IN[:, j, 0:T], w, VEC[:, V_CB + j:V_CB + j + 1], ALU.mult, ALU.add)
                        else:
                            dve.wait_ge(sem("tap"), 4 * (k - 1) + j + 1)
                            i = dve.scalar_tensor_tensor(out=o, in0=CONV_IN[:, j, k:k + T], scalar=w, in1=o,
                                                         op0=ALU.mult, op1=ALU.add)
                        i.then_inc(sem("tap"), 1)
                conv[0] = min(conv[0] + n, TAPS)

            ada_products(2)
            taps(3)
            dve.wait_ge(sem("evac_act"), 11)
            R = [SQ[0:8, i * T:(i + 1) * T] for i in range(8)]
            log_sigmoid(R[0], R[1:6], 256, 2)
            link(dve.memset(R[6], 1.0))
            link(dve.tensor_tensor_scan(R[7], R[6], R[5], 0.0, ALU.mult, ALU.add))
            dve.tensor_scalar(NEGF[0:8, :], R[7], -1.0 / QSCALE, None, ALU.mult).then_inc(sem("negf_ready"), 1)
            ada(2)

            def normalise(n, widths):
                st = ST[:, n % 2, :]
                link(dve.reciprocal(st[:, 0:2], st[:, 4:6]))
                for a in range(2):
                    o = PROB[:, n % 2, a, 0:widths[a]]
                    i = dve.tensor_scalar(o, o, st[:, a:a + 1], None, ALU.mult)
                i.then_inc(sem("probs_ready"), 1)

            for i in range(10):
                if i < 8:
                    h = i
                    st = ST[:, h % 2, :]
                    dve.wait_ge(sem("scores_ready"), h + 1)
                    dve.reduce_max(st[:, 0:1], ps(4 + h % 2, P), AX)
                    link(dve.reduce_max(st[:, 1:2], ps(4 + h % 2, T, c0=P), AX))
                    dve.tensor_scalar(st[:, 2:4], st[:, 0:2], -QSCALE, None, ALU.mult).then_inc(sem("max_ready"), 1)
                    taps(3)
                    dve.wait_ge(sem("exp_done"), h + 1)
                    normalise(h, (P, T))
                if i >= 2 and i % 2 == 1:
                    p = (i - 3) // 2
                    dve.wait_ge(sem("values_done"), 2 * p + 2)
                    dve.tensor_copy(Z[:, (UG + p) * T:(UG + p + 1) * T], ps(7, T, c0=(p % 2) * T)).then_inc(sem("pair_copied"), 1)
            taps(TAPS)
            dve.wait_ge(sem("tap"), 4 * TAPS)
            link(dve.tensor_copy(GS[:, 16:17], GS[:, 0:1]))
            dve.tensor_copy(GS[:, 17:18], GS[:, 0:1]).then_inc(sem("norm_in"), 1)
            centre(z(UV, UV + 4), 4, CW).then_inc(sem("conv_normed"), 1)

            def gated(lin, g0, acc=None):
                for s in range(2):
                    for part in range(2):
                        b = linear_ready(lin, s, part)
                        t = 4 * s + 2 * part
                        o = z(g0 + t, g0 + t + 2)
                        i = dve.tensor_tensor(o, ps2(b), o, ALU.mult)
                        i.then_inc(sem("evac_dve"), 1)

            gated(lins["conv_out"], GC)
            gated(lins["attn_out"], GA)
            dve.wait_ge(sem("evac_dve"), job_evac[lins["attn_out"].job0 + 3][1])
            dve.tensor_tensor(z(GC, GC + 8), z(GC, GC + 8), z(GA, GA + 8), ALU.add).then_inc(sem("mix_ready"), 1)
            lin = lins["w_out"]
            for s in range(4):
                b = linear_ready(lin, s)
                for j in range(2):
                    k = 2 * s + j
                    i = dve.scalar_tensor_tensor(out=X[:, k, :], in0=ps(b, T, c0=j * T), scalar=MOD[:, 16 + k:17 + k],
                                                 in1=X[:, k, :], op0=ALU.mult, op1=ALU.add)
                i.then_inc(sem("evac_dve"), 1)
            dve.wait_ge(sem("evac_dve"), job_evac[lin.job0 + 3][1])
            link(dve.scalar_tensor_tensor(out=GS[:, 8:16], in0=MOD[:, 32:40], scalar=1.0, in1=VEC[:, V_N2G:V_N2G + 8],
                                          op0=ALU.add, op1=ALU.mult))
            rms(X[:, :, :], H[:, :, :], GS[:, 8:16], MOD[:, 24:32]).then_inc(sem("h_ready"), 1)

            def experts(m, br):
                E, top = m.n, m.top
                dve.wait_ge(sem("h_ready") if m is m1 else sem("x2_ready"), 2 if m is m1 else 4)
                if m is m2:
                    link(dve.memset(Y, 0.0))
                link(dve.memset(LOG[:, :, E:E + 8], NEG))
                link(dve.memset(ONE32, 1.0))
                dve.memset(YS[:, 0:512], 0.0).then_inc(msem(m, "ys_dve"), 1)
                dve.memset(PICKG, 0.0).then_inc(msem(m, "pickg"), 1)
                if m is m2:
                    dve.memset(PART[:, 0:1], 0.0).then_inc(msem(m, "hm"), 1)
                for name in ("ys_dve", "pickg") + (("hm",) if m is m2 else ()):
                    dve.wait_ge(msem(m, name), 1)
                dve.memset(FREE, 0.0).then_inc(sem("moe_scratch_free"), 1)
                dve.wait_ge(sem("moe_scratch_free"), 1 if m is m1 else 2)
                dve.wait_ge(msem(m, "x_turned"), 1)
                dve.tensor_copy(HT[:, 1, :], PS[:, 6:8, :].rearrange("p b n -> p (b n)")).then_inc(msem(m, "ht_dve"), 1)
                dve.wait_ge(msem(m, "logits"), 1)
                link(dve.tensor_tensor(LOG[:, :, 0:E], PS[:, 0, 0:2 * E].rearrange("p (a e) -> p a e", a=2),
                                       bc(ROWB[:, br:br + E], 2), ALU.add))
                for a in range(2):
                    link(dve.max(TOP8[:, a, :], LOG[:, a, 0:E]))
                link(dve.tensor_scalar(NTOP, TOP8[:, :, 0], -1.0, None, ALU.mult))
                dve.memset(TOP8[:, :, top:8], NEG).then_inc(msem(m, "top"), 1)
                dve.wait_ge(msem(m, "top"), 1)
                for a in range(2):
                    link(dve.match_replace(LOGR[:, a, 0:E + 8], TOP8[:, a, :], LOG[:, a, 0:E + 8], 3e38))
                dve.tensor_tensor(MASK[:, :, 0:E], LOGR[:, :, 0:E], LOG[:, :, 0:E], ALU.not_equal).then_inc(msem(m, "mask"), 1)
                dve.wait_ge(msem(m, "mask"), 1)
                dve.wait_ge(msem(m, "gate_exp"), 1)
                link(dve.tensor_tensor(GATE[:, :, 0:E], GATE[:, :, 0:E], MASK[:, :, 0:E], ALU.mult))
                link(dve.reduce_sum(GSUM, GATE[:, :, 0:E], AX))
                link(dve.reciprocal(GSUM, GSUM))
                dve.tensor_tensor(GATE[:, :, 0:E], GATE[:, :, 0:E], bl(GSUM, E), ALU.mult).then_inc(msem(m, "gates"), 1)
                dve.wait_ge(msem(m, "gates"), 1)
                dve.wait_ge(msem(m, "counts"), 1)
                n = ps(1, E)
                link(dve.tensor_scalar(NCH[:, 0:E], n, float(m.slots), 1.0, ALU.is_gt, ALU.add))
                for more in range(2 * m.slots, T, m.slots):
                    link(dve.scalar_tensor_tensor(out=NCH[:, 0:E], in0=n, scalar=float(more), in1=NCH[:, 0:E],
                                                  op0=ALU.is_gt, op1=ALU.add))
                link(dve.tensor_tensor_scan(CUM[:, 0:E], ONE32[:, 0:E], NCH[:, 0:E], 0.0, ALU.mult, ALU.add))
                link(dve.tensor_tensor(START[:, 0:E], CUM[:, 0:E], NCH[:, 0:E], ALU.subtract))
                for a in range(2):
                    link(dve.scalar_tensor_tensor(out=RANK[:, a, 0:E], in0=ps(1, E, c0=64 + 32 * a), scalar=1.0,
                                                  in1=MASK[:, a, 0:E], op0=ALU.add, op1=ALU.mult))
                link(dve.tensor_scalar(RANK[:, :, 0:E], RANK[:, :, 0:E], -1.0, None, ALU.add))
                link(dve.tensor_scalar(LE[:, 0:E], CUM[:, 0:E], IOTAP[:, 0:1], None, ALU.is_le))
                link(dve.tensor_tensor(LEN_[:, 0:E], LE[:, 0:E], NCH[:, 0:E], ALU.mult))
                link(dve.reduce_sum(TCOL[:, 0:1], LE[:, 0:E], AX))
                link(dve.reduce_sum(TCOL[:, 1:2], LEN_[:, 0:E], AX))
                link(dve.tensor_scalar(TCOL[:, 0:1], TCOL[:, 0:1], float(E - 1), None, ALU.min))
                link(dve.tensor_tensor(TCOL[:, 1:2], IOTAP[:, 0:1], TCOL[:, 1:2], ALU.subtract))
                dve.tensor_scalar(TCOL[:, 1:2], TCOL[:, 1:2], float(T // m.slots - 1), float(m.slots), ALU.min, ALU.mult)\
                    .then_inc(msem(m, "table_cols"), 1)
                dve.wait_ge(msem(m, "table_rows"), 1)
                link(dve.tensor_copy(TAB[0:1, 0:2 * P], ps(2, 2 * P, 0, 1)))
                link(dve.tensor_scalar(TAB[0:1, 2 * P:2 * P + E], START[0:1, 0:E], -1.0, None, ALU.add))
                link(dve.tensor_scalar(TAB[0:1, 2 * P + 33:2 * P + 34], CUM[0:1, E - 1:E], -1.0, None, ALU.add))
                dve.tensor_copy(TAB[0:1, 2 * P + 32:2 * P + 33], CUM[0:1, E - 1:E]).then_inc(msem(m, "tables"), 1)
                dve.wait_ge(msem(m, "tables"), 1)
                count = dve.value_load(TAB[0:1, 2 * P + 32:2 * P + 33], min_val=m.n, max_val=48)
                dve.wait_ge(msem(m, "iota"), 1)
                if m is m1:
                    dve.wait_ge(sem("bias_sum"), 1)
                    dve.tensor_copy(Y.rearrange("p k t -> p (k t)"), PS[:, 4:8, :].rearrange("p b n -> p (b n)"))\
                        .then_inc(sem("bias_copied"), 1)
                    dve.wait_ge(sem("bias_copied"), 1)

                def window(c):
                    return IOTA[:, bass.ds(c, m.slots)].unsqueeze(1).broadcast_to([P, CHUNK // m.slots, m.slots])

                def slots_of(ap):
                    return ap.rearrange("p (r c) -> p r c", c=m.slots)

                def pick(e, c):
                    for a in range(2):
                        i = dve.tensor_scalar(slots_of(PICK[:, a, :]), window(c), RANK[:, a, bass.ds(e, 1)], None,
                                              ALU.is_equal)
                    i.then_inc(msem(m, "pick"), 1)

                def pick_gated(e, c):
                    for a in range(2):
                        i = dve.tensor_scalar(slots_of(PICKG[:, a, :]), window(c), RANK[:, a, bass.ds(e, 1)],
                                              GATE[:, a, bass.ds(e, 1)], ALU.is_equal, ALU.mult)
                    i.then_inc(msem(m, "pickg"), 1)

                def add(g, qs_=range(4)):
                    for q in qs_:
                        dve.wait_ge(msem(m, "scattered"), g * 4 + (q + 1))
                        o = Y[:, 2 * q:2 * q + 2, :]
                        dve.tensor_tensor(o, o, ps2(6 + q % 2), ALU.add).then_inc(msem(m, "added"), 1)

                def tokens_lo(g1):
                    dve.wait_ge(msem(m, "gathered"), g1)
                    dve.wait_ge(msem(m, "x_hi"), g1)
                    for b in range(2):
                        i = dve.tensor_tensor(X2[:, 4 * b:4 * b + 4, HALF:], ps(6 + b).rearrange("p (k c) -> p k c", k=4)[:, :, HALF:],
                                              X2[:, 4 * b:4 * b + 4, 0:HALF].bitcast(F32), ALU.subtract)
                    i.then_inc(msem(m, "x_lo"), 1)

                def chunk_of(g):
                    return (dve.value_load(TAB[0:1, bass.ds(g, 1)], min_val=0, max_val=m.n - 1),
                            dve.value_load(TAB[0:1, bass.ds(g + P, 1)], min_val=0, max_val=T - m.slots))

                if m is m1:
                    dve.memset(FREE, 0.0).then_inc(msem(m, "added"), 1)
                    dve.wait_ge(msem(m, "added"), 1)
                pick(0, 0)
                mch = Chain(dve, msem(m, "dve_step"))
                if m is m1:
                    dve.tensor_tensor(STACK, IDENT[:, 0:HALF], IDENT[:, HALF:], ALU.add).then_inc(sem("stack_ready"), 1)
                    tokens_lo(1)
                    for s in (0, 1, 3):
                        split_lo(dve, 0, s, first=True)
                    with dve.Fori(0, count) as g:
                        mch.enter(g * 7)
                        split_lo(dve, g, 4)
                        e, c = chunk_of(g)
                        dve.wait_ge(msem(m, "turned"), g + 1)
                        pick_gated(e, c)
                        mch.link(dve.tensor_copy(B1C, VEC[:, bass.ds(e * 16 + V_B1, 16)]))
                        for s in (6, 7):
                            split_lo(dve, g, s)
                        e1, c1 = chunk_of(g + 1)
                        dve.wait_ge(msem(m, "gathered"), g + 1)
                        pick(e1, c1)
                        for s in (9, 10):
                            split_lo(dve, g, s)
                        dve.wait_ge(msem(m, "group_done"), g * NG + 8)
                        dve.tensor_copy(HS[:, 1024:2048], PS[:, 2:4, :].rearrange("p b n -> p (b n)"))\
                            .then_inc(msem(m, "hs_dve"), 1)
                        tokens_lo(g + 2)
                        hidden = [ps(4 + i).rearrange("p (k c) -> p k c", k=KT) for i in range(2)]
                        dve.wait_ge(msem(m, "hidden_turned"), g * 2 + 1)
                        mch.link(dve.tensor_tensor(GPART, hidden[0], bl(B1C[:, 0:KT], HALF), ALU.add))
                        dve.tensor_scalar(GPART, GPART, 7.0, None, ALU.min).then_inc(msem(m, "gate_part"), 1)
                        dve.wait_ge(msem(m, "hidden_turned"), g * 2 + 2)
                        mch.link(dve.tensor_tensor(UPART, hidden[1], bl(B1C[:, KT:2 * KT], HALF), ALU.add))
                        mch.link(dve.tensor_scalar(UPART, UPART, 7.0, -7.0, ALU.min, ALU.max))
                        dve.wait_ge(msem(m, "gate_part"), g + 1)
                        mch.link(dve.scalar_tensor_tensor(out=UPART, in0=UPART, scalar=1.0, in1=GPART, op0=ALU.add, op1=ALU.mult))
                        dve.wait_ge(msem(m, "sig"), g + 1)
                        mch.link(dve.tensor_tensor(UPART, UPART, SIG, ALU.mult))
                        mch.link(dve.tensor_copy(HM2[:, :, 0:HALF], UPART))
                        dve.tensor_tensor(HM2[:, :, HALF:], UPART, HM2[:, :, 0:HALF].bitcast(F32), ALU.subtract)\
                            .then_inc(msem(m, "hm"), 1)
                        dve.wait_ge(msem(m, "hm"), g + 1)
                        add(g, (0, 1))
                        for s in (0, 1):
                            split_lo(dve, g + 1, s)
                        add(g, (2, 3))
                        dve.wait_ge(msem(m, "group_done"), g * NG + NG)
                        dve.tensor_copy(YS[:, 0:512], ps(4)).then_inc(msem(m, "ys_dve"), 1)
                        split_lo(dve, g + 1, 3)
                        assert mch.n == 7, mch.n
                    dve.wait_ge(sem("m1_lo_pool"), count * LO_POOL + 1)
                    dve.wait_ge(sem("m1_lo_dve"), count * LO_DVE + 3)
                    dve.memset(FREE, 0.0).then_inc(sem("m1_bytes_free"), 1)
                else:
                    with dve.Fori(0, count) as g:
                        e, c = chunk_of(g)
                        dve.wait_ge(msem(m, "turned"), g + 1)
                        pick_gated(e, c)
                        e1, c1 = chunk_of(g + 1)
                        dve.wait_ge(msem(m, "gathered"), g + 1)
                        pick(e1, c1)
                        add(g)
                        dve.wait_ge(msem(m, "group_done"), g * NG + 8)
                        for i in range(3):
                            n = min(512, 1408 - i * 512)
                            dve.wait_ge(msem(m, "sig"), g * 3 + (i + 1))
                            dve.tensor_tensor(HM.rearrange("p k c -> p (k c)")[:, i * 512:i * 512 + n], ps(3 + i, n),
                                              PART[:, i * 512:i * 512 + n], ALU.mult).then_inc(msem(m, "hm"), 1)
                        dve.wait_ge(msem(m, "group_done"), g * NG + NG)
                        dve.tensor_copy(YS[:, 0:512], ps(0)).then_inc(msem(m, "ys_dve"), 1)
                add(count)
                dve.wait_ge(msem(m, "added"), count * 4 + (4 + m.free))

            experts(m1, R_BR1)
            for k in range(KT):
                i = dve.scalar_tensor_tensor(out=X[:, k, :], in0=Y[:, k, :], scalar=MOD[:, 40 + k:41 + k], in1=X[:, k, :],
                                             op0=ALU.mult, op1=ALU.add)
            link(i)
            i = rms(X[:, :, :], X[:, :, :], VEC[:, V_FG:V_FG + 8], None)
            i.then_inc(sem("norm_in"), 1)
            dve.wait_ge(sem("norm_in"), norm[0] + 1)
            layer_norm(X[:, :, :], VEC[:, V_EG:V_EG + 8], VEC[:, V_EB:V_EB + 8], "x2_ready")

            def vcols(c, l):
                return VEC[:, c + 8 * l:c + 8 * l + 8]

            def residual(lin, ready):
                for s in range(4):
                    b = linear_ready(lin, s)
                    o = X[:, 2 * s:2 * s + 2, :]
                    dve.scalar_tensor_tensor(out=o, in0=o, scalar=ALPHA, in1=ps2(b), op0=ALU.mult, op1=ALU.add)\
                        .then_inc(sem("evac_dve"), 1)
                dve.wait_ge(sem("evac_dve"), job_evac[lin.job0 + lin.jobs - 1][1])

            def x_in():
                dve.tensor_copy(GS[:, 16:17], GS[:, 0:1]).then_inc(sem("norm_in"), 1)

            def mixer2(l):
                dve.wait_ge(sem("dist_ready"), 1)
                for i in range(12):
                    n = HEADS * (l + 1) + i
                    if i < 8:
                        h = 4 * (i % 2) + i // 2
                        st = ST[:, i % 2, :]
                        dve.wait_ge(sem("scores_ready"), n + 1)
                        dve.wait_ge(sem("probs_turned"), n - 1)
                        pr = PROB[:, i % 2]
                        link(dve.scalar_tensor_tensor(out=pr, in0=DIST[:, :, :], scalar=-SLOPES[h] / QSCALE, in1=ps2(4 + i % 2),
                                                      op0=ALU.mult, op1=ALU.add))
                        link(dve.reduce_max(st[:, 0:2], pr, AX))
                        sk = ROWB[:, R_SINK + HEADS * l + h:R_SINK + HEADS * l + h + 1]
                        link(dve.tensor_scalar(st[:, 0:2], st[:, 0:2], QSCALE, sk, ALU.mult, ALU.max))
                        dve.tensor_scalar(st[:, 2:4], st[:, 0:2], -1.0, None, ALU.mult).then_inc(sem("max_ready"), 1)
                        rn = HEADS * l + i
                        dve.wait_ge(sem("ret_scores"), rn + 1)
                        dve.wait_ge(sem("decay_masked"), rn + 1)
                        if i >= 2:
                            dve.wait_ge(sem("ret_values"), rn - 1)
                        dec, ra = DEC[:, i % 2, :], RA[:, i % 2]
                        for o, p_, d_ in ((ra[:, 0, 0, :], ps(2, T), dec[:, 0:T]),
                                          (ra[:, 0, 1, P:T], ps(2, P, c0=3 * P), dec[:, 0:P]),
                                          (ra[:, 1, 1, :], ps(2, T, c0=T), dec[:, T:2 * T]),
                                          (ra[:, 1, 0, 0:P], ps(2, P), dec[:, 3 * P:4 * P])):
                            j = dve.scalar_tensor_tensor(out=o, in0=p_, scalar=RSCALE, in1=d_, op0=ALU.mult, op1=ALU.mult)
                        j.then_inc(sem("ret_weighted"), 1)
                        dve.wait_ge(sem("exp_done"), n + 1)
                        link(dve.tensor_tensor(st[:, 4:6], st[:, 4:6], st[:, 6:8], ALU.add))
                        normalise(i, (T, T))
                    if 3 <= i < 11 and i % 2 == 1:
                        p = (i - 3) // 2
                        dve.wait_ge(sem("values_done"), HEADS * (l + 1) + 2 * p + 2)
                        dve.tensor_copy(Z[:, (QA + p) * T:(QA + p + 1) * T], ps(7, T, c0=(p % 2) * T))\
                            .then_inc(sem("pair_copied"), 1)
                dve.wait_ge(sem("ret_copied"), 4 * (l + 1))
                x_in()
                sums()
                for b in range(4):
                    o = H[:, 2 * b:2 * b + 2, :]
                    i = dve.scalar_tensor_tensor(out=o, in0=ps2(4 + b), scalar=-1.0 / HD, in1=o, op0=ALU.mult, op1=ALU.add)
                link(i)
                dve.tensor_tensor(SQV, H[:, :, :], H[:, :, :], ALU.mult).then_inc(sem("norm_in"), 1)

                def gated(lin, g0, js):
                    for j in js:
                        b = linear_ready(lin, j // 2, j % 2)
                        o = z(g0 + 2 * j, g0 + 2 * j + 2)
                        dve.tensor_tensor(o, ps2(b), o, ALU.mult).then_inc(sem("evac_dve"), 1)

                lin = lins[f"wo_attn{l}"]
                gated(lin, G2A, (0, 1))
                sums()
                reciprocal_root([(SQV[:, 2 * b:2 * b + 2, :], ps2(4 + b)) for b in range(4)], HD, KT * T)
                gated(lin, G2A, (2, 3))
                link(dve.tensor_tensor(H[:, :, :], H[:, :, :], SQV, ALU.mult))
                link(dve.tensor_tensor(H[:, :, :], H[:, :, :], z(GF, GF + 8), ALU.mult))
                dve.tensor_tensor(z(QR, QR + 4), H[:, 0:4, :], H[:, 4:8, :], ALU.add).then_inc(sem("ret_out"), 1)
                lin = lins[f"wo_ret{l}"]
                gated(lin, G2R, range(4))
                dve.wait_ge(sem("evac_dve"), job_evac[lin.job0 + 3][1])
                dve.tensor_tensor(z(G2A, G2A + 8), z(G2A, G2A + 8), z(G2R, G2R + 8), ALU.add).then_inc(sem("mix_ready"), 1)
                residual(lins[f"w_out{l}"], 0)
                x_in()
                layer_norm(X[:, :, :], vcols(V_LN1G, l), vcols(V_LN1B, l), "x2_ready")

            mixer2(0)
            for s in range(11):
                b = linear_ready(lins["ffn3"], s)
                o = z(2 * s, 2 * s + 2)
                dve.tensor_tensor(o, ps2(b), o, ALU.mult).then_inc(sem("evac_dve"), 1)
            dve.wait_ge(sem("lin_done"), lins["ffn2"].group0 + 11)
            for b in (2, 3, 0, 1):
                o = X[:, 2 * b:2 * b + 2, :]
                i = dve.scalar_tensor_tensor(out=o, in0=o, scalar=ALPHA, in1=ps2(b), op0=ALU.mult, op1=ALU.add)
                if b in (0, 1):
                    i.then_inc(sem("evac_dve"), 1)
            dve.wait_ge(sem("evac_dve"), job_evac[lins["ffn2"].job0 + 1][1])
            x_in()
            layer_norm(X[:, :, :], vcols(V_LN2G, 0), vcols(V_LN2B, 0), "x2_ready")
            mixer2(1)
            experts(m2, R_BR2)
            link(dve.scalar_tensor_tensor(out=X[:, :, :], in0=X[:, :, :], scalar=ALPHA, in1=Y, op0=ALU.mult, op1=ALU.add))
            x_in()
            layer_norm(X[:, :, :], vcols(V_LN2G, 1), vcols(V_LN2B, 1), "x2_ready")


INPUTS = ["x", "c", "w_ada", "b_ada", "norm1_g", "w_in", "b_forget", "conv_w", "conv_b", "conv_ln_g", "conv_ln_b",
          "w_conv_out", "w_attn_out", "w_out", "norm2_g", "w_router", "b_router", "w_exp_in", "b_exp_in", "w_exp_out",
          "b_exp_out", "final_g", "ln_emb_g_2", "ln_emb_b_2", "w_in_2", "b_gate_2", "sink_logits_2", "decay_fwd_2",
          "decay_bwd_2", "w_o_attn_2", "w_o_ret_2", "w_out_2", "ln1_g_2", "ln1_b_2", "ffn_w1_2", "ffn_w3_2",
          "ffn_w2_2", "router_w_2", "router_b_2", "moe_w1_2", "moe_w3_2", "moe_w2_2", "ln2_g_2", "ln2_b_2"]


def kernel(**inputs):
    import numpy as _np
    import concourse.bacc as _bacc
    from concourse import mybir as _mybir
    from concourse.bass_utils import run_bass_kernel_spmd as _run

    nc = _bacc.Bacc("TRN2", target_bir_lowering=False, num_devices=1)
    arrays, aps = {}, {}
    for name in INPUTS:
        a = _np.ascontiguousarray(inputs[name])
        arrays[f"in_{name}"] = a
        aps[name] = nc.dram_tensor(f"in_{name}", a.shape, _mybir.dt.from_np(a.dtype), kind="ExternalInput").ap()
    out = nc.dram_tensor("out_0", (1, T, D), _mybir.dt.float32, kind="ExternalOutput").ap()
    build_two_blocks(nc, aps, out)
    r = _run(nc, [arrays], core_ids=[0])
    return r.results[0]["out_0"]
```

```python
from contextlib import ExitStack

import numpy as np
import concourse.bass as bass
from concourse import mybir

F32 = mybir.dt.float32
F32R = mybir.dt.float32r
I32 = mybir.dt.int32
ALU = mybir.AluOpType
ACT = mybir.ActivationFunctionType
AX = mybir.AxisListType.X

P = 128
T = 256
D = 1024
KT = D // P
CW = 512
TAPS = 31
HEADS = 8
HD = 64
CHUNK = 128
HALF = 64
EPS = 1e-5
NEG = -1e30
FAR = 1e34
ALPHA = (2 * 2) ** 0.25
RK = 32
RSCALE = RK ** -0.5
QSCALE = HD ** -0.5
RAW_N, SPLIT_N = 6, 4
RING = 15
RING2 = 5
SLOT = 2048
SLOPES = [2.0 ** -(h + 1) for h in range(HEADS)]

V_C, V_BADA, V_N1G, V_N2G, V_FG, V_CB, V_CLG, V_CLB, V_EG, V_EB = 0, 8, 56, 64, 72, 80, 84, 88, 92, 100
V_LN1G, V_LN1B, V_LN2G, V_LN2B, V_BG = 128, 144, 160, 176, 192
V_CONVW, V_B1 = 256, 384
R_SINK, R_DECAY, R_BR1, R_BR2, R_N = 0, 16, 48, 80, 88


class Linear:

    def __init__(self, name, slots, jobs_per_slot, evac, k_major=0):
        self.name, self.slots, self.per, self.evac, self.k_major = name, slots, jobs_per_slot, evac, k_major
        self.is_ada = name.startswith("ada")
        self.split = name.rstrip("01") in ("qa", "kva", "ret", "gg") or name in ("ffn1", "ffn3")


def plan():
    order = [Linear("ada0", 8, 1, "dve", 1), Linear("uqkv_a", 4, 1, "act"),
             Linear("ada1", 8, 1, "dve", 1), Linear("uqkv_b", 6, 1, "act"), Linear("forget", 0, 1, "act"),
             Linear("ada2", 8, 1, "dve", 1), Linear("gates", 8, 1, "act"),
             Linear("conv_out", 2, 2, "dve"), Linear("attn_out", 2, 2, "dve"),
             Linear("w_out", 4, 1, "dve")]
    for l in range(2):
        order += [Linear(f"qa{l}", 2, 1, "act"), Linear(f"kva{l}", 1, 2, "act"),
                  Linear(f"ret{l}", 4, 1, "act"), Linear(f"gg{l}", 12, 1, "act"),
                  Linear(f"wo_attn{l}", 2, 2, "dve"), Linear(f"wo_ret{l}", 2, 2, "dve"),
                  Linear(f"w_out{l}", 4, 1, "dve")]
        if l == 0:
            order += [Linear("ffn1", 11, 1, "act"), Linear("ffn3", 11, 1, "dve"),
                      Linear("ffn2", 11, 1, "dve", 2)]
    group = job = 0
    evacs = {"act": 0, "dve": 0}
    lins, job_evac = {}, []
    for lin in order:
        jobs = lin.k_major or max(1, lin.slots) * lin.per
        groups = 1 if lin.is_ada else lin.slots if lin.k_major else max(1, lin.slots) * lin.per
        lin.group0, lin.job0, lin.jobs, lin.groups, lin.at = group, job, jobs, groups, []
        group, job = group + groups, job + jobs
        for _ in range(jobs):
            evacs[lin.evac] += 1
            job_evac.append((lin.evac, evacs[lin.evac]))
        lins[lin.name] = lin
    stream = [("ada0", s) for s in range(8)]
    for name, n, ada in (("uqkv_a", 4, "ada1"), ("uqkv_b", 6, "ada2")):
        for s in range(n):
            stream.append((name, s))
            stream += [(ada, k) for k in range(min(2 * s, 8), min(2 * s + 2, 8))]
    done = {name for name, _ in stream}
    for lin in order:
        if lin.name == "qa0":
            n_block1 = len(stream)
        if lin.name not in done:
            stream += [(lin.name, s) for s in range(lin.slots)]
    free_at, split_slots = [], []
    for n, (name, s) in enumerate(stream):
        lin = lins[name]
        assert len(lin.at) == s
        lin.at.append(n)
        if lin.split:
            split_slots.append((n, lin.group0 + (s + 1) * lin.per))
            free_at.append(("dense_lo", len(split_slots)))
        elif lin.is_ada:
            free_at.append(("ada_used", 8 * int(name[-1]) + s + 1))
        else:
            free_at.append(("lin_done", lin.group0 + (s + 1) * (1 if lin.k_major else lin.per)))
    return lins, job_evac, stream, free_at, n_block1, split_slots


class Chain:

    def __init__(self, eng, sem):
        self.eng, self.sem, self.base, self.n = eng, sem, 0, 0

    def link(self, ins):
        self.n += 1
        ins.then_inc(self.sem, 1)
        self.eng.wait_ge(self.sem, self.base + self.n)

    def enter(self, base):
        self.base, self.n = base, 0


def build_two_blocks(nc, A, out):
    lins, job_evac, stream, free_at, N_A, split_slots = plan()
    N_SLOTS = len(stream)
    ctx = ExitStack()
    with ctx:
        sems = {}

        def sem(name):
            if name not in sems:
                sems[name] = ctx.enter_context(nc.semaphore(name))
            return sems[name]

        def sb(name, shape, dt=F32):
            return ctx.enter_context(nc.sbuf_tensor(name, shape, dt))

        w_bytes = (RING + 1) * SLOT + 1024
        with nc.sbuf_tensor("W", [P, w_bytes], F32) as W:
            pass
        with nc.sbuf_tensor("RAW_D", [P, RING2 * SLOT], F32), \
                nc.sbuf_tensor("WHI_D", [P, SPLIT_N, SLOT], F32R) as WHI_D, \
                nc.sbuf_tensor("WLO_D", [P, SPLIT_N, SLOT], F32R) as WLO_D, \
                nc.sbuf_tensor("XHI", [P, KT, T], F32R) as XHI, nc.sbuf_tensor("XLO", [P, KT, T], F32R) as XLO:
            pass
        RAW = sb("RAW", [P, RAW_N, SLOT])
        WHI = sb("WHI", [P, SPLIT_N, SLOT], F32R)
        WLO = sb("WLO", [P, SPLIT_N, SLOT], F32R)
        with nc.sbuf_tensor("X2_1", [P, KT, 2 * HALF], F32R) as X2_1, nc.sbuf_tensor("HM2_1", [P, KT, 2 * HALF], F32R) as HM2_1:
            pass
        X2_2 = sb("X2_2", [P, KT, 2 * CHUNK], F32R)
        HM2_2 = sb("HM2_2", [P, 11, 2 * CHUNK], F32R)
        sb("W_REST", [P, w_bytes - (RAW_N + 2 * SPLIT_N) * SLOT - (KT + 11) * 2 * CHUNK])
        Z = sb("Z", [P, 38 * T])
        X = sb("X", [P, KT, T])
        H = sb("H", [P, KT, T])
        SQ = sb("SQ", [P, KT * T])
        VEC = sb("VEC", [P, 7 * P])
        IDENT = sb("IDENT", [P, P])
        ONES = sb("ONES", [P, P])
        BLK = sb("BLK", [P, P])
        HEADROW = sb("HEADROW", [P, KT, 16])
        BEFORE = sb("BEFORE", [P, P])
        DIST = sb("DIST", [P, 2, T])
        LAGS = sb("LAGS", [P, 4, P])
        MOD = sb("MOD", [P, 48])
        ROWS = sb("ROWS", [1, R_N])
        ROWB = sb("ROWB", [P, R_N])
        WR1 = sb("WR1", [P, KT, 32])
        WR2 = sb("WR2", [P, KT, 8])
        LG = sb("LG", [P, 32])
        GS = sb("GS", [P, 3 * KT])
        CSIL = sb("CSIL", [P, KT])
        BFG = sb("BFG", [8, 1])
        IOTAP = sb("IOTAP", [P, 1])
        ST = sb("ST", [P, 2, 8])
        PS = ctx.enter_context(nc.psum_tensor("PS", [P, 8, 512], F32))

        SCR = W[:, RING * SLOT:RING * SLOT + 3072]

        def z(a, b):
            return Z[:, a * T:b * T].rearrange("p (k t) -> p k t", t=T)

        def slot(n):
            r = n % RING if n < N_A else (n - N_A) % RING2
            return W[:, r * SLOT:(r + 1) * SLOT], r

        XT = H[:, :, :].rearrange("p k t -> p (k t)").rearrange("p (a d) -> p a d", a=2)
        VROWS = SQ[:, 0:7 * P].rearrange("p (a c) -> p a c", c=P)
        CONV_IN = SCR[:, 0:4 * 286].rearrange("p (j t) -> p j t", t=286)
        SEL = SCR[:, 1144:2168].rearrange("p (h m) -> p h m", m=P)
        CAUSAL = SCR[:, 2168:2296]
        NEGF = SCR[:, 2296:2552]
        WF = SCR[:, 2552:2616].rearrange("p (k n) -> p k n", n=8)
        PROB = SQ[:, 0:1024].rearrange("p (b a k) -> p b a k", b=2, a=2)
        PROBT = SQ[:, 1024:2048].rearrange("p (b k) -> p b k", b=2)
        DEC = SCR[:, 0:1024].rearrange("p (b f) -> p b f", b=2)
        RA = SCR[:, 1024:3072].rearrange("p (b d s t) -> p b d s t", b=2, d=2, s=2)
        SPREAD = SCR[0:16, 0:1024].rearrange("p (k c) -> p k c", k=KT)
        UV, UG, Q1, K1, GC, GA = 0, 4, 8, 12, 20, 28
        VT1 = Z[:, 16 * T:20 * T].rearrange("p (a n) -> p a n", a=2)
        ADA = Z[:, GA * T:(GA + 8) * T]
        QA, KA, QR, KR, GF, GB, G2A, G2R = 0, 4, 5, 7, 14, 18, 22, 30
        VR = Z[:, 9 * T:13 * T].rearrange("p (a n) -> p a n", a=2)
        VA = Z[:, 13 * T:14 * T].rearrange("p (a n) -> p a n", a=2)

        at = [0]

        def zs(n):
            at[0] += n
            return Z[:, at[0] - n:at[0]]

        HT = zs(2048).rearrange("p (a d) -> p a d", a=2)
        Y = zs(2048).rearrange("p (k t) -> p k t", t=T)
        XG = zs(1024).rearrange("p (k c) -> p k c", c=CHUNK)
        HM = zs(11 * CHUNK).rearrange("p (k c) -> p k c", c=CHUNK)
        PART = zs(2048)
        GT = zs(T)
        PICK = zs(2 * CHUNK).rearrange("p (a c) -> p a c", c=CHUNK)
        PICKG = zs(2 * CHUNK).rearrange("p (a c) -> p a c", c=CHUNK)
        IOTA = zs(T)
        HS = PART
        HF = HM.rearrange("p k c -> p (k c)")
        GPART, UPART = XG[:, 0:4, :].rearrange("p k (a c) -> p (k a) c", a=2), XG[:, 4:8, :].rearrange("p k (a c) -> p (k a) c", a=2)
        SIG = HM[:, 0:4, :].rearrange("p k (a c) -> p (k a) c", a=2)
        STACK = HM[:, 4, 0:HALF]
        YS = SQ[:, 0:1024]
        COUNT, LAST = 2 * P, 2 * P + 1
        TAB = SQ[0:1, 1024:1024 + 2 * P + 2].bitcast(I32)
        at = [1024 + 2 * P + 2]

        def qs(n):
            at[0] += n
            return SQ[:, at[0] - n:at[0]]

        B1C = qs(16)
        LOG = qs(80).rearrange("p (a e) -> p a e", e=40)
        LOGR = qs(80).rearrange("p (a e) -> p a e", e=40)
        MASK = qs(64).rearrange("p (a e) -> p a e", e=32)
        GATE = qs(64).rearrange("p (a e) -> p a e", e=32)
        RANK = qs(64).rearrange("p (a e) -> p a e", e=32)
        TOP8 = qs(16).rearrange("p (a e) -> p a e", e=8)
        NTOP, GSUM = qs(2), qs(2)
        NCH, CUM, LE, LEN_, ONE32 = qs(32), qs(32), qs(32), qs(32), qs(32)
        TCOL, FREE = qs(2), qs(1)
        BOUT = SCR[0:32, 0:1024]

        def bc(ap, n):
            return ap.unsqueeze(1).broadcast_to([P, n, ap.shape[1]])

        def bl(ap, n):
            return ap.unsqueeze(2).broadcast_to([P, ap.shape[1], n])

        def ps(b, n=512, p0=0, p1=P, c0=0):
            return PS[p0:p1, b, c0:c0 + n]

        def ps2(b):
            return PS[:, b, :].rearrange("p (a t) -> p a t", a=2)

        w_in, w_in2 = A["w_in"], A["w_in_2"]

        def cols(w, c0, n, buf, k=KT):
            return [(buf[:, 0:k * n].rearrange("p (k n) -> p k n", k=k),
                     w[:, c0:c0 + n].rearrange("(k p) n -> p k n", p=P))]

        def rows(w, k0, nk, c0, n, buf):
            return [(buf[:, 0:nk * n].rearrange("p (k n) -> p k n", k=nk),
                     w[k0 * P:(k0 + nk) * P, c0:c0 + n].rearrange("(k p) n -> p k n", p=P))]

        def transfers(name, s, buf):
            l = int(name[-1]) if name[-1].isdigit() else 0
            if name.startswith("ada"):
                return rows(A["w_ada"][0], s, 1, 2048 * l, 2048, buf)
            if name.startswith("uqkv"):
                return cols(w_in[0], 256 * (s + (4 if name == "uqkv_b" else 0)), 256, buf)
            if name == "gates":
                return cols(w_in[0], 5 * CW + HEADS + 256 * s, 256, buf)
            if name in ("conv_out", "attn_out"):
                return cols(A["w_" + name][0], 512 * s, 512, buf, 4)
            if name == "w_out":
                return cols(A["w_out"][0], 256 * s, 256, buf)
            if name.startswith("qa"):
                src = w_in2[l][:, 0:512].rearrange("(k p) (g c) -> p k g c", p=P, g=2)
                dst = buf.rearrange("p (k g c) -> p k g c", k=KT, g=4)
                return [(dst[:, :, 2 * i + g, :], src[:, :, g, (2 * s + i) * HD:(2 * s + i + 1) * HD])
                        for i in range(2) for g in range(2)]
            if name.startswith("kva"):
                return cols(w_in2[l], 512, 256, buf)
            if name.startswith("ret"):
                return cols(w_in2[l], 768 + 256 * s, 256, buf)
            if name.startswith("gg"):
                return cols(w_in2[l], 1792 + 256 * s, 256, buf)
            if name.startswith("wo_attn"):
                src = A["w_o_attn_2"][l][:, 512 * s:512 * (s + 1)].rearrange("(g i r) n -> g r i n", g=2, i=4)
                return [(buf[64 * g:64 * (g + 1), :].rearrange("p (k n) -> p k n", k=4), src[g]) for g in range(2)]
            if name.startswith("wo_ret"):
                return cols(A["w_o_ret_2"][l], 512 * s, 512, buf, 4)
            if name.startswith("w_out"):
                return cols(A["w_out_2"][l], 256 * s, 256, buf)
            if name == "ffn1":
                return cols(A["ffn_w1_2"][0], 256 * s, 256, buf)
            if name == "ffn3":
                return cols(A["ffn_w3_2"][0], 256 * s, 256, buf)
            return rows(A["ffn_w2_2"][0], 2 * s, 2, 0, 1024, buf)

        arrive, total = [], [0] * RING
        for n, (name, s) in enumerate(stream):
            buf, r = slot(n)
            total[r] += 16 * len(transfers(name, s, buf))
            arrive.append((r, total[r]))

        class Moe:
            pass

        m1, m2 = Moe(), Moe()
        m1.tag, m1.n, m1.top, m1.ht, m1.slots, m1.groups, m1.first, m1.x, m1.h = "m1", 32, 4, 8, HALF, 12, 8, X2_1, HM2_1
        m2.tag, m2.n, m2.top, m2.ht, m2.slots, m2.groups, m2.first, m2.x, m2.h = "m2", 8, 2, 11, CHUNK, 24, 16, X2_2, HM2_2

        def msem(m, name):
            return sem(f"{m.tag}_{name}")

        def group_kts(m, s):
            if s < m.first:
                return [s] if m is m1 else [s // 2]
            s -= m.first
            return [2 * s, 2 * s + 1] if m is m1 or s < 3 else [s + 3]

        def group_width(m, s):
            return len(group_kts(m, s)) * D if s >= m.first else 2048 if m is m1 else 1408

        def wait_split(eng, m, g, s):
            for name in ("lo_dve", "lo_pool"):
                eng.wait_ge(msem(m, name), g * m.groups + (s + 1))
                if eng is nc.sync:
                    eng.nop(nofuse=True)

        def split_hi(eng, m, g, s, first=False):
            eng.wait_ge(msem(m, f"raw{s % RAW_N}"), g * (16 * (m.groups // RAW_N)) + 16 * (s // RAW_N + 1))
            if not first:
                eng.wait_ge(msem(m, "group_done"), g * m.groups + (s + 1 - SPLIT_N))
            n = group_width(m, s)
            eng.activation(WHI[:, s % SPLIT_N, 0:n], RAW[:, s % RAW_N, 0:n], ACT.Copy).then_inc(msem(m, "hi"), 1)

        def split_lo(eng, m, g, s, first=False):
            eng.wait_ge(msem(m, "hi"), g * m.groups + (s + 1))
            if not first:
                eng.wait_ge(msem(m, "group_done"), g * m.groups + (s + 1 - SPLIT_N))
            n = group_width(m, s)
            c0, c1, name = (0, n * 11 // 16, "lo_dve") if eng is nc.vector else (n * 11 // 16, n, "lo_pool")
            eng.tensor_tensor(WLO[:, s % SPLIT_N, c0:c1], RAW[:, s % RAW_N, c0:c1], WHI[:, s % SPLIT_N, c0:c1].bitcast(F32),
                              ALU.subtract).then_inc(msem(m, name), 1)

        def split_dense(eng, q):
            n, _ = split_slots[q]
            raw, r = slot(n)
            if q >= SPLIT_N:
                eng.wait_ge(sem("lin_done"), split_slots[q - SPLIT_N][1])
            hi, lo = WHI_D[:, q % SPLIT_N, :], WLO_D[:, q % SPLIT_N, :]
            if eng is nc.scalar:
                eng.wait_ge(sem(f"arrived{r}"), arrive[n][1])
                eng.activation(hi, raw, ACT.Copy).then_inc(sem("dense_hi"), 1)
            else:
                eng.wait_ge(sem("dense_hi"), q + 1)
                eng.tensor_tensor(lo, raw, hi.bitcast(F32), ALU.subtract).then_inc(sem("dense_lo"), 1)

        def group_src(m, s, e):
            ks = group_kts(m, s)
            if s >= m.first:
                w, n = A["w_exp_out"] if m is m1 else A["moe_w2_2"], D
            else:
                w, n = (A["w_exp_in"], 2048) if m is m1 else (A["moe_w3_2"] if s % 2 else A["moe_w1_2"], 1408)
            src = w[0, bass.ds(e, 1), ks[0] * P:(ks[-1] + 1) * P, :].rearrange("a (k p) n -> p (a k) n", p=P)
            return RAW[:, s % RAW_N, 0:len(ks) * n].rearrange("p (k n) -> p k n", k=len(ks)), src

        block = ctx.enter_context(nc.Block())

        @block.sync
        def _(sp):
            def wait_free(n):
                name, count = free_at[n]
                sp.wait_ge(sem(name), count)

            def dense(n0, n1):
                for n in range(n0, n1):
                    name, s = stream[n]
                    buf, r = slot(n)
                    if n == 2:
                        sp.wait_ge(sem("ld_vec"), 16 * 17)
                    ring = RING if n0 == 0 else RING2
                    if n - n0 >= ring:
                        wait_free(n - ring)
                    for dst, src in transfers(name, s, buf):
                        sp.dma_start(dst, src).then_inc(sem(f"arrived{r}"), 16)

            def experts(m, n0, n1):
                def group(s, e):
                    dst, src = group_src(m, s, e)
                    sp.dma_start(dst, src).then_inc(msem(m, f"raw{s % RAW_N}"), 16)

                for s in range(m.groups):
                    if m is m2 and s == RING2:
                        sp.wait_ge(sem("lin_done"), split_slots[-1][1])
                    elif s < RAW_N:
                        wait_free(max(k for k in range(n0, n1) if slot(k)[1] == s))
                    else:
                        wait_split(sp, m, 0, s - RAW_N)
                    group(s, 0)
                sp.wait_ge(msem(m, "tables"), 1)
                last = sp.value_load(TAB[0:1, LAST:LAST + 1], min_val=0, max_val=47)
                with sp.Fori(0, last) as before:
                    e = sp.value_load(TAB[0:1, bass.ds(before + 1, 1)], min_val=0, max_val=m.n - 1)
                    for s in range(m.groups):
                        wait_split(sp, m, before + (s >= RAW_N), (s - RAW_N) % m.groups)
                        group(s, e)
                for s in range(SPLIT_N):
                    wait_split(sp, m, last, s - RAW_N + m.groups)
                    group(s, m.n - 1)

            dense(0, N_A)
            experts(m1, 0, N_A)
            sp.wait_ge(msem(m1, "bytes_free"), 1)
            dense(N_A, N_SLOTS)
            experts(m2, N_A, N_SLOTS)
            sp.wait_ge(sem("out_staged"), 4)
            sp.dma_start(out[0].rearrange("(a p) d -> p a d", p=P), XT).then_inc(sem("stored"), 16)
            sp.wait_ge(sem("stored"), 16)

        @block.gpsimd
        def _(pool):
            ch = Chain(pool, sem("pool_step"))
            ch.link(pool.memset(IDENT[:, :], 0.0))
            ch.link(pool.affine_select(out=IDENT[:, :], in_=IDENT[:, :], compare_op=ALU.not_equal, fill=1.0,
                                       base=0, pattern=[[-1, P]], channel_multiplier=1))
            pool.memset(ONES[:, :], 1.0).then_inc(sem("ident_ready"), 1)
            ch.link(pool.memset(BLK[:, :], 0.0))
            ch.link(pool.memset(BLK[0:64, 0:64], 1.0))
            ch.link(pool.memset(BLK[64:128, 64:128], 1.0))
            ch.link(pool.memset(BEFORE[:, :], 1.0))
            ch.link(pool.affine_select(out=BEFORE[:, :], in_=BEFORE[:, :], compare_op=ALU.is_gt, fill=0.0,
                                       base=0, pattern=[[1, P]], channel_multiplier=-1))
            ch.link(pool.memset(HEADROW[:, :, :], 0.0))
            for half in range(2):
                rows_ = HEADROW[64 * half:64 * half + 64, :, :]
                ch.link(pool.affine_select(out=rows_, in_=rows_, compare_op=ALU.not_equal, fill=1.0,
                                           base=-half, pattern=[[-2, KT], [1, 16]], channel_multiplier=0))
            ch.link(pool.memset(SEL, 0.0))
            ch.link(pool.affine_select(out=SEL, in_=SEL, compare_op=ALU.not_equal, fill=1.0,
                                       base=0, pattern=[[-1, HEADS], [0, P]], channel_multiplier=1))
            ch.link(pool.memset(CAUSAL, 0.0))
            ch.link(pool.affine_select(out=CAUSAL, in_=CAUSAL, compare_op=ALU.is_ge, fill=NEG,
                                       base=0, pattern=[[-1, P]], channel_multiplier=1))
            ch.link(pool.memset(NEGF, 0.0))
            ch.link(pool.memset(CONV_IN[:, :, 0:TAPS - 1], 0.0))
            ch.link(pool.iota(IOTAP[:, :], pattern=[[0, 1]], base=0, channel_multiplier=1,
                              allow_small_or_imprecise_dtypes=True))
            for i, (base, step) in enumerate(((0, 1), (P, 1), (P, -1), (0, -1))):
                ch.link(pool.iota(LAGS[:, i, :], pattern=[[step, P]], base=base, channel_multiplier=-step,
                                  allow_small_or_imprecise_dtypes=True))
            ch.link(pool.iota(DIST[:, :, :], pattern=[[P, 2], [-1, T]], base=0, channel_multiplier=1,
                              allow_small_or_imprecise_dtypes=True))
            pool.wait_ge(sem("dist_abs"), 1)
            ch.link(pool.affine_select(out=DIST[:, :, :], in_=DIST[:, :, :], compare_op=ALU.is_ge, fill=FAR,
                                       base=P, pattern=[[-P, 2], [1, T]], channel_multiplier=-1))
            pool.affine_select(out=DIST[:, :, :], in_=DIST[:, :, :], compare_op=ALU.is_ge, fill=FAR,
                               base=P, pattern=[[P, 2], [-1, T]], channel_multiplier=1)\
                .then_inc(sem("pool_tables"), 1)

            def mixer2(l):
                q0 = 41 * l
                for q in range(q0, q0 + 11):
                    split_dense(pool, q)
                for h in range(HEADS):
                    n = l * HEADS + h
                    pool.wait_ge(sem("decay_exp"), n + 1)
                    dec = DEC[:, h % 2, :]
                    ch.link(pool.affine_select(out=dec[:, 0:P], in_=dec[:, 0:P], compare_op=ALU.is_ge, fill=0.0,
                                               base=0, pattern=[[1, P]], channel_multiplier=-1))
                    pool.affine_select(out=dec[:, 3 * P:], in_=dec[:, 3 * P:], compare_op=ALU.is_gt, fill=0.0,
                                       base=0, pattern=[[-1, P]], channel_multiplier=1)\
                        .then_inc(sem("decay_masked"), 1)
                    split_dense(pool, q0 + 11 + h)
                pool.wait_ge(sem("ret_weighted"), HEADS * (l + 1))
                ch.link(pool.memset(SPREAD, 0.0))
                spread = SPREAD.rearrange("p k (g c) -> p k g c", g=2)
                for half in range(2):
                    i = pool.affine_select(out=spread[:, :, half, :], in_=spread[:, :, half, :], compare_op=ALU.not_equal,
                                           fill=1.0, base=-half, pattern=[[-2, KT], [0, HD]], channel_multiplier=1)
                i.then_inc(sem("pool_tables"), 1)

            def slot_iota(m):
                pool.wait_ge(sem("moe_scratch_free"), 1 if m is m1 else 2)
                pool.iota(IOTA, pattern=[[1, T]], base=0, channel_multiplier=0,
                          allow_small_or_imprecise_dtypes=True).then_inc(msem(m, "iota"), 1)

            def remainders(m):
                for s in range(SPLIT_N):
                    split_lo(pool, m, 0, s, first=True)
                pool.wait_ge(msem(m, "tables"), 1)
                count = pool.value_load(TAB[0:1, COUNT:COUNT + 1], min_val=m.n, max_val=48)
                with pool.Fori(0, count) as g:
                    for s in range(SPLIT_N, m.groups):
                        split_lo(pool, m, g, s)
                    for s in range(SPLIT_N):
                        split_lo(pool, m, g + 1, s)

            slot_iota(m1)
            remainders(m1)
            mixer2(0)
            for q in range(19, 41):
                split_dense(pool, q)
            mixer2(1)
            slot_iota(m2)
            remainders(m2)

        @block.tensor
        def _(pe):
            norm = [0]

            def bank_free(job):
                if job >= 2:
                    e, c = job_evac[job - 2]
                    pe.wait_ge(sem("evac_" + e), c)
                else:
                    pe.wait_ge(sem("init_act"), 1)

            def weights(n):
                r, c = arrive[n]
                pe.wait_ge(sem(f"arrived{r}"), c)
                return slot(n)[0]

            PASSES = ((WHI_D, XHI), (WLO_D, XHI), (WHI_D, XLO))

            def split_ready(lin, s):
                q = next(q for q, (n, _) in enumerate(split_slots) if n == lin.at[s])
                pe.wait_ge(sem("dense_lo"), q + 1)
                return q

            def stream_lo(lin):
                pe.wait_ge(sem("stream_lo"), 1 + ("qa0", "ffn1", "qa1").index(lin.name))

            def feature_job(lin, s, x, nk=KT, part=0, width=256):
                job = lin.job0 + s * lin.per + part
                if lin.split:
                    q = split_ready(lin, s)
                    bank_free(job)
                    for j in range(width // P):
                        c = part * width + j * P
                        for i, (w, xp) in enumerate(PASSES):
                            if lin.name in ("qa0", "ffn1", "qa1") and s == j == 0 and xp is XLO:
                                stream_lo(lin)
                            w = w[:, q % SPLIT_N, :].rearrange("p (k n) -> p k n", k=KT)
                            for k in range(KT):
                                mm = pe.matmul(ps(job % 2, T, c0=j * T), w[:, k, c:c + P], xp[:, k, :],
                                               start=(i == k == 0), stop=(i == 2 and k == KT - 1))
                    mm.then_inc(sem("lin_done"), 1)
                    return
                w = weights(lin.at[s]).rearrange("p (k n) -> p k n", k=nk)
                bank_free(job)
                for j in range(width // P):
                    for k in range(nk):
                        c = part * width + j * P
                        mm = pe.matmul(ps(job % 2, T, c0=j * T), w[:, k, c:c + P], x[:, k, :],
                                       start=(k == 0), stop=(k == nk - 1))
                mm.then_inc(sem("lin_done"), 1)

            def token_job(lin, s, x, c0, width, part=0):
                job = lin.job0 + s * lin.per + part
                if lin.split:
                    q = split_ready(lin, s)
                    bank_free(job)
                    for a in range(2):
                        for i, (w, xp) in enumerate(PASSES):
                            w = w[:, q % SPLIT_N, :].rearrange("p (k n) -> p k n", k=KT)
                            for k in range(KT):
                                mm = pe.matmul(ps(job % 2, width, c0=a * width), xp[:, k, a * P:(a + 1) * P],
                                               w[:, k, c0:c0 + width], start=(i == k == 0), stop=(i == 2 and k == KT - 1))
                    mm.then_inc(sem("lin_done"), 1)
                    return
                w = weights(lin.at[s]).rearrange("p (k n) -> p k n", k=KT)
                bank_free(job)
                for a in range(2):
                    for k in range(KT):
                        mm = pe.matmul(ps(job % 2, width, c0=a * width), x[:, k, a * P:(a + 1) * P],
                                       w[:, k, c0:c0 + width], start=(k == 0), stop=(k == KT - 1))
                mm.then_inc(sem("lin_done"), 1)

            def ada(l):
                lin = lins[f"ada{l}"]
                pe.wait_ge(sem("ada_used"), 8 * (l + 1))
                bank_free(lin.job0)
                for j in range(16):
                    mm = pe.matmul(PS[:, lin.job0 % 2, j:j + 1], ADA[:, j * P:(j + 1) * P], ONES[:, 0:1], start=True, stop=True)
                mm.then_inc(sem("lin_done"), 1)

            def norm_sum(src, nk, col=0):
                norm[0] += 1
                pe.wait_ge(sem("norm_in"), norm[0])
                for k in range(nk):
                    mm = pe.matmul(ps(4, T, c0=col), ONES[:, :], src[:, k, :], start=(k == 0), stop=(k == nk - 1))
                mm.then_inc(sem("norm_sum"), 1)

            SQV = SQ[:, :].rearrange("p (k t) -> p k t", t=T)

            def rms():
                norm_sum(SQV, KT)

            def layer_norm(src, nk=KT):
                norm_sum(src, nk)
                norm_sum(SQV, nk, T)

            pe.wait_ge(sem("ident_ready"), 1)
            pe.wait_ge(sem("ld_vec"), 16 * 17)
            for i, r in enumerate([108, 96, 124] + [P] * 4):
                tr = pe.transpose(PS[:, i // 4, (i % 4) * P:(i % 4) * P + r], VROWS[0:r, i, :], IDENT[0:r, 0:r])
            tr.then_inc(sem("vec_turned"), 1)
            pe.wait_ge(sem("ld_rows"), 16 * 5)
            pe.matmul(ps(3, R_N), ONES[0:1, :], ROWS[0:1, :], start=True, stop=True).then_inc(sem("rows_spread"), 1)
            pe.wait_ge(sem("ld_x"), 16)
            for k in range(KT):
                for a in range(2):
                    tr = pe.transpose(PS[:, 4 + k // 2, (k % 2) * T + a * P:(k % 2) * T + (a + 1) * P],
                                      XT[:, a, k * P:(k + 1) * P], IDENT[:, :])
            tr.then_inc(sem("x_turned"), 1)

            ada(0)
            pe.wait_ge(sem("x_ready"), 1)
            rms()
            pe.wait_ge(sem("h_ready"), 1)
            for s in range(4):
                feature_job(lins["uqkv_a"], s, H)
            ada(1)
            for s in range(4):
                feature_job(lins["uqkv_b"], s, H)
            for s in range(4, 6):
                token_job(lins["uqkv_b"], s, H, 0, 256)
            job = lins["forget"].job0
            pe.wait_ge(sem("ld_small"), 16 * 4)
            bank_free(job)
            for k in range(KT):
                mm = pe.matmul(PS[0:8, job % 2, 0:T], WF[:, k, :], H[:, k, :], start=(k == 0), stop=(k == KT - 1))
            mm.then_inc(sem("lin_done"), 1)
            ada(2)

            def scores1(h):
                r = (h % 2) * HD
                q, k = Z[r:r + HD, (Q1 + h // 2) * T:(Q1 + h // 2 + 1) * T], Z[r:r + HD, (K1 + h // 2) * T:(K1 + h // 2 + 1) * T]
                b = 4 + h % 2
                if h >= 2:
                    pe.wait_ge(sem("exp_done"), h - 1)
                else:
                    pe.wait_ge(sem("negf_ready"), 1)
                pe.matmul(ps(b, P), q[:, 0:P], k[:, 0:P], start=True, stop=False)
                pe.matmul(ps(b, P), SEL[:, h, :], NEGF[:, 0:P], start=False, stop=False)
                pe.matmul(ps(b, P), IDENT[:, :], CAUSAL, start=False, stop=True)
                pe.matmul(ps(b, T, c0=P), q[:, P:T], k[:, :], start=True, stop=False)
                pe.matmul(ps(b, T, c0=P), SEL[:, h, :], NEGF, start=False, stop=True)
                pe.matmul(ps(b, P, c0=2 * P), IDENT[:, :], CAUSAL, start=False, stop=True,
                          skip_group_check=True).then_inc(sem("scores_ready"), 1)

            def turn_probs(n, h, blocks):
                pe.wait_ge(sem("probs_ready"), n + 1)
                if n >= 1:
                    pe.wait_ge(sem("probs_copied"), n)
                for i, (qa, ka) in enumerate(blocks):
                    tr = pe.transpose(ps(6, P, c0=i * P), PROB[:, n % 2, qa, ka * P:(ka + 1) * P], IDENT[:, :])
                tr.then_inc(sem("probs_turned"), 1)

            def values(n, half, pair, last_half, v, blocks):
                pe.wait_ge(sem("probs_copied"), n + 1)
                if half == 0 and pair >= 1:
                    pe.wait_ge(sem("pair_copied"), pair)
                for i, (ka, q0, wd, c) in enumerate(blocks):
                    mm = pe.matmul(ps(7, wd, HD * half, HD * half + HD, (pair % 2) * T + q0),
                                   v[:, ka, :], PROBT[:, n % 2, c:c + wd], start=(i == 0),
                                   stop=True, skip_group_check=True)
                mm.then_inc(sem("values_done"), 1)

            lin = lins["gates"]
            for i in range(10):
                if i < 8:
                    feature_job(lin, i, H)
                    if i == 0:
                        pe.wait_ge(sem("evac_act"), 10)
                    scores1(i)
                if 1 <= i < 9:
                    turn_probs(i - 1, i - 1, ((0, 0), (1, 0), (1, 1)))
                if i >= 2:
                    h = i - 2
                    values(h, h % 2, h // 2, h % 2, VT1[:, :, h * HD:(h + 1) * HD], ((0, 0, T, 0), (1, P, P, T)))
            layer_norm(z(UV, UV + 4), 4)
            pe.wait_ge(sem("conv_ready"), 1)
            for s in range(2):
                for part in range(2):
                    feature_job(lins["conv_out"], s, z(UV, UV + 4), 4, part)
            pe.wait_ge(sem("pair_copied"), 4)
            for s in range(2):
                for part in range(2):
                    feature_job(lins["attn_out"], s, z(UG, UG + 4), 4, part)
            pe.wait_ge(sem("mix_ready"), 1)
            for s in range(4):
                feature_job(lins["w_out"], s, z(GC, GC + 8))
            rms()
            pe.wait_ge(sem("h_ready"), 2)

            def experts(m, x, wr, hr_name, hr_n):
                E = m.n
                pe.wait_ge(sem("moe_scratch_free"), 1 if m is m1 else 2)
                for a in range(2):
                    for k in range(KT):
                        tr = pe.transpose(ps(4 + 2 * a + k // 4, P, c0=(k % 4) * P), x[:, k, a * P:(a + 1) * P], IDENT[:, :])
                tr.then_inc(msem(m, "x_turned"), 1)
                for a in range(2):
                    for k in range(KT):
                        mm = pe.matmul(ps(0, E, c0=a * E), x[:, k, a * P:(a + 1) * P], wr[:, k, :],
                                       start=(k == 0), stop=(k == KT - 1))
                mm.then_inc(msem(m, "logits"), 1)
                pe.wait_ge(msem(m, "mask"), 1)
                for a in range(2):
                    pe.matmul(ps(1, E), ONES[:, :], MASK[:, a, 0:E], start=(a == 0), stop=(a == 1))
                pe.matmul(ps(1, E, c0=64), BEFORE[:, :], MASK[:, 0, 0:E], start=True, stop=True)
                pe.matmul(ps(1, E, c0=96), ONES[:, :], MASK[:, 0, 0:E], start=True, stop=False)
                pe.matmul(ps(1, E, c0=96), BEFORE[:, :], MASK[:, 1, 0:E], start=False, stop=True)\
                    .then_inc(msem(m, "counts"), 1)
                pe.wait_ge(msem(m, "table_cols"), 1)
                for j in range(2):
                    mm = pe.matmul(ps(2, P, 0, 1, j * P), TCOL[:, j:j + 1], IDENT[:, :], start=True, stop=True)
                mm.then_inc(msem(m, "table_rows"), 1)
                pe.wait_ge(msem(m, "tables"), 1)
                count = pe.value_load(TAB[0:1, COUNT:COUNT + 1], min_val=m.n, max_val=48)

                def gather(g1, last=None):
                    pe.wait_ge(msem(m, "pick"), g1)
                    if last is not None:
                        pe.wait_ge(msem(m, "turned_copied"), last + 1)
                    for k in range(KT):
                        for a in range(2):
                            mm = pe.matmul(ps(6 + k // 4, CHUNK, c0=(k % 4) * CHUNK), HT[:, a, k * P:(k + 1) * P],
                                           PICK[:, a, :], start=(a == 0), stop=(a == 1))
                    mm.then_inc(msem(m, "gathered"), 1)

                def turn(g):
                    pe.wait_ge(msem(m, "pickg"), g + 1)
                    pe.wait_ge(msem(m, "added"), g * 4 + 1)
                    pe.nop(nofuse=True)
                    for a in range(2):
                        tr = pe.transpose(ps(6, P, c0=a * P), PICKG[:, a, :], IDENT[:, :])
                    tr.then_inc(msem(m, "turned"), 1)

                def scatter(g, qs_=range(4)):
                    pe.wait_ge(msem(m, "turned_copied"), g + 1)
                    pe.wait_ge(msem(m, "ys_dve"), g + 1)
                    pe.wait_ge(msem(m, "ys_act"), g + 1)
                    for q in qs_:
                        if q >= 2:
                            pe.wait_ge(msem(m, "added"), g * 4 + q)
                        for j in range(2):
                            k = 2 * q + j
                            mm = pe.matmul(ps(6 + q % 2, T, c0=j * T), YS[:, k * P:(k + 1) * P], GT,
                                           start=True, stop=True)
                        mm.then_inc(msem(m, "scattered"), 1)

                def split_product(g, s):
                    wait_split(pe, m, g, s)
                    if s < m.first:
                        x, b0, width, last_k = m.x, 0 if m is m1 else 3 * (s % 2), group_width(m, s), KT - 1
                    else:
                        x, b0, width, last_k = m.h, 4 if m is m1 else 3, D, m.ht - 1
                    passes = [(0, WHI), (0, WLO)] + ([(CHUNK, WHI)] if m is m2 else [])
                    for i, k in enumerate(group_kts(m, s)):
                        for c0, part in passes:
                            for j in range(0, width, 512):
                                n = min(512, width - j)
                                mm = pe.matmul(ps(b0 + j // 512, n), x[:, k, c0:c0 + CHUNK],
                                               part[:, s % SPLIT_N, i * width + j:i * width + j + n],
                                               start=(k == 0 and c0 == 0 and part is WHI),
                                               stop=(k == last_k and (c0, part) == passes[-1]), skip_group_check=True)
                    mm.then_inc(msem(m, "group_done"), 1)

                def turn_hidden(g):
                    pe.wait_ge(msem(m, "ys_dve"), g + 1)
                    pe.wait_ge(msem(m, "ys_act"), g + 1)
                    for half, copied in ((0, "hs_act"), (1, "hs_dve")):
                        pe.wait_ge(msem(m, copied), g + 1)
                        for j in range(KT):
                            f = (half * KT + j) * P
                            mm = pe.matmul(ps(4 + half, HALF, c0=j * HALF), HS[:, f:f + P], STACK, start=True, stop=True)
                        mm.then_inc(msem(m, "hidden_turned"), 1)

                def turn_part(g, i):
                    pe.wait_ge(msem(m, "hidden"), g * 3 + (i + 1))
                    pe.nop(nofuse=True)
                    for k in range(4 * i, min(4 * i + 4, m.ht)):
                        tr = pe.transpose(ps(i, P, c0=(k % 4) * P), HF[:, k * P:(k + 1) * P], IDENT[:, :])
                    tr.then_inc(msem(m, "hidden_turned"), 1)

                if m is m1:
                    pe.wait_ge(msem(m, "gates"), 1)
                    for a in range(2):
                        tr = pe.transpose(ps(3, P, 0, 32, a * P), GATE[:, a, :], IDENT[:, :])
                    tr.then_inc(sem("gates_turned"), 1)
                    pe.wait_ge(sem("gates_copied"), 1)
                    pe.wait_ge(sem("ld_bout"), 16)
                    for k in range(KT):
                        mm = pe.matmul(ps(4 + k // 2, T, c0=(k % 2) * T), BOUT[:, k * P:(k + 1) * P], GT[0:32, :],
                                       start=True, stop=True)
                    mm.then_inc(sem("bias_sum"), 1)
                    pe.wait_ge(sem("bias_copied"), 1)
                pe.wait_ge(msem(m, "ht_act"), 1)
                pe.wait_ge(msem(m, "ht_dve"), 1)
                gather(1)
                if m is m1:
                    pe.wait_ge(sem("stack_ready"), 1)
                with pe.Fori(0, count) as g:
                    pe.wait_ge(msem(m, "x_hi"), g + 1)
                    pe.wait_ge(msem(m, "x_lo"), g + 1)
                    split_product(g, 0)
                    if m is m2:
                        pe.wait_ge(msem(m, "ys_dve"), g + 1)
                        pe.wait_ge(msem(m, "ys_act"), g + 1)
                    split_product(g, 1)
                    turn(g)
                    for s in range(2, m.first):
                        split_product(g, s)
                    gather(g + 2, g)
                    if m is m1:
                        turn_hidden(g)
                    else:
                        for i in range(3):
                            turn_part(g, i)
                    pe.wait_ge(msem(m, "x_hi"), g + 2)
                    pe.wait_ge(msem(m, "x_lo"), g + 2)
                    scatter(g, (0, 1))
                    half = 2 if m is m1 else 3
                    for s in range(m.first, m.first + half):
                        if m is m1 and s == m.first:
                            pe.wait_ge(msem(m, "hm"), g + 1)
                        elif m is m2 and group_kts(m, s)[0] % 4 == 0:
                            pe.wait_ge(msem(m, "hm"), g * 3 + (group_kts(m, s)[0] // 4 + 1))
                        split_product(g, s)
                    scatter(g, (2, 3))
                    for s in range(m.first + half, m.groups):
                        if m is m2 and group_kts(m, s)[0] % 4 == 0:
                            pe.wait_ge(msem(m, "hm"), g * 3 + (group_kts(m, s)[0] // 4 + 1))
                        split_product(g, s)
                pe.wait_ge(msem(m, "x_hi"), count + 1)
                pe.wait_ge(msem(m, "x_lo"), count + 1)
                turn(count)
                scatter(count)

            experts(m1, H, WR1, "h_ready", 2)

            rms()
            layer_norm(X)

            def mixer2(l):
                pe.wait_ge(sem("stream_hi"), 2 * l + 1)
                for s in range(2):
                    feature_job(lins[f"qa{l}"], s, X)
                lin = lins[f"kva{l}"]
                feature_job(lin, 0, X, width=P)
                token_job(lin, 0, X, P, P, part=1)
                lin = lins[f"ret{l}"]
                for s in range(2):
                    feature_job(lin, s, X)
                for s in range(2, 4):
                    token_job(lin, s, X, 0, 256)

                def scores2(i):
                    g, q = i % 2, i // 2
                    n = HEADS * (l + 1) + i
                    r = g * HD
                    pe.wait_ge(sem("exp_done"), n - 1)
                    for a in range(2):
                        mm = pe.matmul(ps(4 + g, T, c0=a * T), Z[r:r + HD, (QA + q) * T + a * P:(QA + q) * T + (a + 1) * P],
                                       Z[r:r + HD, KA * T:(KA + 1) * T], start=True, stop=True)
                    mm.then_inc(sem("scores_ready"), 1)

                def ret_scores(h):
                    r = (h % 4) * RK
                    n = HEADS * l + h
                    if n:
                        pe.wait_ge(sem("ret_weighted"), n)
                    for a in range(2):
                        k0, q0 = (KR + h // 4) * T + a * P, (QR + h // 4) * T
                        mm = pe.matmul(ps(2, T, c0=a * T), Z[r:r + RK, k0:k0 + P], Z[r:r + RK, q0:q0 + T],
                                       start=True, stop=True, tile_position=(r, 0))
                    mm.then_inc(sem("ret_scores"), 1)

                def ret_values(h):
                    n = HEADS * l + h
                    r = (h % 2) * HD
                    pe.wait_ge(sem("ret_weighted"), n + 1)
                    if h % 2 == 0 and n:
                        pe.wait_ge(sem("ret_copied"), n // 2)
                    a = RA[:, h % 2]
                    v = VR[:, :, h * HD:(h + 1) * HD]
                    pe.matmul(ps(3, T, r, r + HD, 0), v[:, 0, :], a[:, 0, 0, :], start=True, stop=True, skip_group_check=True)
                    pe.matmul(ps(3, P, r, r + HD, P), v[:, 1, :], a[:, 0, 1, P:T], start=False, stop=True, skip_group_check=True)
                    pe.matmul(ps(3, T, r, r + HD, T), v[:, 1, :], a[:, 1, 1, :], start=True, stop=True, skip_group_check=True)
                    pe.matmul(ps(3, P, r, r + HD, T), v[:, 0, :], a[:, 1, 0, 0:P], start=False, stop=True,
                              skip_group_check=True).then_inc(sem("ret_values"), 1)

                lin = lins[f"gg{l}"]
                pe.wait_ge(sem("pair_copied"), 4 * (l + 1))
                for i in range(12):
                    feature_job(lin, i, X)
                    if i == 0:
                        e, c = job_evac[lin.job0 - 1]
                        pe.wait_ge(sem("evac_" + e), c)
                    if i < 8:
                        scores2(i)
                        ret_scores(i)
                    n = HEADS * (l + 1) + i
                    if 1 <= i < 9:
                        turn_probs(n - 1, 0, ((0, 0), (1, 0), (0, 1), (1, 1)))
                        ret_values(i - 1)
                    if 2 <= i < 10:
                        i2 = i - 2
                        g, q = i2 % 2, i2 // 2
                        values(n - 2, g, 4 * (l + 1) + q, g, VA[:, :, g * HD:(g + 1) * HD], ((0, 0, T, 0), (1, 0, T, T)))

                def head_sums(src):
                    norm[0] += 1
                    pe.wait_ge(sem("norm_in"), norm[0])
                    for k in range(KT):
                        mm = pe.matmul(ps(4 + k // 2, T, c0=(k % 2) * T), BLK[:, :], src[:, k, :], start=True, stop=True)
                    mm.then_inc(sem("norm_sum"), 1)

                head_sums(H)
                pe.wait_ge(sem("pair_copied"), 4 * (l + 2))
                lin = lins[f"wo_attn{l}"]
                for part in range(2):
                    feature_job(lin, 0, z(QA, QA + 4), 4, part)
                norm[0] += 1
                pe.wait_ge(sem("norm_in"), norm[0])
                for k in range(KT):
                    mm = pe.matmul(ps(4, T, 0, 16), HEADROW[:, k, :], SQV[:, k, :], start=(k == 0), stop=(k == KT - 1))
                mm.then_inc(sem("norm_sum"), 1)
                for part in range(2):
                    feature_job(lin, 1, z(QA, QA + 4), 4, part)
                pe.wait_ge(sem("pool_tables"), l + 2)
                norm[0] += 1
                pe.wait_ge(sem("norm_in"), norm[0])
                for k in range(KT):
                    mm = pe.matmul(ps(4 + k // 2, T, c0=(k % 2) * T), SPREAD[:, k, :], SQ[0:16, 0:T], start=True, stop=True)
                mm.then_inc(sem("norm_sum"), 1)
                pe.wait_ge(sem("ret_out"), l + 1)
                for s in range(2):
                    for part in range(2):
                        feature_job(lins[f"wo_ret{l}"], s, z(QR, QR + 4), 4, part)
                pe.wait_ge(sem("mix_ready"), l + 2)
                for s in range(4):
                    feature_job(lins[f"w_out{l}"], s, z(G2A, G2A + 8))
                layer_norm(X)
                pe.wait_ge(sem("x2_ready"), 2 * l + 2)

            mixer2(0)
            pe.wait_ge(sem("stream_hi"), 2)
            for s in range(11):
                feature_job(lins["ffn1"], s, X)
            for s in range(11):
                feature_job(lins["ffn3"], s, X)
            lin = lins["ffn2"]
            for s in range(11):
                w = weights(lin.at[s]).rearrange("p (k n) -> p k n", k=2)
                e, c = job_evac[lins["ffn3"].job0 + s]
                pe.wait_ge(sem("evac_" + e), max(c, job_evac[lin.job0 - 1][1] if s == 0 else 0))
                for i in range(2):
                    for j in range(KT):
                        k = 2 * s + i
                        mm = pe.matmul(ps(j // 2, T, c0=(j % 2) * T), w[:, i, j * P:(j + 1) * P],
                                       Z[:, k * T:(k + 1) * T], start=(k == 0 and j % 2 == 0), stop=(k == 21),
                                       skip_group_check=True)
                mm.then_inc(sem("lin_done"), 1)
            layer_norm(X)
            mixer2(1)
            experts(m2, X, WR2, "x2_ready", 4)
            layer_norm(X)

            pe.wait_ge(sem("x2_ready"), 5)
            for a in range(2):
                for k in range(KT):
                    tr = pe.transpose(ps(4 + 2 * a + k // 4, P, c0=(k % 4) * P), X[:, k, a * P:(a + 1) * P], IDENT[:, :])
            tr.then_inc(sem("out_turned"), 1)

        @block.scalar
        def _(act):
            ch = Chain(act, sem("act_step"))

            def rows_of(name, pat="l (r c) -> (l r) c"):
                return A[name].rearrange(pat, c=P)

            vec = [("c", 0, V_C, 8), ("b_ada", 0, V_BADA, 48), ("norm1_g", 0, V_N1G, 8), ("norm2_g", 0, V_N2G, 8),
                   ("final_g", 0, V_FG, 8), ("conv_b", 0, V_CB, 4), ("conv_ln_g", 0, V_CLG, 4),
                   ("conv_ln_b", 0, V_CLB, 4), ("ln_emb_g_2", 0, V_EG, 8), ("ln_emb_b_2", 0, V_EB, 8),
                   ("ln1_g_2", 1, 0, 16), ("ln1_b_2", 1, 16, 16), ("ln2_g_2", 1, 32, 16), ("ln2_b_2", 1, 48, 16),
                   ("b_gate_2", 1, 64, 32)]
            for name, tile, r, n in vec:
                src = rows_of(name, "(r c) -> r c" if len(A[name].shape) == 1 else "l (r c) -> (l r) c")
                act.dma_start(VROWS[r:r + n, tile, :], src).then_inc(sem("ld_vec"), 16)
            act.dma_start(VROWS[0:124, 2, :], A["conv_w"][0].rearrange("k (j c) -> (k j) c", c=P)).then_inc(sem("ld_vec"), 16)
            act.dma_start(VROWS[:, 3:7, :], A["b_exp_in"][0].rearrange("(t a) (j c) -> (a j) t c", t=4, c=P))\
                .then_inc(sem("ld_vec"), 16)
            act.dma_start(XT, A["x"][0].rearrange("(a p) d -> p a d", p=P)).then_inc(sem("ld_x"), 16)
            for name, c0, n in (("sink_logits_2", R_SINK, 16), ("decay_fwd_2", R_DECAY, 16), ("decay_bwd_2", R_DECAY + 16, 16),
                                ("b_router", R_BR1, 32), ("router_b_2", R_BR2, 8)):
                act.dma_start(ROWS[0:1, c0:c0 + n], A[name].rearrange("l h -> (l h)").unsqueeze(0)).then_inc(sem("ld_rows"), 16)
            act.dma_start(WF, w_in[0][:, 5 * CW:5 * CW + HEADS].rearrange("(k p) n -> p k n", p=P)).then_inc(sem("ld_small"), 16)
            act.dma_start(WR1[:, :, :], A["w_router"][0].rearrange("(k p) n -> p k n", p=P)).then_inc(sem("ld_small"), 16)
            act.dma_start(WR2[:, :, :], A["router_w_2"][0].rearrange("(k p) n -> p k n", p=P)).then_inc(sem("ld_small"), 16)
            act.dma_start(BFG[:, :], A["b_forget"].rearrange("l h -> h l")).then_inc(sem("ld_small"), 16)

            def linear_ready(lin, s, part=0):
                g = lin.group0 + (lin.groups if lin.k_major else s * lin.per + part + 1)
                act.wait_ge(sem("lin_done"), g)
                return (lin.job0 + s * lin.per + part) % 2

            sq = [0]

            def root():
                sq[0] += 1
                act.wait_ge(sem("root_in"), sq[0])
                act.activation(SQ[:, 0:T], SQ[:, 0:T], ACT.Sqrt).then_inc(sem("root_out"), 1)

            act.wait_ge(sem("vec_turned"), 1)
            V = PS[:, 0:3, :].rearrange("p b n -> p (b n)")
            act.activation(VEC[:, 0:108], V[:, 0:108], ACT.Copy)
            act.activation(VEC[:, P:P + 96], V[:, P:P + 96], ACT.Copy)
            act.activation(VEC[:, 2 * P:2 * P + 124], V[:, 2 * P:2 * P + 124], ACT.Copy)
            act.activation(VEC[:, 3 * P:4 * P], V[:, 3 * P:4 * P], ACT.Copy)
            ch.link(act.activation(VEC[:, 4 * P:7 * P], V[:, 4 * P:7 * P], ACT.Copy))
            act.wait_ge(sem("rows_spread"), 1)
            ch.link(act.activation(ROWB[:, :], ps(3, R_N), ACT.Copy))
            act.activation(CSIL[:, :], VEC[:, V_C:V_C + 8], ACT.Silu).then_inc(sem("init_act"), 1)
            act.wait_ge(sem("logsig_in"), 1)
            act.activation(SQ[:, 32:64], SQ[:, 0:32], ACT.Exp, scale=-1.0).then_inc(sem("logsig_exp"), 1)
            root()

            dst = [z(UV, UV + 2), z(UV + 2, UV + 4), z(UG, UG + 2), z(UG + 2, UG + 4),
                   z(Q1, Q1 + 2), z(Q1 + 2, Q1 + 4), z(K1, K1 + 2), z(K1 + 2, K1 + 4),
                   VT1[:, :, 0:256], VT1[:, :, 256:512]]
            for s in range(10):
                b = linear_ready(lins["uqkv_a"], s) if s < 4 else linear_ready(lins["uqkv_b"], s - 4)
                act.activation(dst[s], ps2(b), ACT.Sigmoid if s in (2, 3) else ACT.Copy).then_inc(sem("evac_act"), 1)
            b = linear_ready(lins["forget"], 0)
            act.wait_ge(sem("ld_small"), 16 * 4)
            act.activation(SQ[0:8, 0:T], PS[0:8, b, 0:T], ACT.Identity, bias=BFG[:, 0:1]).then_inc(sem("evac_act"), 1)
            act.wait_ge(sem("logsig_in"), 2)
            act.activation(SQ[0:8, 2 * T:3 * T], SQ[0:8, T:2 * T], ACT.Exp, scale=-1.0).then_inc(sem("logsig_exp"), 1)

            lin = lins["gates"]
            for i in range(10):
                if i < 8:
                    b = linear_ready(lin, i)
                    act.activation(z(GC + 2 * i, GC + 2 * i + 2), ps2(b), ACT.Sigmoid).then_inc(sem("evac_act"), 1)
                    h = i
                    act.wait_ge(sem("max_ready"), h + 1)
                    b = 4 + h % 2
                    st = ST[:, h % 2, :]
                    if h >= 2:
                        act.wait_ge(sem("probs_turned"), h - 1)
                    act.activation(PROB[:, h % 2, 0, 0:P], ps(b, P), ACT.Exp, bias=st[:, 2:3], scale=QSCALE,
                                   accum_out=st[:, 4:5])
                    act.activation(PROB[:, h % 2, 1, :], ps(b, T, c0=P), ACT.Exp, bias=st[:, 3:4], scale=QSCALE,
                                   accum_out=st[:, 5:6]).then_inc(sem("exp_done"), 1)
                if 1 <= i < 9:
                    n = i - 1
                    act.wait_ge(sem("probs_turned"), n + 1)
                    if n >= 2:
                        act.wait_ge(sem("values_done"), n - 1)
                    act.activation(PROBT[:, n % 2, 0:3 * P], ps(6, 3 * P), ACT.Copy).then_inc(sem("probs_copied"), 1)

            root()
            act.wait_ge(sem("conv_normed"), 1)
            for j in range(4):
                a = act.activation(Z[:, (UV + j) * T:(UV + j + 1) * T], Z[:, (UV + j) * T:(UV + j + 1) * T], ACT.Silu,
                                   bias=VEC[:, V_CLB + j:V_CLB + j + 1], scale=VEC[:, V_CLG + j:V_CLG + j + 1])
            a.then_inc(sem("conv_ready"), 1)
            act.dma_start(BOUT, A["b_exp_out"][0]).then_inc(sem("ld_bout"), 16)
            root()

            def experts(m):
                act.wait_ge(msem(m, "x_turned"), 1)
                act.activation(HT[:, 0, :], PS[:, 4:6, :].rearrange("p b n -> p (b n)"), ACT.Copy).then_inc(msem(m, "ht_act"), 1)

                act.wait_ge(sem("lin_done"), free_at[(N_A if m is m1 else N_SLOTS) - 1][1])
                for s in range(2):
                    split_hi(act, m, 0, s, first=True)
                act.wait_ge(msem(m, "top"), 1)
                for a in range(2):
                    e = act.activation(GATE[:, a, 0:m.n], LOG[:, a, 0:m.n], ACT.Exp, bias=NTOP[:, a:a + 1])
                e.then_inc(msem(m, "gate_exp"), 1)
                for s in range(2, SPLIT_N):
                    split_hi(act, m, 0, s, first=True)
                act.wait_ge(msem(m, "tables"), 1)
                count = act.value_load(TAB[0:1, COUNT:COUNT + 1], min_val=m.n, max_val=48)

                if m is m1:
                    act.wait_ge(sem("gates_turned"), 1)
                    act.activation(GT[0:32, :], ps(3, T, 0, 32), ACT.Copy).then_inc(sem("gates_copied"), 1)

                def turned(g):
                    act.wait_ge(msem(m, "turned"), g + 1)
                    act.activation(GT, ps(6, T), ACT.Copy).then_inc(msem(m, "turned_copied"), 1)

                act.wait_ge(msem(m, "ys_dve"), 1)
                act.activation(YS[:, 512:1024], YS[:, 0:512], ACT.Copy).then_inc(msem(m, "ys_act"), 1)

                def tokens_hi(g1):
                    act.wait_ge(msem(m, "gathered"), g1)
                    for b in range(2):
                        i = act.activation(m.x[:, 4 * b:4 * b + 4, 0:m.slots],
                                           ps(6 + b).rearrange("p (k c) -> p k c", k=4)[:, :, 0:m.slots], ACT.Copy)
                    i.then_inc(msem(m, "x_hi"), 1)

                def next_groups(g):
                    for s in range(3):
                        split_hi(act, m, g + 1, s)
                    act.wait_ge(msem(m, "group_done"), g * m.groups + m.groups)
                    act.activation(YS[:, 512:1024], ps(5 if m is m1 else 4), ACT.Copy).then_inc(msem(m, "ys_act"), 1)
                    split_hi(act, m, g + 1, 3)

                tokens_hi(1)
                with act.Fori(0, count) as g:
                    split_hi(act, m, g, 4)
                    turned(g)
                    for s in range(5, m.first + 3):
                        split_hi(act, m, g, s)
                    if m is m1:
                        act.wait_ge(msem(m, "group_done"), g * m.groups + m.first)
                        act.activation(HS[:, 0:1024], PS[:, 0:2, :].rearrange("p b n -> p (b n)"), ACT.Copy)\
                            .then_inc(msem(m, "hs_act"), 1)
                        tokens_hi(g + 2)
                        split_hi(act, m, g, 11)
                        act.wait_ge(msem(m, "gate_part"), g + 1)
                        act.activation(SIG, GPART, ACT.Sigmoid, scale=1.702).then_inc(msem(m, "sig"), 1)
                    else:
                        act.wait_ge(msem(m, "group_done"), g * m.groups + m.first)
                        for i in range(3):
                            n = min(512, 1408 - i * 512)
                            act.activation(PART[:, i * 512:i * 512 + n], ps(i, n), ACT.Silu).then_inc(msem(m, "sig"), 1)
                        tokens_hi(g + 2)
                        for i in range(3):
                            k1 = min(4 * i + 4, m.ht)
                            act.wait_ge(msem(m, "hidden_turned"), g * 3 + (i + 1))
                            act.activation(m.h[:, 4 * i:k1, 0:CHUNK], ps(i, (k1 - 4 * i) * P).rearrange("p (k c) -> p k c", c=P),
                                           ACT.Copy).then_inc(msem(m, "h_hi"), 1)
                        for s in range(m.first + 3, m.groups):
                            split_hi(act, m, g, s)
                    next_groups(g)
                turned(count)

            def stream_hi(i):
                act.wait_ge(sem("x2_ready"), i)
                act.activation(XHI[:, :, :], X[:, :, :], ACT.Copy).then_inc(sem("stream_hi"), 1)

            experts(m1)
            root()
            act.wait_ge(msem(m1, "bytes_free"), 1)
            for q in range(2):
                split_dense(act, q)
            root()
            stream_hi(1)
            for q in range(2, SPLIT_N):
                split_dense(act, q)

            def mixer2(l):
                def copy(lin, s, dst, f=ACT.Copy, part=0):
                    b = linear_ready(lin, s, part)
                    act.activation(dst, ps2(b), f).then_inc(sem("evac_act"), 1)

                q0 = 41 * l + SPLIT_N
                for s in range(2):
                    copy(lins[f"qa{l}"], s, z(QA + 2 * s, QA + 2 * s + 2))
                    split_dense(act, q0 + s)
                b = linear_ready(lins[f"kva{l}"], 0, 0)
                act.activation(Z[:, KA * T:(KA + 1) * T], ps(b, T), ACT.Copy).then_inc(sem("evac_act"), 1)
                b = linear_ready(lins[f"kva{l}"], 0, 1)
                act.activation(VA, PS[:, b, 0:T].rearrange("p (a n) -> p a n", a=2), ACT.Copy).then_inc(sem("evac_act"), 1)
                split_dense(act, q0 + 2)
                lin = lins[f"ret{l}"]
                for s, dst_ in enumerate((z(QR, QR + 2), z(KR, KR + 2), VR[:, :, 0:256], VR[:, :, 256:512])):
                    copy(lin, s, dst_)
                    split_dense(act, q0 + 3 + s)
                lin = lins[f"gg{l}"]
                for i in range(12):
                    if i < 4:
                        copy(lin, i, z(GF + 2 * i, GF + 2 * i + 2), ACT.Silu)
                    else:
                        b = linear_ready(lin, i)
                        for j in range(2):
                            t = 2 * (i - 4) + j
                            a = act.activation(Z[:, (G2A + t) * T:(G2A + t + 1) * T], ps(b, T, c0=j * T), ACT.Sigmoid,
                                               bias=VEC[:, V_BG + 16 * l + t:V_BG + 16 * l + t + 1])
                        a.then_inc(sem("evac_act"), 1)
                    if i < 8:
                        h = 4 * (i % 2) + i // 2
                        n = HEADS * (l + 1) + i
                        rn = HEADS * l + i
                        if i >= 2:
                            act.wait_ge(sem("ret_weighted"), rn - 1)
                        for d in range(2):
                            c = 16 * d + HEADS * l + i
                            for j in range(2):
                                a = act.activation(DEC[:, i % 2, (2 * d + j) * P:(2 * d + j + 1) * P], LAGS[:, 2 * d + j, :],
                                                   ACT.Exp, scale=LG[:, c:c + 1])
                        a.then_inc(sem("decay_exp"), 1)
                        st = ST[:, i % 2, :]
                        act.wait_ge(sem("max_ready"), n + 1)
                        act.activation(st[:, 6:8], st[:, 2:4], ACT.Exp, bias=ROWB[:, R_SINK + HEADS * l + h:R_SINK + HEADS * l + h + 1])
                        for a_ in range(2):
                            a = act.activation(PROB[:, i % 2, a_, :], PROB[:, i % 2, a_, :], ACT.Exp, bias=st[:, 2 + a_:3 + a_],
                                               scale=QSCALE, accum_out=st[:, 4 + a_:5 + a_])
                        a.then_inc(sem("exp_done"), 1)
                    if 1 <= i < 9:
                        n = HEADS * (l + 1) + i - 1
                        act.wait_ge(sem("probs_turned"), n + 1)
                        act.wait_ge(sem("values_done"), n - 1)
                        act.activation(PROBT[:, n % 2, :], ps(6), ACT.Copy).then_inc(sem("probs_copied"), 1)
                        if i % 2 == 0:
                            pr = i // 2 - 1
                            act.wait_ge(sem("ret_values"), HEADS * l + i)
                            for d in range(2):
                                a = act.activation(H[:, 4 * d + pr, :], ps(3, T, c0=d * T), ACT.Copy)
                            a.then_inc(sem("ret_copied"), 1)
                    if i < 8:
                        split_dense(act, q0 + 7 + i)
                sq[0] += 1
                act.wait_ge(sem("root_in"), sq[0])
                act.activation(SQ[0:16, 0:T], SQ[0:16, 0:T], ACT.Sqrt).then_inc(sem("root_out"), 1)
                if l == 0:
                    for q in range(19, 19 + SPLIT_N):
                        split_dense(act, q)
                root()

            mixer2(0)
            stream_hi(2)
            for s in range(11):
                b = linear_ready(lins["ffn1"], s)
                act.activation(z(2 * s, 2 * s + 2), ps2(b), ACT.Silu).then_inc(sem("evac_act"), 1)
                split_dense(act, 19 + SPLIT_N + s)
            for q in range(19 + SPLIT_N + 11, 41 + SPLIT_N):
                split_dense(act, q)
            root()
            stream_hi(3)
            mixer2(1)
            experts(m2)
            root()
            act.wait_ge(sem("out_turned"), 1)
            for b in range(4):
                act.activation(XT[:, b // 2, (b % 2) * 512:(b % 2) * 512 + 512], ps(4 + b), ACT.Copy)\
                    .then_inc(sem("out_staged"), 1)

        @block.vector
        def _(dve):
            ch = Chain(dve, sem("dve_step"))
            link = ch.link
            norm, rt = [0], [0]
            SQV = SQ[:, :].rearrange("p (k t) -> p k t", t=T)

            def log_sigmoid(y, t, n, k):
                link(dve.scalar_tensor_tensor(out=t[0], in0=y, scalar=-1.0, in1=y, op0=ALU.mult, op1=ALU.max))
                dve.tensor_scalar(t[0], t[0], 0.0, None, ALU.max).then_inc(sem("logsig_in"), 1)
                dve.wait_ge(sem("logsig_exp"), k)
                link(dve.tensor_scalar(t[2], t[1], 2.0, None, ALU.add))
                link(dve.reciprocal(t[2], t[2]))
                link(dve.tensor_tensor(t[1], t[1], t[2], ALU.mult))
                link(dve.tensor_tensor(t[2], t[1], t[1], ALU.mult))
                link(dve.tensor_scalar(t[3], t[2], 1.0 / 17.0, None, ALU.mult))
                for c in (15, 13, 11, 9, 7, 5, 3):
                    link(dve.scalar_tensor_tensor(out=t[3], in0=t[3], scalar=1.0 / c, in1=t[2], op0=ALU.add, op1=ALU.mult))
                link(dve.scalar_tensor_tensor(out=t[3], in0=t[3], scalar=1.0, in1=t[1], op0=ALU.add, op1=ALU.mult))
                link(dve.tensor_scalar(t[2], y, 0.0, None, ALU.min))
                link(dve.scalar_tensor_tensor(out=t[4], in0=t[3], scalar=-2.0, in1=t[2], op0=ALU.mult, op1=ALU.add))

            def sums():
                norm[0] += 1
                dve.wait_ge(sem("norm_sum"), norm[0])

            def reciprocal_root(sum_, n, w=T):
                for o, s in sum_:
                    i = dve.tensor_scalar(o, s, 1.0 / n, EPS, ALU.mult, ALU.add)
                i.then_inc(sem("root_in"), 1)
                rt[0] += 1
                dve.wait_ge(sem("root_out"), rt[0])
                link(dve.reciprocal(SQ[:, 0:w], SQ[:, 0:w]))

            def rms(src, dst, gain, bias):
                dve.tensor_tensor(SQV, src, src, ALU.mult).then_inc(sem("norm_in"), 1)
                sums()
                reciprocal_root([(SQ[:, 0:T], ps(4, T))], D)
                link(dve.tensor_tensor(dst, src, bc(SQ[:, 0:T], KT), ALU.mult))
                return affine(dst, gain, bias)

            def affine(dst, gain, bias):
                for k in range(dst.shape[1]):
                    if bias is None:
                        i = dve.tensor_scalar(dst[:, k, :], dst[:, k, :], gain[:, k:k + 1], None, ALU.mult)
                    else:
                        i = dve.tensor_scalar(dst[:, k, :], dst[:, k, :], gain[:, k:k + 1], bias[:, k:k + 1], ALU.mult, ALU.add)
                return i

            def centre(x, nk, n):
                sums()
                link(dve.scalar_tensor_tensor(out=x, in0=bc(ps(4, T), nk), scalar=-1.0 / n, in1=x,
                                              op0=ALU.mult, op1=ALU.add))
                dve.tensor_tensor(SQV[:, 0:nk, :], x, x, ALU.mult).then_inc(sem("norm_in"), 1)
                sums()
                reciprocal_root([(SQ[:, 0:T], ps(4, T, c0=T))], n)
                return dve.tensor_tensor(x, x, bc(SQ[:, 0:T], nk), ALU.mult)

            def layer_norm(x, g, b, ready):
                link(centre(x, KT, D))
                affine(x, g, b).then_inc(sem(ready), 1)

            def linear_ready(lin, s, part=0):
                g = lin.group0 + (lin.groups if lin.k_major else s * lin.per + part + 1)
                dve.wait_ge(sem("lin_done"), g)
                return (lin.job0 + s * lin.per + part) % 2

            dve.wait_ge(sem("pool_step"), 21)
            link(dve.tensor_scalar(LAGS[:, 0, :], LAGS[:, 0, :], 0.0, None, ALU.max))
            link(dve.tensor_scalar(LAGS[:, 3, :], LAGS[:, 3, :], 0.0, None, ALU.max))
            dve.wait_ge(sem("pool_step"), 22)
            dve.scalar_tensor_tensor(out=DIST[:, :, :], in0=DIST[:, :, :], scalar=-1.0, in1=DIST[:, :, :],
                                     op0=ALU.mult, op1=ALU.max).then_inc(sem("dist_abs"), 1)
            dve.wait_ge(sem("init_act"), 1)
            log_sigmoid(ROWB[:, R_DECAY:R_DECAY + 32],
                        [SQ[:, 0:32], SQ[:, 32:64], SQ[:, 64:96], SQ[:, 96:128], LG[:, :]], 32, 1)
            dve.wait_ge(sem("x_turned"), 1)
            for b in range(4):
                i = dve.tensor_copy(X[:, 2 * b:2 * b + 2, :], ps2(4 + b))
            i.then_inc(sem("x_ready"), 1)
            dve.wait_ge(sem("x_ready"), 1)

            def ada_products(l):
                lin = lins[f"ada{l}"]
                for s in range(KT):
                    r, c = arrive[lin.at[s]]
                    dve.wait_ge(sem(f"arrived{r}"), c)
                    w = slot(lin.at[s])[0]
                    if s == 0:
                        i = dve.tensor_scalar(ADA, w, CSIL[:, 0:1], None, ALU.mult)
                    else:
                        dve.wait_ge(sem("ada_used"), 8 * l + s)
                        i = dve.scalar_tensor_tensor(out=ADA, in0=w, scalar=CSIL[:, s:s + 1], in1=ADA, op0=ALU.mult, op1=ALU.add)
                    i.then_inc(sem("ada_used"), 1)

            def ada(l):
                b = linear_ready(lins[f"ada{l}"], 0)
                dve.tensor_tensor(MOD[:, 16 * l:16 * l + 16], ps(b, 16), VEC[:, V_BADA + 16 * l:V_BADA + 16 * l + 16],
                                  ALU.add).then_inc(sem("evac_dve"), 1)
                dve.wait_ge(sem("evac_dve"), l + 1)

            ada_products(0)
            ada(0)
            link(dve.scalar_tensor_tensor(out=GS[:, 0:8], in0=MOD[:, 8:16], scalar=1.0, in1=VEC[:, V_N1G:V_N1G + 8],
                                          op0=ALU.add, op1=ALU.mult))
            rms(X[:, :, :], H[:, :, :], GS[:, 0:8], MOD[:, 0:8]).then_inc(sem("h_ready"), 1)

            ada_products(1)
            ada(1)
            dve.wait_ge(sem("evac_act"), 4)
            link(dve.tensor_tensor(CONV_IN[:, :, TAPS - 1:], z(UV, UV + 4), z(UG, UG + 4), ALU.mult))
            conv = [0]

            def taps(n):
                for k in range(conv[0], min(conv[0] + n, TAPS)):
                    for j in range(4):
                        o = Z[:, (UV + j) * T:(UV + j + 1) * T]
                        w = VEC[:, V_CONVW + 4 * k + j:V_CONVW + 4 * k + j + 1]
                        if k == 0:
                            i = dve.tensor_scalar(o, CONV_IN[:, j, 0:T], w, VEC[:, V_CB + j:V_CB + j + 1], ALU.mult, ALU.add)
                        else:
                            dve.wait_ge(sem("tap"), 4 * (k - 1) + j + 1)
                            i = dve.scalar_tensor_tensor(out=o, in0=CONV_IN[:, j, k:k + T], scalar=w, in1=o,
                                                         op0=ALU.mult, op1=ALU.add)
                        i.then_inc(sem("tap"), 1)
                conv[0] = min(conv[0] + n, TAPS)

            ada_products(2)
            taps(3)
            dve.wait_ge(sem("evac_act"), 11)
            R = [SQ[0:8, i * T:(i + 1) * T] for i in range(8)]
            log_sigmoid(R[0], R[1:6], 256, 2)
            link(dve.memset(R[6], 1.0))
            link(dve.tensor_tensor_scan(R[7], R[6], R[5], 0.0, ALU.mult, ALU.add))
            dve.tensor_scalar(NEGF[0:8, :], R[7], -1.0 / QSCALE, None, ALU.mult).then_inc(sem("negf_ready"), 1)
            ada(2)

            def normalise(n, widths):
                st = ST[:, n % 2, :]
                link(dve.reciprocal(st[:, 0:2], st[:, 4:6]))
                for a in range(2):
                    o = PROB[:, n % 2, a, 0:widths[a]]
                    i = dve.tensor_scalar(o, o, st[:, a:a + 1], None, ALU.mult)
                i.then_inc(sem("probs_ready"), 1)

            for i in range(10):
                if i < 8:
                    h = i
                    st = ST[:, h % 2, :]
                    dve.wait_ge(sem("scores_ready"), h + 1)
                    dve.reduce_max(st[:, 0:1], ps(4 + h % 2, P), AX)
                    link(dve.reduce_max(st[:, 1:2], ps(4 + h % 2, T, c0=P), AX))
                    dve.tensor_scalar(st[:, 2:4], st[:, 0:2], -QSCALE, None, ALU.mult).then_inc(sem("max_ready"), 1)
                    taps(3)
                    dve.wait_ge(sem("exp_done"), h + 1)
                    normalise(h, (P, T))
                if i >= 2 and i % 2 == 1:
                    p = (i - 3) // 2
                    dve.wait_ge(sem("values_done"), 2 * p + 2)
                    dve.tensor_copy(Z[:, (UG + p) * T:(UG + p + 1) * T], ps(7, T, c0=(p % 2) * T)).then_inc(sem("pair_copied"), 1)
            taps(TAPS)
            dve.wait_ge(sem("tap"), 4 * TAPS)
            link(dve.tensor_copy(GS[:, 16:17], GS[:, 0:1]))
            dve.tensor_copy(GS[:, 17:18], GS[:, 0:1]).then_inc(sem("norm_in"), 1)
            centre(z(UV, UV + 4), 4, CW).then_inc(sem("conv_normed"), 1)

            def gated(lin, g0):
                for s in range(2):
                    for part in range(2):
                        b = linear_ready(lin, s, part)
                        t = 4 * s + 2 * part
                        o = z(g0 + t, g0 + t + 2)
                        i = dve.tensor_tensor(o, ps2(b), o, ALU.mult)
                        i.then_inc(sem("evac_dve"), 1)

            gated(lins["conv_out"], GC)
            gated(lins["attn_out"], GA)
            dve.wait_ge(sem("evac_dve"), job_evac[lins["attn_out"].job0 + 3][1])
            dve.tensor_tensor(z(GC, GC + 8), z(GC, GC + 8), z(GA, GA + 8), ALU.add).then_inc(sem("mix_ready"), 1)
            lin = lins["w_out"]
            for s in range(4):
                b = linear_ready(lin, s)
                for j in range(2):
                    k = 2 * s + j
                    i = dve.scalar_tensor_tensor(out=X[:, k, :], in0=ps(b, T, c0=j * T), scalar=MOD[:, 16 + k:17 + k],
                                                 in1=X[:, k, :], op0=ALU.mult, op1=ALU.add)
                i.then_inc(sem("evac_dve"), 1)
            dve.wait_ge(sem("evac_dve"), job_evac[lin.job0 + 3][1])
            link(dve.scalar_tensor_tensor(out=GS[:, 8:16], in0=MOD[:, 32:40], scalar=1.0, in1=VEC[:, V_N2G:V_N2G + 8],
                                          op0=ALU.add, op1=ALU.mult))
            rms(X[:, :, :], H[:, :, :], GS[:, 8:16], MOD[:, 24:32]).then_inc(sem("h_ready"), 1)

            def experts(m, br):
                E, top = m.n, m.top
                dve.wait_ge(sem("h_ready") if m is m1 else sem("x2_ready"), 2 if m is m1 else 4)
                if m is m2:
                    link(dve.memset(Y, 0.0))
                link(dve.memset(LOG[:, :, E:E + 8], NEG))
                link(dve.memset(ONE32, 1.0))
                dve.memset(YS[:, 0:512], 0.0).then_inc(msem(m, "ys_dve"), 1)
                dve.memset(PICKG, 0.0).then_inc(msem(m, "pickg"), 1)
                for name in ("ys_dve", "pickg"):
                    dve.wait_ge(msem(m, name), 1)
                dve.memset(FREE, 0.0).then_inc(sem("moe_scratch_free"), 1)
                dve.wait_ge(sem("moe_scratch_free"), 1 if m is m1 else 2)
                dve.wait_ge(msem(m, "x_turned"), 1)
                dve.tensor_copy(HT[:, 1, :], PS[:, 6:8, :].rearrange("p b n -> p (b n)")).then_inc(msem(m, "ht_dve"), 1)
                dve.wait_ge(msem(m, "logits"), 1)
                link(dve.tensor_tensor(LOG[:, :, 0:E], PS[:, 0, 0:2 * E].rearrange("p (a e) -> p a e", a=2),
                                       bc(ROWB[:, br:br + E], 2), ALU.add))
                for a in range(2):
                    link(dve.max(TOP8[:, a, :], LOG[:, a, 0:E]))
                link(dve.tensor_scalar(NTOP, TOP8[:, :, 0], -1.0, None, ALU.mult))
                dve.memset(TOP8[:, :, top:8], NEG).then_inc(msem(m, "top"), 1)
                dve.wait_ge(msem(m, "top"), 1)
                for a in range(2):
                    link(dve.match_replace(LOGR[:, a, 0:E + 8], TOP8[:, a, :], LOG[:, a, 0:E + 8], 3e38))
                dve.tensor_tensor(MASK[:, :, 0:E], LOGR[:, :, 0:E], LOG[:, :, 0:E], ALU.not_equal).then_inc(msem(m, "mask"), 1)
                dve.wait_ge(msem(m, "mask"), 1)
                dve.wait_ge(msem(m, "gate_exp"), 1)
                link(dve.tensor_tensor(GATE[:, :, 0:E], GATE[:, :, 0:E], MASK[:, :, 0:E], ALU.mult))
                link(dve.reduce_sum(GSUM, GATE[:, :, 0:E], AX))
                link(dve.reciprocal(GSUM, GSUM))
                dve.tensor_tensor(GATE[:, :, 0:E], GATE[:, :, 0:E], bl(GSUM, E), ALU.mult).then_inc(msem(m, "gates"), 1)
                dve.wait_ge(msem(m, "gates"), 1)
                dve.wait_ge(msem(m, "counts"), 1)
                n = ps(1, E)
                link(dve.tensor_scalar(NCH[:, 0:E], n, float(m.slots), 1.0, ALU.is_gt, ALU.add))
                for more in range(2 * m.slots, T, m.slots):
                    link(dve.scalar_tensor_tensor(out=NCH[:, 0:E], in0=n, scalar=float(more), in1=NCH[:, 0:E],
                                                  op0=ALU.is_gt, op1=ALU.add))
                link(dve.tensor_tensor_scan(CUM[:, 0:E], ONE32[:, 0:E], NCH[:, 0:E], 0.0, ALU.mult, ALU.add))
                for a in range(2):
                    link(dve.scalar_tensor_tensor(out=RANK[:, a, 0:E], in0=ps(1, E, c0=64 + 32 * a), scalar=1.0,
                                                  in1=MASK[:, a, 0:E], op0=ALU.add, op1=ALU.mult))
                link(dve.tensor_scalar(RANK[:, :, 0:E], RANK[:, :, 0:E], -1.0, None, ALU.add))
                link(dve.tensor_scalar(LE[:, 0:E], CUM[:, 0:E], IOTAP[:, 0:1], None, ALU.is_le))
                link(dve.tensor_tensor(LEN_[:, 0:E], LE[:, 0:E], NCH[:, 0:E], ALU.mult))
                link(dve.reduce_sum(TCOL[:, 0:1], LE[:, 0:E], AX))
                link(dve.reduce_sum(TCOL[:, 1:2], LEN_[:, 0:E], AX))
                link(dve.tensor_scalar(TCOL[:, 0:1], TCOL[:, 0:1], float(E - 1), None, ALU.min))
                link(dve.tensor_tensor(TCOL[:, 1:2], IOTAP[:, 0:1], TCOL[:, 1:2], ALU.subtract))
                dve.tensor_scalar(TCOL[:, 1:2], TCOL[:, 1:2], float(T // m.slots - 1), float(m.slots), ALU.min, ALU.mult)\
                    .then_inc(msem(m, "table_cols"), 1)
                dve.wait_ge(msem(m, "table_rows"), 1)
                link(dve.tensor_copy(TAB[0:1, 0:2 * P], ps(2, 2 * P, 0, 1)))
                link(dve.tensor_scalar(TAB[0:1, LAST:LAST + 1], CUM[0:1, E - 1:E], -1.0, None, ALU.add))
                dve.tensor_copy(TAB[0:1, COUNT:COUNT + 1], CUM[0:1, E - 1:E]).then_inc(msem(m, "tables"), 1)
                dve.wait_ge(msem(m, "tables"), 1)
                count = dve.value_load(TAB[0:1, COUNT:COUNT + 1], min_val=m.n, max_val=48)
                dve.wait_ge(msem(m, "iota"), 1)
                if m is m1:
                    dve.wait_ge(sem("bias_sum"), 1)
                    dve.tensor_copy(Y.rearrange("p k t -> p (k t)"), PS[:, 4:8, :].rearrange("p b n -> p (b n)"))\
                        .then_inc(sem("bias_copied"), 1)
                    dve.wait_ge(sem("bias_copied"), 1)

                def window(c):
                    return IOTA[:, bass.ds(c, m.slots)].unsqueeze(1).broadcast_to([P, CHUNK // m.slots, m.slots])

                def slots_of(ap):
                    return ap.rearrange("p (r c) -> p r c", c=m.slots)

                def pick(e, c):
                    for a in range(2):
                        i = dve.tensor_scalar(slots_of(PICK[:, a, :]), window(c), RANK[:, a, bass.ds(e, 1)], None,
                                              ALU.is_equal)
                    i.then_inc(msem(m, "pick"), 1)

                def pick_gated(e, c):
                    for a in range(2):
                        i = dve.tensor_scalar(slots_of(PICKG[:, a, :]), window(c), RANK[:, a, bass.ds(e, 1)],
                                              GATE[:, a, bass.ds(e, 1)], ALU.is_equal, ALU.mult)
                    i.then_inc(msem(m, "pickg"), 1)

                def add(g, qs_=range(4)):
                    for q in qs_:
                        dve.wait_ge(msem(m, "scattered"), g * 4 + (q + 1))
                        o = Y[:, 2 * q:2 * q + 2, :]
                        dve.tensor_tensor(o, o, ps2(6 + q % 2), ALU.add).then_inc(msem(m, "added"), 1)

                def tokens_lo(g1):
                    dve.wait_ge(msem(m, "gathered"), g1)
                    dve.wait_ge(msem(m, "x_hi"), g1)
                    for b in range(2):
                        i = dve.tensor_tensor(m.x[:, 4 * b:4 * b + 4, m.slots:2 * m.slots],
                                              ps(6 + b).rearrange("p (k c) -> p k c", k=4)[:, :, CHUNK - m.slots:],
                                              m.x[:, 4 * b:4 * b + 4, 0:m.slots].bitcast(F32), ALU.subtract)
                    i.then_inc(msem(m, "x_lo"), 1)

                def chunk_of(g):
                    return (dve.value_load(TAB[0:1, bass.ds(g, 1)], min_val=0, max_val=m.n - 1),
                            dve.value_load(TAB[0:1, bass.ds(g + P, 1)], min_val=0, max_val=T - m.slots))

                dve.memset(FREE, 0.0).then_inc(msem(m, "added"), 1)
                dve.wait_ge(msem(m, "added"), 1)
                pick(0, 0)
                if m is m1:
                    mch = Chain(dve, msem(m, "dve_step"))
                    dve.tensor_tensor(STACK, IDENT[:, 0:HALF], IDENT[:, HALF:], ALU.add).then_inc(sem("stack_ready"), 1)
                tokens_lo(1)
                for s in range(SPLIT_N):
                    split_lo(dve, m, 0, s, first=True)

                def remainders(g, s0, s1):
                    for s in range(s0, s1):
                        split_lo(dve, m, g, s)

                def last_groups(g):
                    remainders(g + 1, 0, 2)
                    add(g, (2, 3))
                    remainders(g + 1, 2, 3)
                    dve.wait_ge(msem(m, "group_done"), g * m.groups + m.groups)
                    dve.tensor_copy(YS[:, 0:512], ps(4 if m is m1 else 3)).then_inc(msem(m, "ys_dve"), 1)
                    remainders(g + 1, 3, 4)

                if m is m1:
                    with dve.Fori(0, count) as g:
                        mch.enter(g * 7)
                        split_lo(dve, m, g, 4)
                        e, c = chunk_of(g)
                        dve.wait_ge(msem(m, "turned"), g + 1)
                        pick_gated(e, c)
                        mch.link(dve.tensor_copy(B1C, VEC[:, bass.ds(e * 16 + V_B1, 16)]))
                        remainders(g, 5, 8)
                        e1, c1 = chunk_of(g + 1)
                        dve.wait_ge(msem(m, "gathered"), g + 1)
                        pick(e1, c1)
                        remainders(g, 8, 11)
                        dve.wait_ge(msem(m, "group_done"), g * m.groups + m.first)
                        dve.tensor_copy(HS[:, 1024:2048], PS[:, 2:4, :].rearrange("p b n -> p (b n)"))\
                            .then_inc(msem(m, "hs_dve"), 1)
                        tokens_lo(g + 2)
                        hidden = [ps(4 + i).rearrange("p (k c) -> p k c", k=KT) for i in range(2)]
                        dve.wait_ge(msem(m, "hidden_turned"), g * 2 + 1)
                        mch.link(dve.tensor_tensor(GPART, hidden[0], bl(B1C[:, 0:KT], HALF), ALU.add))
                        dve.tensor_scalar(GPART, GPART, 7.0, None, ALU.min).then_inc(msem(m, "gate_part"), 1)
                        dve.wait_ge(msem(m, "hidden_turned"), g * 2 + 2)
                        mch.link(dve.tensor_tensor(UPART, hidden[1], bl(B1C[:, KT:2 * KT], HALF), ALU.add))
                        mch.link(dve.tensor_scalar(UPART, UPART, 7.0, -7.0, ALU.min, ALU.max))
                        dve.wait_ge(msem(m, "gate_part"), g + 1)
                        mch.link(dve.scalar_tensor_tensor(out=UPART, in0=UPART, scalar=1.0, in1=GPART, op0=ALU.add, op1=ALU.mult))
                        dve.wait_ge(msem(m, "sig"), g + 1)
                        mch.link(dve.tensor_tensor(UPART, UPART, SIG, ALU.mult))
                        mch.link(dve.tensor_copy(m.h[:, :, 0:HALF], UPART))
                        dve.tensor_tensor(m.h[:, :, HALF:], UPART, m.h[:, :, 0:HALF].bitcast(F32), ALU.subtract)\
                            .then_inc(msem(m, "hm"), 1)
                        dve.wait_ge(msem(m, "hm"), g + 1)
                        add(g, (0, 1))
                        remainders(g, 11, 12)
                        last_groups(g)
                        assert mch.n == 7, mch.n
                    dve.wait_ge(msem(m, "lo_pool"), count * m.groups + SPLIT_N)
                    dve.wait_ge(msem(m, "lo_dve"), count * m.groups + SPLIT_N)
                    dve.memset(FREE, 0.0).then_inc(msem(m, "bytes_free"), 1)
                else:
                    with dve.Fori(0, count) as g:
                        split_lo(dve, m, g, 4)
                        e, c = chunk_of(g)
                        dve.wait_ge(msem(m, "turned"), g + 1)
                        pick_gated(e, c)
                        remainders(g, 5, 12)
                        e1, c1 = chunk_of(g + 1)
                        dve.wait_ge(msem(m, "gathered"), g + 1)
                        pick(e1, c1)
                        remainders(g, 12, 19)
                        dve.wait_ge(msem(m, "group_done"), g * m.groups + m.first)
                        for i in range(3):
                            n = min(512, 1408 - i * 512)
                            dve.wait_ge(msem(m, "sig"), g * 3 + (i + 1))
                            dve.tensor_tensor(HF[:, i * 512:i * 512 + n], ps(3 + i, n), PART[:, i * 512:i * 512 + n], ALU.mult)\
                                .then_inc(msem(m, "hidden"), 1)
                        tokens_lo(g + 2)
                        for i in range(3):
                            k1 = min(4 * i + 4, m.ht)
                            dve.wait_ge(msem(m, "h_hi"), g * 3 + (i + 1))
                            dve.tensor_tensor(m.h[:, 4 * i:k1, CHUNK:], ps(i, (k1 - 4 * i) * P).rearrange("p (k c) -> p k c", c=P),
                                              m.h[:, 4 * i:k1, 0:CHUNK].bitcast(F32), ALU.subtract).then_inc(msem(m, "hm"), 1)
                        remainders(g, 19, 20)
                        add(g, (0, 1))
                        remainders(g, 20, 24)
                        last_groups(g)
                add(count)
                dve.wait_ge(msem(m, "added"), count * 4 + 5)

            experts(m1, R_BR1)
            for k in range(KT):
                i = dve.scalar_tensor_tensor(out=X[:, k, :], in0=Y[:, k, :], scalar=MOD[:, 40 + k:41 + k], in1=X[:, k, :],
                                             op0=ALU.mult, op1=ALU.add)
            link(i)
            i = rms(X[:, :, :], X[:, :, :], VEC[:, V_FG:V_FG + 8], None)
            i.then_inc(sem("norm_in"), 1)
            dve.wait_ge(sem("norm_in"), norm[0] + 1)
            layer_norm(X[:, :, :], VEC[:, V_EG:V_EG + 8], VEC[:, V_EB:V_EB + 8], "x2_ready")

            def vcols(c, l):
                return VEC[:, c + 8 * l:c + 8 * l + 8]

            def residual(lin):
                for s in range(4):
                    b = linear_ready(lin, s)
                    o = X[:, 2 * s:2 * s + 2, :]
                    dve.scalar_tensor_tensor(out=o, in0=o, scalar=ALPHA, in1=ps2(b), op0=ALU.mult, op1=ALU.add)\
                        .then_inc(sem("evac_dve"), 1)
                dve.wait_ge(sem("evac_dve"), job_evac[lin.job0 + lin.jobs - 1][1])

            def x_in():
                dve.tensor_copy(GS[:, 16:17], GS[:, 0:1]).then_inc(sem("norm_in"), 1)

            def mixer2(l):
                dve.wait_ge(sem("pool_tables"), 1)
                for i in range(12):
                    n = HEADS * (l + 1) + i
                    if i < 8:
                        h = 4 * (i % 2) + i // 2
                        st = ST[:, i % 2, :]
                        dve.wait_ge(sem("scores_ready"), n + 1)
                        dve.wait_ge(sem("probs_turned"), n - 1)
                        pr = PROB[:, i % 2]
                        link(dve.scalar_tensor_tensor(out=pr, in0=DIST[:, :, :], scalar=-SLOPES[h] / QSCALE, in1=ps2(4 + i % 2),
                                                      op0=ALU.mult, op1=ALU.add))
                        link(dve.reduce_max(st[:, 0:2], pr, AX))
                        sk = ROWB[:, R_SINK + HEADS * l + h:R_SINK + HEADS * l + h + 1]
                        link(dve.tensor_scalar(st[:, 0:2], st[:, 0:2], QSCALE, sk, ALU.mult, ALU.max))
                        dve.tensor_scalar(st[:, 2:4], st[:, 0:2], -1.0, None, ALU.mult).then_inc(sem("max_ready"), 1)
                        rn = HEADS * l + i
                        dve.wait_ge(sem("ret_scores"), rn + 1)
                        dve.wait_ge(sem("decay_masked"), rn + 1)
                        if i >= 2:
                            dve.wait_ge(sem("ret_values"), rn - 1)
                        dec, ra = DEC[:, i % 2, :], RA[:, i % 2]
                        for o, p_, d_ in ((ra[:, 0, 0, :], ps(2, T), dec[:, 0:T]),
                                          (ra[:, 0, 1, P:T], ps(2, P, c0=3 * P), dec[:, 0:P]),
                                          (ra[:, 1, 1, :], ps(2, T, c0=T), dec[:, T:2 * T]),
                                          (ra[:, 1, 0, 0:P], ps(2, P), dec[:, 3 * P:4 * P])):
                            j = dve.scalar_tensor_tensor(out=o, in0=p_, scalar=RSCALE, in1=d_, op0=ALU.mult, op1=ALU.mult)
                        j.then_inc(sem("ret_weighted"), 1)
                        dve.wait_ge(sem("exp_done"), n + 1)
                        link(dve.tensor_tensor(st[:, 4:6], st[:, 4:6], st[:, 6:8], ALU.add))
                        normalise(i, (T, T))
                    if 3 <= i < 11 and i % 2 == 1:
                        p = (i - 3) // 2
                        dve.wait_ge(sem("values_done"), HEADS * (l + 1) + 2 * p + 2)
                        dve.tensor_copy(Z[:, (QA + p) * T:(QA + p + 1) * T], ps(7, T, c0=(p % 2) * T))\
                            .then_inc(sem("pair_copied"), 1)
                dve.wait_ge(sem("ret_copied"), 4 * (l + 1))
                x_in()
                sums()
                for b in range(4):
                    o = H[:, 2 * b:2 * b + 2, :]
                    i = dve.scalar_tensor_tensor(out=o, in0=ps2(4 + b), scalar=-1.0 / HD, in1=o, op0=ALU.mult, op1=ALU.add)
                link(i)
                dve.tensor_tensor(SQV, H[:, :, :], H[:, :, :], ALU.mult).then_inc(sem("norm_in"), 1)

                def gated(lin, g0, js):
                    for j in js:
                        b = linear_ready(lin, j // 2, j % 2)
                        o = z(g0 + 2 * j, g0 + 2 * j + 2)
                        dve.tensor_tensor(o, ps2(b), o, ALU.mult).then_inc(sem("evac_dve"), 1)

                lin = lins[f"wo_attn{l}"]
                gated(lin, G2A, (0, 1))
                sums()
                dve.tensor_scalar(SQ[0:16, 0:T], ps(4, T, 0, 16), 1.0 / HD, EPS, ALU.mult, ALU.add).then_inc(sem("root_in"), 1)
                rt[0] += 1
                dve.wait_ge(sem("root_out"), rt[0])
                dve.reciprocal(SQ[0:16, 0:T], SQ[0:16, 0:T]).then_inc(sem("norm_in"), 1)
                gated(lin, G2A, (2, 3))
                sums()
                for b in range(4):
                    o = H[:, 2 * b:2 * b + 2, :]
                    i = dve.tensor_tensor(o, o, ps2(4 + b), ALU.mult)
                link(i)
                link(dve.tensor_tensor(H[:, :, :], H[:, :, :], z(GF, GF + 8), ALU.mult))
                dve.tensor_tensor(z(QR, QR + 4), H[:, 0:4, :], H[:, 4:8, :], ALU.add).then_inc(sem("ret_out"), 1)
                lin = lins[f"wo_ret{l}"]
                gated(lin, G2R, range(4))
                dve.wait_ge(sem("evac_dve"), job_evac[lin.job0 + 3][1])
                dve.tensor_tensor(z(G2A, G2A + 8), z(G2A, G2A + 8), z(G2R, G2R + 8), ALU.add).then_inc(sem("mix_ready"), 1)
                residual(lins[f"w_out{l}"])
                x_in()
                layer_norm(X[:, :, :], vcols(V_LN1G, l), vcols(V_LN1B, l), "x2_ready")

            def stream_lo(i):
                dve.wait_ge(sem("stream_hi"), i)
                dve.tensor_tensor(XLO[:, :, :], X[:, :, :], XHI[:, :, :].bitcast(F32), ALU.subtract).then_inc(sem("stream_lo"), 1)

            stream_lo(1)
            mixer2(0)
            stream_lo(2)
            for s in range(11):
                b = linear_ready(lins["ffn3"], s)
                o = z(2 * s, 2 * s + 2)
                dve.tensor_tensor(o, ps2(b), o, ALU.mult).then_inc(sem("evac_dve"), 1)
            dve.wait_ge(sem("lin_done"), lins["ffn2"].group0 + 11)
            for b in (2, 3, 0, 1):
                o = X[:, 2 * b:2 * b + 2, :]
                i = dve.scalar_tensor_tensor(out=o, in0=o, scalar=ALPHA, in1=ps2(b), op0=ALU.mult, op1=ALU.add)
                if b in (0, 1):
                    i.then_inc(sem("evac_dve"), 1)
            dve.wait_ge(sem("evac_dve"), job_evac[lins["ffn2"].job0 + 1][1])
            x_in()
            layer_norm(X[:, :, :], vcols(V_LN2G, 0), vcols(V_LN2B, 0), "x2_ready")
            stream_lo(3)
            mixer2(1)
            experts(m2, R_BR2)
            link(dve.scalar_tensor_tensor(out=X[:, :, :], in0=X[:, :, :], scalar=ALPHA, in1=Y, op0=ALU.mult, op1=ALU.add))
            x_in()
            layer_norm(X[:, :, :], vcols(V_LN2G, 1), vcols(V_LN2B, 1), "x2_ready")


INPUTS = ["x", "c", "w_ada", "b_ada", "norm1_g", "w_in", "b_forget", "conv_w", "conv_b", "conv_ln_g", "conv_ln_b",
          "w_conv_out", "w_attn_out", "w_out", "norm2_g", "w_router", "b_router", "w_exp_in", "b_exp_in", "w_exp_out",
          "b_exp_out", "final_g", "ln_emb_g_2", "ln_emb_b_2", "w_in_2", "b_gate_2", "sink_logits_2", "decay_fwd_2",
          "decay_bwd_2", "w_o_attn_2", "w_o_ret_2", "w_out_2", "ln1_g_2", "ln1_b_2", "ffn_w1_2", "ffn_w3_2",
          "ffn_w2_2", "router_w_2", "router_b_2", "moe_w1_2", "moe_w3_2", "moe_w2_2", "ln2_g_2", "ln2_b_2"]


def kernel(**inputs):
    import numpy as _np
    import concourse.bacc as _bacc
    from concourse import mybir as _mybir
    from concourse.bass_utils import run_bass_kernel_spmd as _run

    nc = _bacc.Bacc("TRN2", target_bir_lowering=False, num_devices=1)
    arrays, aps = {}, {}
    for name in INPUTS:
        a = _np.ascontiguousarray(inputs[name])
        arrays[f"in_{name}"] = a
        aps[name] = nc.dram_tensor(f"in_{name}", a.shape, _mybir.dt.from_np(a.dtype), kind="ExternalInput").ap()
    out = nc.dram_tensor("out_0", (1, T, D), _mybir.dt.float32, kind="ExternalOutput").ap()
    build_two_blocks(nc, aps, out)
    r = _run(nc, [arrays], core_ids=[0])
    return r.results[0]["out_0"]
```
